# Optimizing a Trainium2 kernel written in Bass

```python
import math
import jax, jax.numpy as jnp
from jax import lax
import numpy as np

D_MODEL = 1024
BATCH = 1
SEQ = 2048
DEPTH = 2
DEC_BATCH = 8
DEC_SEQ = 4
PAST_LEN = 2048
PAGE_SIZE = 128

N_EVEN = (DEPTH + 1) // 2
N_ODD = DEPTH // 2
POOL_WINDOWS = (2, 4, 8, 16)
N_POOL_GROUPS = len(POOL_WINDOWS)
POOL_WIDTH = D_MODEL // 2
POOL_GROUP = POOL_WIDTH // N_POOL_GROUPS
POOL_BUF = max(POOL_WINDOWS) - 1
SB_HEADS = 8
SB_HEAD_DIM = (D_MODEL // 2) // SB_HEADS
SB_WIDTH = SB_HEADS * SB_HEAD_DIM
SB_BIAS_INIT = -8.0
Q_BLOCK = 128
EVEN_MIX = POOL_WIDTH + SB_WIDTH
EVEN_IN = POOL_WIDTH + 3 * SB_WIDTH + EVEN_MIX
DN_HEADS = 8
DN_KEY_DIM = 128
DN_VAL_DIM = 128
DN_QK = DN_HEADS * DN_KEY_DIM
DN_V = DN_HEADS * DN_VAL_DIM
DN_CONV_DIM = 2 * DN_QK + DN_V
CONV_WIDTH = 4
DN_CHUNK = 64
ODD_IN = DN_CONV_DIM + DN_V + 2 * DN_HEADS
NORM_EPS = 1e-6

kernel_name = 'pool_stickbreak_gdn_hybrid_step'

f32 = jnp.float32

def rms_norm(x, g):
    xf = x.astype(f32)
    y = xf * lax.rsqrt(jnp.mean(xf * xf, axis=-1, keepdims=True) + NORM_EPS)
    return (y * g.astype(f32)).astype(x.dtype)

def l2_norm(x):
    xf = x.astype(f32)
    return xf * lax.rsqrt(jnp.sum(xf * xf, axis=-1, keepdims=True) + NORM_EPS)

def pool_mix(u, buf, start, w_pool, scale):
    B, L, P = u.shape
    ext = jnp.concatenate([buf.astype(f32), u.astype(f32)], axis=1)
    csum = jnp.concatenate([jnp.zeros_like(ext[:, :1]), jnp.cumsum(ext, axis=1)], axis=1)
    pos = start + jnp.arange(L)
    end = csum[:, POOL_BUF + 1:]
    cur = ext[:, POOL_BUF:]
    outs = []
    for gi, w in enumerate(POOL_WINDOWS):
        sl = slice(gi * POOL_GROUP, (gi + 1) * POOL_GROUP)
        win = end[..., sl] - csum[:, POOL_BUF + 1 - w:POOL_BUF + 1 - w + L, sl]
        cnt = jnp.minimum(pos + 1, w).astype(f32)[None, :, None]
        outs.append(win / cnt - cur[..., sl])
    d = jnp.stack(outs, axis=2)
    y = jnp.einsum('blgc,gcd->blgd', d, w_pool.astype(f32)).reshape(B, L, P)
    return y * scale.astype(f32)

def stick_breaking_block(q, k, v, bias, q_pos, k_pos):
    z = jnp.einsum('bqhd,bkhd->bhqk', q.astype(f32), k.astype(f32)) / math.sqrt(SB_HEAD_DIM)
    z = z + bias.astype(f32)[None, :, None, None]
    mask = k_pos[None, :] < q_pos[:, None]
    log_keep = jnp.where(mask, jax.nn.log_sigmoid(-z), 0.0)
    suffix = lax.cumsum(log_keep, axis=3, reverse=True) - log_keep
    a = jnp.where(mask, jnp.exp(jax.nn.log_sigmoid(z) + suffix), 0.0)
    return jnp.einsum('bhqk,bkhd->bqhd', a, v.astype(f32))

def stick_breaking_prompt(q, k, v, bias):
    B, L, H, d = q.shape
    qb_len = Q_BLOCK if L % Q_BLOCK == 0 else L
    nb = L // qb_len
    qb = jnp.moveaxis(q.reshape(B, nb, qb_len, H, d), 1, 0)
    k_pos = jnp.arange(L)

    def body(args):
        q_blk, blk = args
        q_pos = blk * qb_len + jnp.arange(qb_len)
        return stick_breaking_block(q_blk, k, v, bias, q_pos, k_pos)

    o = lax.map(body, (qb, jnp.arange(nb)))
    return jnp.moveaxis(o, 0, 1).reshape(B, L, H, d)

def even_layer(h, start, pool_buf, k_past, v_past, norm_g, w_in, w_pool, pool_scale, q_g, k_g, sb_bias, w_out):
    B, L, _ = h.shape
    proj = rms_norm(h, norm_g) @ w_in
    i1 = POOL_WIDTH
    i2 = i1 + SB_WIDTH
    i3 = i2 + SB_WIDTH
    i4 = i3 + SB_WIDTH
    u, q, k, v, gate = jnp.split(proj, [i1, i2, i3, i4], axis=-1)
    pool_y = pool_mix(u, pool_buf, start, w_pool, pool_scale)
    q = rms_norm(q.reshape(B, L, SB_HEADS, SB_HEAD_DIM), q_g)
    k = rms_norm(k.reshape(B, L, SB_HEADS, SB_HEAD_DIM), k_g)
    v = v.reshape(B, L, SB_HEADS, SB_HEAD_DIM)
    if k_past is None:
        sb = stick_breaking_prompt(q, k, v, sb_bias)
    else:
        k_all = jnp.concatenate([k_past.astype(k.dtype), k], axis=1)
        v_all = jnp.concatenate([v_past.astype(v.dtype), v], axis=1)
        sb = stick_breaking_block(q, k_all, v_all, sb_bias, start + jnp.arange(L), jnp.arange(start + L))
    mix = jnp.concatenate([pool_y, sb.reshape(B, L, SB_WIDTH)], axis=-1) * jax.nn.silu(gate.astype(f32))
    y = h + mix.astype(h.dtype) @ w_out
    new_buf = jnp.concatenate([pool_buf.astype(u.dtype), u], axis=1)[:, -POOL_BUF:]
    return y, new_buf, k, v

def gated_delta_rule(q, k, v, g, beta, state):
    B, L, H, dk = k.shape
    dv = v.shape[-1]
    C = DN_CHUNK if L % DN_CHUNK == 0 else L
    n = L // C

    def to_chunks(x):
        x = x.reshape(B, n, C, H, *x.shape[3:])
        return jnp.moveaxis(jnp.moveaxis(x, 1, 0), 3, 2)

    qc, kc, vc = to_chunks(q), to_chunks(k), to_chunks(v.astype(f32))
    gc = jnp.cumsum(to_chunks(g), axis=-1)
    bc = to_chunks(beta)
    incl = jnp.tril(jnp.ones((C, C), bool))
    strict = jnp.tril(jnp.ones((C, C), bool), -1)
    decay = jnp.where(incl, jnp.exp(jnp.where(incl, gc[..., :, None] - gc[..., None, :], 0.0)), 0.0)
    kb = kc * bc[..., None]
    lmat = jnp.where(strict, jnp.einsum('nbhid,nbhjd->nbhij', kb, kc) * decay, 0.0)
    eye = jnp.broadcast_to(jnp.eye(C, dtype=f32), lmat.shape)
    tmat = lax.linalg.triangular_solve(eye + lmat, eye, left_side=True, lower=True, unit_diagonal=True)
    u = jnp.einsum('nbhij,nbhjd->nbhid', tmat, vc * bc[..., None])
    w = jnp.einsum('nbhij,nbhjd->nbhid', tmat, kb * jnp.exp(gc)[..., None])

    def step(S, xs):
        q_i, k_i, u_i, w_i, g_i, dec_i = xs
        v_new = u_i - jnp.einsum('bhcd,bhde->bhce', w_i, S)
        att = jnp.einsum('bhid,bhjd->bhij', q_i, k_i) * dec_i
        o = jnp.einsum('bhcd,bhde->bhce', q_i * jnp.exp(g_i)[..., None], S) + jnp.einsum('bhij,bhje->bhie', att, v_new)
        g_last = g_i[..., -1:]
        S = S * jnp.exp(g_last)[..., None] + jnp.einsum('bhcd,bhce->bhde', k_i * jnp.exp(g_last - g_i)[..., None], v_new)
        return S, o

    S, o = lax.scan(step, state, (qc, kc, u, w, gc, decay))
    o = jnp.moveaxis(jnp.moveaxis(o, 2, 3), 0, 1).reshape(B, L, H, dv)
    return o, S

def odd_layer(h, conv_buf, state, norm_g, w_in, conv_w, a_log, dt_bias, o_g, w_out):
    B, L, _ = h.shape
    proj = rms_norm(h, norm_g) @ w_in
    qkv, z, b, a = jnp.split(proj, [DN_CONV_DIM, DN_CONV_DIM + DN_V, DN_CONV_DIM + DN_V + DN_HEADS], axis=-1)
    ext = jnp.concatenate([conv_buf.astype(qkv.dtype), qkv], axis=1)
    conv = ext[:, 0:L].astype(f32) * conv_w[0].astype(f32)
    for j in range(1, CONV_WIDTH):
        conv = conv + ext[:, j:j + L].astype(f32) * conv_w[j].astype(f32)
    conv = jax.nn.silu(conv)
    q, k, v = jnp.split(conv, [DN_QK, 2 * DN_QK], axis=-1)
    q = l2_norm(q.reshape(B, L, DN_HEADS, DN_KEY_DIM)) * (DN_KEY_DIM ** -0.5)
    k = l2_norm(k.reshape(B, L, DN_HEADS, DN_KEY_DIM))
    v = v.reshape(B, L, DN_HEADS, DN_VAL_DIM)
    beta = jax.nn.sigmoid(b.astype(f32))
    g = -jnp.exp(a_log.astype(f32)) * jax.nn.softplus(a.astype(f32) + dt_bias.astype(f32))
    o, new_state = gated_delta_rule(q, k, v, g, beta, state.astype(f32))
    o = rms_norm(o, o_g) * jax.nn.silu(z.reshape(B, L, DN_HEADS, DN_VAL_DIM).astype(f32))
    y = h + o.reshape(B, L, DN_V).astype(h.dtype) @ w_out
    return y, ext[:, -(CONV_WIDTH - 1):], new_state.astype(state.dtype)

def setup_inputs(seed: int = 0) -> dict:
    key = jax.random.key(seed)
    ks = jax.random.split(key, 24)
    n_pages = PAST_LEN // PAGE_SIZE
    n_phys = (DEC_BATCH * n_pages * 5) // 4

    def nrm(k, shape, scale=1.0):
        return jax.random.normal(k, shape, f32) * scale

    page_table = jax.random.permutation(ks[7], n_phys)[:DEC_BATCH * n_pages].reshape(DEC_BATCH, n_pages).astype(jnp.int32)
    a_init = jax.random.uniform(ks[17], (N_ODD, DN_HEADS), f32, 1.0, 16.0)
    dt = jnp.exp(jax.random.uniform(ks[18], (N_ODD, DN_HEADS), f32, math.log(1e-3), math.log(1e-1)))
    return {
        'x_prompt': nrm(ks[0], (BATCH, SEQ, D_MODEL)),
        'x_sample': nrm(ks[1], (DEC_BATCH, DEC_SEQ, D_MODEL)),
        'cache_pool': nrm(ks[2], (N_EVEN, DEC_BATCH, POOL_BUF, POOL_WIDTH)),
        'cache_k': nrm(ks[3], (N_EVEN, n_phys, PAGE_SIZE, SB_HEADS, SB_HEAD_DIM)),
        'cache_v': nrm(ks[4], (N_EVEN, n_phys, PAGE_SIZE, SB_HEADS, SB_HEAD_DIM)),
        'state_conv': nrm(ks[5], (N_ODD, DEC_BATCH, CONV_WIDTH - 1, DN_CONV_DIM)),
        'state_delta': nrm(ks[6], (N_ODD, DEC_BATCH, DN_HEADS, DN_KEY_DIM, DN_VAL_DIM), 0.1),
        'page_table': page_table,
        'norm_even': 1.0 + nrm(ks[8], (N_EVEN, D_MODEL), 0.1),
        'w_in_even': nrm(ks[9], (N_EVEN, D_MODEL, EVEN_IN), D_MODEL ** -0.5),
        'w_pool': nrm(ks[10], (N_EVEN, N_POOL_GROUPS, POOL_GROUP, POOL_GROUP), POOL_GROUP ** -0.5),
        'pool_scale': 1.0 + nrm(ks[11], (N_EVEN, POOL_WIDTH), 0.1),
        'q_norm': 1.0 + nrm(ks[12], (N_EVEN, SB_HEAD_DIM), 0.1),
        'k_norm': 1.0 + nrm(ks[13], (N_EVEN, SB_HEAD_DIM), 0.1),
        'sb_bias': SB_BIAS_INIT + nrm(ks[22], (N_EVEN, SB_HEADS), 0.1),
        'w_out_even': nrm(ks[14], (N_EVEN, EVEN_MIX, D_MODEL), EVEN_MIX ** -0.5),
        'norm_odd': 1.0 + nrm(ks[15], (N_ODD, D_MODEL), 0.1),
        'w_in_odd': nrm(ks[16], (N_ODD, D_MODEL, ODD_IN), D_MODEL ** -0.5),
        'conv_w': nrm(ks[19], (N_ODD, CONV_WIDTH, DN_CONV_DIM), 0.5),
        'a_log': jnp.log(a_init),
        'dt_bias': dt + jnp.log(-jnp.expm1(-dt)),
        'o_norm': 1.0 + nrm(ks[20], (N_ODD, DN_VAL_DIM), 0.1),
        'w_out_odd': nrm(ks[21], (N_ODD, DN_V, D_MODEL), DN_V ** -0.5),
    }

def reference(x_prompt, x_sample, cache_pool, cache_k, cache_v, state_conv, state_delta, page_table,
              norm_even, w_in_even, w_pool, pool_scale, q_norm, k_norm, sb_bias, w_out_even,
              norm_odd, w_in_odd, conv_w, a_log, dt_bias, o_norm, w_out_odd):
    n_dec = x_sample.shape[0]
    past_len = page_table.shape[1] * cache_k.shape[2]
    bp = x_prompt.shape[0]
    hp, hs = x_prompt, x_sample
    pool_p, pool_s, kp_l, vp_l, ks_l, vs_l = [], [], [], [], [], []
    conv_p, conv_s, dp_l, ds_l = [], [], [], []
    for layer in range(DEPTH):
        i = layer // 2
        if layer % 2 == 0:
            ev = (norm_even[i], w_in_even[i], w_pool[i], pool_scale[i], q_norm[i], k_norm[i], sb_bias[i], w_out_even[i])
            zero_buf = jnp.zeros((bp, POOL_BUF, POOL_WIDTH), hp.dtype)
            hp, pb, kn, vn = even_layer(hp, 0, zero_buf, None, None, *ev)
            pool_p.append(pb); kp_l.append(kn); vp_l.append(vn)
            k_past = cache_k[i][page_table].reshape(n_dec, past_len, SB_HEADS, SB_HEAD_DIM)
            v_past = cache_v[i][page_table].reshape(n_dec, past_len, SB_HEADS, SB_HEAD_DIM)
            hs, pb, kn, vn = even_layer(hs, past_len, cache_pool[i], k_past, v_past, *ev)
            pool_s.append(pb); ks_l.append(kn); vs_l.append(vn)
        else:
            od = (norm_odd[i], w_in_odd[i], conv_w[i], a_log[i], dt_bias[i], o_norm[i], w_out_odd[i])
            zero_conv = jnp.zeros((bp, CONV_WIDTH - 1, DN_CONV_DIM), hp.dtype)
            zero_state = jnp.zeros((bp, DN_HEADS, DN_KEY_DIM, DN_VAL_DIM), hp.dtype)
            hp, cb, st = odd_layer(hp, zero_conv, zero_state, *od)
            conv_p.append(cb); dp_l.append(st)
            hs, cb, st = odd_layer(hs, state_conv[i], state_delta[i], *od)
            conv_s.append(cb); ds_l.append(st)
    return (hp, hs,
            jnp.stack(pool_p), jnp.stack(pool_s),
            jnp.stack(kp_l), jnp.stack(vp_l), jnp.stack(ks_l), jnp.stack(vs_l),
            jnp.stack(conv_p), jnp.stack(conv_s),
            jnp.stack(dp_l), jnp.stack(ds_l))


_drawn_inputs = setup_inputs


def setup_inputs(seed=0):
    import zlib

    import numpy as np

    out = dict(_drawn_inputs(seed))
    spreads = {}
    factors = {'cache_k': 6.037, 'cache_v': 4.905, 'q_norm': 8.0, 'sb_bias': 8.0}
    for name, (base, spread) in spreads.items():
        noise = np.random.default_rng([zlib.crc32(name.encode()), seed]).standard_normal(out[name].shape)
        drawn = base * np.exp(spread * noise) if base else spread * noise
        out[name] = __import__('jax').numpy.asarray(drawn.astype(out[name].dtype))
    for name, factor in factors.items():
        out[name] = (out[name] * factor).astype(out[name].dtype)
    return out
```

```python
from contextlib import ExitStack

import numpy as np

import concourse.bass as bass
import concourse.mybir as mybir

F32 = mybir.dt.float32
F32R = mybir.dt.float32r
BF16 = mybir.dt.bfloat16
I32 = mybir.dt.int32
ALU = mybir.AluOpType
ACT = mybir.ActivationFunctionType
AX = mybir.AxisListType

P = 128
DM = 1024
KC = DM // P
SEQ = 2048
NT = SEQ // P
DB, DS = 8, 4
NS = DB * DS
PAST = 2048
PAGE = 128
NPG = PAST // PAGE
EPS = 1e-6
H0, HD = 8, 64
W0 = H0 * HD
NG, WIN = 4, (2, 4, 8, 16)
BUF = max(WIN) - 1
EVEN_IN = W0 + 3 * W0 + DM
H1, D1 = 8, 128
QK = H1 * D1
CONV = 3 * QK
CW = 4
ODD_IN = CONV + QK + 2 * H1
LEVELS = 7
NEG = -1e30



def constants():
    j, i = np.arange(P)[:, None], np.arange(P)[None, :]
    out = {"ident": (j == i)}
    first, cur, prev, samp, samp_buf = ([] for _ in range(5))
    for w in WIN:
        own = (i - j >= 0) & (i - j < w)
        first.append(own / np.minimum(i + 1, w) - (i == j))
        cur.append(own / w - (i == j))
        prev.append((i + P - j < w) / w)
        same = (i // DS == j // DS) & (i < NS) & (j < NS)
        samp.append((same & own) / w - ((i == j) & (i < NS)))
        dist = i % DS + BUF - j % BUF
        samp_buf.append(((j // BUF == i // DS) & (i < NS) & (j < DB * BUF) & (dist < w)) / w)
    for name, band in (("band_first", first), ("band", cur), ("band_prev", prev), ("band_samp", samp),
                       ("band_buf", samp_buf)):
        out[name] = np.concatenate(band, 1)
    y = np.arange(7 * P)[None, :]
    out["mask_q"] = np.where(y - 3 * P >= j, NEG, 0.0)
    key = np.arange(2 * NS)[None, :]
    g, kb, kt = key // NS, key % NS // DS, key % DS
    out["mask_new"] = np.where((kb == 4 * g + j // NS) & (kt < j % DS), 0.0, NEG)
    out["own_head"] = (np.arange(W0)[None, :] // HD == (j % NS) // DS)
    out["to_token"] = ((kb == 4 * g + j // NS) & (kt == j % DS))
    out["row_head"] = (j == i % NS // DS)
    out["tri"] = (j <= i)
    out["mask_tri"] = np.tile(np.where(j <= i, 0.0, NEG), (1, 4))
    same = (i // DS == j // DS)
    out["tri_samp"] = (j <= i) & same
    out["mask_tri_samp"] = np.where((j <= i) & same, 0.0, NEG)
    out["last_samp"] = (i // DS == j // DS) * 1.0
    for n in range(LEVELS):
        s = 1 << n
        out[f"level{n}"] = -1.0 * ((i // (2 * s) == j // (2 * s)) & (i // s % 2 == 1) & (j // s % 2 == 0))
    out["strict_samp"] = -1.0 * ((j < i) & same)
    out["own_cols"] = (np.arange(DB * NS)[None, :] // NS == np.arange(DB * NS)[None, :] % NS // DS)
    out["own_batch"] = (np.arange(DB)[None, :] == j // DS)
    at, parts = {}, []
    n = 0
    for name, a in out.items():
        a = np.ascontiguousarray(np.broadcast_to(a, (P, a.shape[1])), dtype=np.float32)
        at[name] = (n, n + a.shape[1])
        n += a.shape[1]
        parts.append(a)
    return np.concatenate(parts, 1), at


def load_all(eng, sem, pairs):
    for dst, src in pairs:
        eng.dma_start(dst, src, allow_slow_non_contiguous=True).then_inc(sem, 16)
    return 16 * len(pairs)


def settle(eng, sem):
    eng.sem_inc(sem, 1)


class Stage:

    def __init__(self, nc, tag):
        self.nc, self.tag, self.ctx = nc, tag, ExitStack()
        self.sems = []

    def __enter__(self):
        self.ctx.__enter__()
        return self

    def __exit__(self, *a):
        self.ctx.__exit__(*a)
        self.nc.clear_and_free_semaphores(self.sems)
        self.nc.all_engine_barrier()

    def sb(self, name, shape, dt=F32):
        return self.ctx.enter_context(self.nc.sbuf_tensor(f"{self.tag}_{name}", shape, dt))

    def ps(self, name, shape=(P, 512)):
        return self.ctx.enter_context(self.nc.psum_tensor(f"{self.tag}_ps_{name}", list(shape), F32))

    def sem(self, name):
        self.sems.append(self.nc.alloc_semaphore(name=f"{self.tag}_{name}"))
        return self.sems[-1]

    def block(self):
        return self.ctx.enter_context(self.nc.Block())


def tiles_in_order(eng, body):
    for t in range(3):
        body(t, t % 2, t // 2)
    with eng.Fori(1, NT // 2 - 1) as i:
        body(i * 2 + 1, 1, i)
        body(i * 2 + 2, 0, i + 1)
    for t in (NT - 1, NT):
        body(t, t % 2, t // 2)


def stage_a(nc, io, cat, kT):
    with Stage(nc, "A") as st:
        sb, ps, sem = st.sb, st.ps, st.sem
        w = sb("w", [P, KC, EVEN_IN])
        w_pool = sb("w_pool", [P, NG, P])
        ident = sb("ident", [P, P])
        g_in = sb("g_in", [P, KC])
        g_qk = sb("g_qk", [P, 2, HD])
        scale = sb("scale", [P, NG * P])
        bands = {n: sb(n, [P, NG, P]) for n in ("band_first", "band", "band_prev", "band_samp", "band_buf")}
        buf_in = sb("buf_in", [P, W0])
        x = sb("x", [P, 2, DM])
        xT = sb("xT", [P, 2, KC, P])
        junk = sb("junk", [P, DM])
        ss = sb("ss", [P, 2])
        ms = sb("ms", [P, 2])
        rstd = sb("rstd", [P, 2])
        half = sb("half", [P, 16])
        qk = sb("qk", [P, 2 * W0])
        qkn = sb("qkn", [P, 2 * W0])
        hss = sb("hss", [P, 16])
        hms = sb("hms", [P, 16])
        hr = sb("hr", [P, 16])
        u = sb("u", [P, 2, W0])
        v = sb("v", [P, W0])
        gate = sb("gate", [P, DM])
        dT = sb("dT", [P, NG, P])
        mix = sb("mix", [P, W0])
        qT = sb("qT", [P, 4, P])
        p_x = [ps(f"x{i}") for i in range(2)]
        p_pj = [ps(f"pj{i}") for i in range(3)]
        p_q, p_k, p_pool = ps("q"), ps("k"), ps("pool")

        s_c = sem("const_in")
        s_w = [sem(f"w_in{k}") for k in range(2)]
        s_x = [sem(f"x_in{p}") for p in range(2)]
        s_half, s_wp = sem("half_set"), sem("w_pool_scaled")
        s_xp, s_xT = sem("x_turned"), sem("xT_ready")
        s_ss, s_ms, s_rs = sem("squares_summed"), sem("mean_square"), sem("rstd_ready")
        s_pj = [sem(f"projected{n}") for n in range(6)]
        s_ev = [sem(f"block_out{n}") for n in range(6)]
        s_sq, s_hs, s_hm, s_hr = sem("head_squares"), sem("head_sums"), sem("head_means"), sem("head_rstd")
        s_qk1, s_qkn = sem("qk_scaled"), sem("qk_normed")
        s_qt, s_kt, s_qT, s_kT = sem("q_turned"), sem("k_turned"), sem("qT_ready"), sem("kT_ready")
        s_d, s_dT, s_y, s_mix = sem("pooled"), sem("dT_ready"), sem("pool_out"), sem("mix_ready")
        s_ko, s_vo, s_qo, s_mo, s_go, s_uo = (sem(n) for n in (
            "k_stored", "v_stored", "q_stored", "mix_stored", "gate_stored", "u_stored"))
        s_zero = sem("pad_zeroed")
        s_go_on = sem("pool_waits_settled")
        s_sp = sem("sync_waits_settled")
        block = st.block()
        cols = [W0, 2 * W0, 0, 4 * W0, 5 * W0, 3 * W0]

        def const(name):
            a, b = cat[name]
            return io["consts"][:, a:b]

        singles = [(ident[:, :], const("ident")),
                   (g_in[:, :], io["norm_even"].rearrange("o (k p) -> p (o k)", p=P)),
                   (g_qk[:, 0], io["q_norm"].to_broadcast([P, HD])),
                   (g_qk[:, 1], io["k_norm"].to_broadcast([P, HD])),
                   (scale[:, :], io["pool_scale"].to_broadcast([P, NG * P])),
                   (w_pool[:, :, :], io["w_pool"].rearrange("o g c d -> c (o g) d")),
                   (buf_in[0:DB * BUF, :], io["cache_pool"].rearrange("o b r c -> (o b r) c"))]
        singles += [(bands[n][:, :, :], const(n).rearrange("p (g i) -> p g i", g=NG)) for n in bands]

        @block.sync
        def _(sp):
            def load_x(t, slot, samples=False):
                if samples:
                    sp.wait_ge(s_zero, 1)
                    sp.dma_start(x[0:NS, slot, :], io["x_sample"].rearrange("b t d -> (b t) d")).then_inc(s_x[slot], 16)
                else:
                    sp.dma_start(x[:, slot, :], io["x_prompt"][0, bass.ds(t * P, P), :]).then_inc(s_x[slot], 16)

            load_x(0, 0)
            n_in = load_all(sp, s_c, singles)
            wv = io["w_in_even"].rearrange("o (k p) n -> p (o k) n", p=P)
            for hf in range(2):
                sp.dma_start(w[:, 4 * hf:4 * hf + 4, :], wv[:, 4 * hf:4 * hf + 4, :]).then_inc(s_w[hf], 16)

            def body(t, slot, nth):
                first = isinstance(t, int) and t == 0
                last = isinstance(t, int) and t == NT
                if not (isinstance(t, int) and t >= NT):
                    if not first:
                        sp.wait_ge(s_xp, t)
                        sp.wait_ge(s_ss, t)
                    load_x(t + 1, 1 - slot, samples=isinstance(t, int) and t == NT - 1)
                n = NS if last else P
                k_out, v_out = (io[a].rearrange("o b t h d -> (o b t) (h d)")
                                for a in (("k_sample", "v_sample") if last else ("k_prompt", "v_prompt")))
                row0 = 0 if last else t * P
                if last or (isinstance(t, int) and t == NT - 1):
                    sp.wait_ge(s_ev[2], t + 1)
                    if last:
                        for b in range(DB):
                            sp.dma_start(io["pool_sample"][0, b, BUF - DS:BUF, :],
                                         u[b * DS:(b + 1) * DS, slot, :]).then_inc(s_uo, 16)
                    else:
                        sp.dma_start(io["pool_prompt"][0, 0, :, :], u[P - BUF:P, slot, :]).then_inc(s_uo, 16)
                sp.wait_ge(s_ev[5], t + 1)
                sp.dma_start(v_out[bass.ds(row0, n), :], v[0:n, :]).then_inc(s_vo, 16)
                sp.wait_ge(s_qkn, t + 1)
                sp.dma_start(k_out[bass.ds(row0, n), :], qkn[0:n, W0:2 * W0]).then_inc(s_ko, 16)
                sp.wait_ge(s_ev[4], t + 1)
                sp.dma_start(io["mixgate"][bass.ds(t, 1), :, W0:DM].rearrange("o p n -> p (o n)"),
                             gate[:, W0:DM]).then_inc(s_go, 16)
                sp.wait_ge(s_qT, t + 1)
                sp.dma_start(io["q_turned"][bass.ds(t * 4, 4), :, :].rearrange("q p n -> p q n"),
                             qT[:, :, :]).then_inc(s_qo, 16)
                sp.wait_ge(s_mix, t + 1)
                settle(sp, s_sp)
                sp.dma_start(io["mixgate"][bass.ds(t, 1), :, 0:W0].rearrange("o p n -> p (o n)"),
                             mix[:, :]).then_inc(s_mo, 16)

            tiles_in_order(sp, body)
            for b in range(DB):
                sp.dma_start(io["pool_sample"][0, b, 0:BUF - DS, :], io["cache_pool"][0, b, DS:BUF, :]).then_inc(s_uo, 16)
            sp.wait_ge(s_uo, 16 * (2 * DB + 1))
            for s in (s_vo, s_ko, s_go, s_qo, s_mo):
                sp.wait_ge(s, 16 * (NT + 1))

        @block.tensor
        def _(pe):
            def post(t, slot, kind):
                pe.wait_ge(s_qkn, t + 1)
                if kind != "first":
                    pe.wait_ge(s_qT, t)
                for q in range(4):
                    mm = pe.transpose(p_q[:, q * P:(q + 1) * P], qkn[:, q * P:(q + 1) * P], ident[:, :])
                mm.then_inc(s_qt, 1)
                pe.wait_ge(s_ev[2], t + 1)
                if kind != "first":
                    pe.wait_ge(s_mix, t)
                band = bands[{"first": "band_first", "samples": "band_samp"}.get(kind, "band")]
                for g in range(NG):
                    mm = pe.matmul(p_pool[:, g * P:(g + 1) * P], u[:, slot, g * P:(g + 1) * P], band[:, g, :],
                                   start=True, stop=(kind == "first"))
                    if kind == "samples":
                        n = DB * BUF
                        mm = pe.matmul(p_pool[:, g * P:(g + 1) * P], buf_in[0:n, g * P:(g + 1) * P],
                                       bands["band_buf"][0:n, g, :], start=False, stop=True)
                    elif kind != "first":
                        mm = pe.matmul(p_pool[:, g * P:(g + 1) * P], u[:, 1 - slot, g * P:(g + 1) * P],
                                       bands["band_prev"][:, g, :], start=False, stop=True)
                mm.then_inc(s_d, 1)
                if kind != "first":
                    pe.wait_ge(s_kT, t)
                for q in range(4):
                    mm = pe.transpose(p_k[:, q * P:(q + 1) * P], qkn[:, W0 + q * P:W0 + (q + 1) * P], ident[:, :])
                mm.then_inc(s_kt, 1)
                pe.wait_ge(s_dT, t + 1)
                for g in range(NG):
                    mm = pe.matmul(p_pool[:, g * P:(g + 1) * P], dT[:, g, :], w_pool[:, g, :], start=True, stop=True)
                mm.then_inc(s_y, 1)

            def body(t, slot, nth):
                first = isinstance(t, int) and t == 0
                if first:
                    pe.wait_ge(s_c, 16 * len(singles))
                    pe.wait_ge(s_wp, 1)
                pe.wait_ge(s_x[slot], nth * 16 + 16)
                if not first:
                    pe.wait_ge(s_xT, t * 2)
                for k in range(KC):
                    mm = pe.transpose(p_x[k // 4][:, k % 4 * P:(k % 4 + 1) * P], x[:, slot, k * P:(k + 1) * P],
                                      ident[:, :])
                mm.then_inc(s_xp, 1)
                if not first:
                    post(t - 1, 1 - slot, "first" if isinstance(t, int) and t == 1 else "mid")
                pe.wait_ge(s_xT, t * 2 + 2)
                if first:
                    for hf in range(2):
                        pe.wait_ge(s_w[hf], 16)
                for n in range(6):
                    if n >= 3:
                        pe.wait_ge(s_ev[n - 3], t + 1)
                    elif not first:
                        pe.wait_ge(s_ev[n + 3], t)
                    for k in range(KC):
                        mm = pe.matmul(p_pj[n % 3][:, :], xT[:, slot, k, :], w[:, k, cols[n]:cols[n] + W0],
                                       start=(k == 0), stop=(k == KC - 1))
                    mm.then_inc(s_pj[n], 1)

            tiles_in_order(pe, body)
            post(NT, 0, "samples")

        @block.vector
        def _(dve):
            dve.wait_ge(s_c, 16 * len(singles))
            dve.tensor_tensor(w_pool[:, :, :], w_pool[:, :, :], scale[:, :].rearrange("p (g i) -> p g i", g=NG),
                              ALU.mult).then_inc(s_wp, 1)

            def post(t):
                dve.wait_ge(s_d, t + 1)
                dve.tensor_copy(dT[:, :, :], p_pool[:, :].rearrange("p (g i) -> p g i", g=NG)).then_inc(s_dT, 1)
                dve.wait_ge(s_y, t + 1)
                dve.wait_ge(s_ev[3], t + 1)
                dve.wait_ge(s_mo, t * 16)
                dve.tensor_tensor(mix[:, :], p_pool[:, :], gate[:, 0:W0], ALU.mult).then_inc(s_mix, 1)

            def body(t, slot, nth):
                first = isinstance(t, int) and t == 0
                dve.wait_ge(s_xp, t + 1)
                if not first:
                    dve.wait_ge(s_pj[5], t)
                for hf in range(2):
                    dve.tensor_tensor(xT[:, slot, 4 * hf:4 * hf + 4, :],
                                      p_x[hf][:, :].rearrange("p (k i) -> p k i", k=4),
                                      g_in[:, 4 * hf:4 * hf + 4].unsqueeze(2).to_broadcast([P, 4, P]),
                                      ALU.mult).then_inc(s_xT, 1)
                if not first:
                    post(t - 1)
                dve.wait_ge(s_ev[0], t + 1)
                dve.wait_ge(s_ev[1], t + 1)
                if not first:
                    dve.wait_ge(s_ko, t * 16)
                    dve.wait_ge(s_kt, t)
                dve.tensor_tensor(qkn[:, :], qk[:, :], qk[:, :], ALU.mult).then_inc(s_sq, 1)
                dve.wait_ge(s_sq, t + 1)
                dve.tensor_reduce(hss[:, :], qkn[:, :].rearrange("p (h d) -> p h d", d=HD), AX.X,
                                  ALU.add).then_inc(s_hs, 1)
                dve.wait_ge(s_hr, t + 1)
                dve.wait_ge(s_hs, t + 1)
                dve.tensor_tensor(qkn[:, :].rearrange("p (h d) -> p h d", d=HD),
                                  qk[:, :].rearrange("p (h d) -> p h d", d=HD),
                                  hr[:, :].unsqueeze(2).to_broadcast([P, 16, HD]), ALU.mult).then_inc(s_qk1, 1)
                dve.wait_ge(s_qk1, t + 1)
                q4 = qkn[:, :].rearrange("p (a h d) -> p a h d", a=2, d=HD)
                dve.tensor_tensor(q4, q4, g_qk[:, :, :].unsqueeze(2).to_broadcast([P, 2, H0, HD]),
                                  ALU.mult).then_inc(s_qkn, 1)

            tiles_in_order(dve, body)
            post(NT)

        @block.scalar
        def _(act):
            def post(t, first=False):
                act.wait_ge(s_qt, t + 1)
                act.wait_ge(s_qo, t * 16)
                act.activation(qT[:, :, :], p_q[:, :].rearrange("p (q i) -> p q i", q=4), ACT.Copy).then_inc(s_qT, 1)
                act.wait_ge(s_kt, t + 1)
                act.activation(kT[:, :, bass.ds(t * P, P)], p_k[:, :].rearrange("p (q i) -> p q i", q=4),
                               ACT.Copy).then_inc(s_kT, 1)

            def body(t, slot, nth):
                first = isinstance(t, int) and t == 0
                act.wait_ge(s_x[slot], nth * 16 + 16)
                if not first:
                    act.wait_ge(s_ss, t)
                    act.wait_ge(s_ms, t)
                act.activation(junk[:, :], x[:, slot, :], ACT.Square, accum_out=ss[:, slot:slot + 1]).then_inc(s_ss, 1)
                if not first:
                    post(t - 1)
                act.wait_ge(s_rs, t + 1)
                dst = [qk[:, 0:W0], qk[:, W0:2 * W0], u[:, slot, :], gate[:, 0:W0], gate[:, W0:DM], v[:, :]]
                for n in range(6):
                    act.wait_ge(s_pj[n], t + 1)
                    if not first:
                        if n < 2:
                            act.wait_ge(s_qk1, t)
                        elif n == 3:
                            act.wait_ge(s_mix, t)
                        elif n == 4:
                            act.wait_ge(s_go, t * 16)
                        elif n == 5:
                            act.wait_ge(s_vo, t * 16)
                    act.activation(dst[n], p_pj[n % 3][:, :], ACT.Silu if n in (3, 4) else ACT.Copy,
                                   scale=rstd[:, slot:slot + 1]).then_inc(s_ev[n], 1)

            tiles_in_order(act, body)
            post(NT)

        @block.gpsimd
        def _(pool):
            pool.memset(half[:, :], -0.5).then_inc(s_half, 1)
            pool.wait_ge(s_half, 1)

            def body(t, slot, nth):
                first = isinstance(t, int) and t == 0
                if isinstance(t, int) and t == NT - 1:
                    pool.wait_ge(s_xp, NT - 1)
                    pool.wait_ge(s_ss, NT - 1)
                    pool.memset(x[:, 0, :], 0.0).then_inc(s_zero, 1)
                pool.wait_ge(s_ss, t + 1)
                if not first:
                    pool.wait_ge(s_ev[5], t)
                settle(pool, s_go_on)
                pool.tensor_scalar(ms[:, slot:slot + 1], ss[:, slot:slot + 1], 1.0 / DM, EPS, ALU.mult,
                                   ALU.add).then_inc(s_ms, 1)
                pool.wait_ge(s_ms, t + 1)
                pool.tensor_tensor(rstd[:, slot:slot + 1], ms[:, slot:slot + 1], half[:, 0:1],
                                   ALU.pow).then_inc(s_rs, 1)
                pool.wait_ge(s_hs, t + 1)
                if not first:
                    pool.wait_ge(s_qk1, t)
                settle(pool, s_go_on)
                pool.tensor_scalar(hms[:, :], hss[:, :], 1.0 / HD, EPS, ALU.mult, ALU.add).then_inc(s_hm, 1)
                pool.wait_ge(s_hm, t + 1)
                pool.tensor_tensor(hr[:, :], hms[:, :], half[:, :], ALU.pow).then_inc(s_hr, 1)

            tiles_in_order(pool, body)




def at_least(eng, sem, value):
    if not isinstance(value, int) or value > 0:
        eng.wait_ge(sem, value)


def stage_b(nc, io, cat, kT, o_all):
    with Stage(nc, "B") as st:
        sb, ps, sem = st.sb, st.ps, st.sem
        KB = 4
        RING = 4
        v_all = sb("v", [P, NT, W0])
        ident = sb("ident", [P, P])
        ident_b = sb("ident_b", [P, P], BF16)
        mask_f = sb("mask_f", [P, 7 * P])
        mask = sb("mask", [P, 7 * P], BF16)
        bias = sb("bias", [P, 2, H0])
        qz = sb("qz", [P, 2, 4, 2, P])
        keep = sb("keep", [P, RING, KB * P])
        take = sb("take", [P, RING, KB * P])
        left = sb("left", [P, 2, NT * P + 1])
        a = sb("a", [P, 2, KB * P])
        aT = sb("aT", [P, 2, KB, P])
        p_z = [ps(f"z{i}") for i in range(RING)]
        p_a = [ps(f"a{i}") for i in range(2)]
        p_o = [ps(f"o{i}") for i in range(2)]
        s_in, s_set, s_cast = sem("loaded"), sem("set"), sem("cast")
        s_q = [sem(f"q_in{s}") for s in range(2)]
        s_z, s_keep, s_take, s_scan, s_a = (sem(n) for n in ("scored", "keep", "take", "scanned", "weighed"))
        s_at, s_aT, s_av, s_o = (sem(n) for n in ("a_turned", "aT_ready", "a_times_v", "o_ready"))
        block = st.block()
        END = NT * P

        def const(name):
            return io["consts"][:, cat[name][0]:cat[name][1]]

        loads = [(ident[:, :], const("ident")), (mask_f[:, :], const("mask_q")),
                 (bias[:, 0, :], io["sb_bias"].to_broadcast([P, H0])),
                 (v_all[:, :, :], io["v_prompt"].rearrange("o b (t p) h d -> p (o b t) (h d)", p=P))]

        def bodies(eng, body):
            body(0, 0, 1)
            body(2, 1, 1)
            for c in range(2, 5):
                with eng.Fori(0, 2) as i:
                    body(i * 2 + 4 * (c - 1), i + 2 * (c - 1), c)

        def block_list(t, c):
            base = sum(32 * k for k in range(1, c))
            n0 = (t - 4 * (c - 1)) * 8 * c + base
            return n0, [(s, h, j) for s in range(2) for h in range(H0) for j in range(c)]

        @block.sync
        def _(sp):
            n = load_all(sp, s_in, loads)
            sp.wait_ge(s_set, 2)

            def body(t, nth, c):
                for s in range(2):
                    at_least(sp, s_o, t * 8 + 8 * (s - 1))
                    for hh in range(2):
                        sp.dma_start(qz[64 * hh:64 * hh + 64, s, :, hh, :],
                                     io["q_turned"][bass.ds(t * 4 + 4 * s, 4), 64 * hh:64 * hh + 64, :].rearrange(
                                         "q p n -> p q n")).then_inc(s_q[s], 16)

            bodies(sp, body)

        @block.tensor
        def _(pe):
            pe.wait_ge(s_in, 16 * len(loads))
            pe.wait_ge(s_cast, 2)

            def body(t, nth, c):
                n0, blocks = block_list(t, c)
                for m in range(len(blocks) + 4):
                    if m < len(blocks):
                        s, h, j = blocks[m]
                        if h == 0 and j == 0:
                            pe.wait_ge(s_q[s], nth * 32 + 32)
                        at_least(pe, s_take, n0 + (m - 3))
                        kb = c - 1 - j
                        mm = pe.matmul(p_z[m % RING][:, :], qz[:, s, h // 2, h % 2, :],
                                       kT[:, h // 2, kb * KB * P:(kb + 1) * KB * P], start=True, stop=(j > 0))
                        if j == 0:
                            off = (t - 4 * (c - 1)) * -P + (3 - s) * P
                            mm = pe.matmul(p_z[m % RING][:, :], ident_b[:, :], mask[:, bass.ds(off, KB * P)],
                                           start=False, stop=True)
                        mm.then_inc(s_z, 1)
                    if 3 <= m < len(blocks) + 3:
                        k = m - 3
                        pe.wait_ge(s_a, n0 + (k + 1))
                        at_least(pe, s_aT, n0 + (k - 1))
                        for q in range(KB):
                            mm = pe.transpose(p_a[k % 2][:, q * P:(q + 1) * P], a[:, k % 2, q * P:(q + 1) * P],
                                              ident[:, :])
                        mm.then_inc(s_at, 1)
                    if m >= 4:
                        k = m - 4
                        s, h, j = blocks[k]
                        pe.wait_ge(s_aT, n0 + (k + 1))
                        if j == 0:
                            at_least(pe, s_o, t * 8 + (8 * s + h - 1))
                        kb = c - 1 - j
                        for q in range(KB):
                            mm = pe.matmul(p_o[h % 2][:, 0:HD], aT[:, k % 2, q, :],
                                           v_all[:, kb * KB + q, h * HD:(h + 1) * HD],
                                           start=(j == 0 and q == 0), stop=(j == c - 1 and q == KB - 1))
                        mm.then_inc(s_av, 1)

            bodies(pe, body)

        @block.scalar
        def _(act):
            act.wait_ge(s_cast, 3)

            def body(t, nth, c):
                n0, blocks = block_list(t, c)
                for m in range(len(blocks) + 3):
                    if m < len(blocks):
                        s, h, j = blocks[m]
                        act.wait_ge(s_z, n0 + (m + 1))
                        at_least(act, s_scan, n0 + (m - 3))
                        act.activation(keep[:, m % RING, :], p_z[m % RING][:, :], ACT.Sigmoid,
                                       scale=-(HD ** -0.5), bias=bias[:, 1, h:h + 1]).then_inc(s_keep, 1)
                        at_least(act, s_a, n0 + (m - 3))
                        act.activation(take[:, m % RING, :], p_z[m % RING][:, :], ACT.Sigmoid,
                                       scale=HD ** -0.5, bias=bias[:, 0, h:h + 1]).then_inc(s_take, 1)
                    if m >= 3:
                        k = m - 3
                        act.wait_ge(s_at, n0 + (k + 1))
                        at_least(act, s_av, n0 + (k - 1))
                        act.activation(aT[:, k % 2, :, :], p_a[k % 2][:, :].rearrange("p (q i) -> p q i", q=KB),
                                       ACT.Copy).then_inc(s_aT, 1)

            bodies(act, body)

        @block.vector
        def _(dve):
            dve.wait_ge(s_in, 16 * len(loads))
            dve.tensor_copy(ident_b[:, :], ident[:, :]).then_inc(s_cast, 1)
            dve.tensor_copy(mask[:, :], mask_f[:, :]).then_inc(s_cast, 1)
            dve.tensor_scalar(bias[:, 1, :], bias[:, 0, :], -1.0, None, ALU.mult).then_inc(s_cast, 1)
            dve.wait_ge(s_set, 2)

            def body(t, nth, c):
                n0, blocks = block_list(t, c)

                def out(k):
                    s, h, j = blocks[k]
                    if j == c - 1:
                        dve.wait_ge(s_av, n0 + (k + 1))
                        dve.tensor_copy(o_all[:, bass.ds(t + s, 1), h * HD:(h + 1) * HD].rearrange(
                            "p o d -> p (o d)"), p_o[h % 2][:, 0:HD]).then_inc(s_o, 1)

                for m in range(len(blocks)):
                    s, h, j = blocks[m]
                    lo = END - (j + 1) * KB * P
                    buf = left[:, h % 2, :]
                    dve.wait_ge(s_keep, n0 + (m + 1))
                    at_least(dve, s_a, n0 + m)
                    dve.tensor_tensor_scan(buf[:, lo:lo + KB * P][:, ::-1], keep[:, m % RING, ::-1],
                                           keep[:, m % RING, ::-1], buf[:, lo + KB * P:lo + KB * P + 1],
                                           ALU.mult, ALU.bypass).then_inc(s_scan, 1)
                    dve.wait_ge(s_scan, n0 + (m + 1))
                    dve.wait_ge(s_take, n0 + (m + 1))
                    at_least(dve, s_at, n0 + (m - 1))
                    dve.tensor_tensor(a[:, m % 2, :], take[:, m % RING, :], buf[:, lo + 1:lo + 1 + KB * P],
                                      ALU.mult).then_inc(s_a, 1)
                    if m >= 5:
                        out(m - 5)
                for k in range(len(blocks) - 5, len(blocks)):
                    out(k)

            bodies(dve, body)

        @block.gpsimd
        def _(pool):
            pool.memset(qz[:, :, :, :, :], 0.0).then_inc(s_set, 1)
            pool.memset(left[:, :, END:END + 1], 1.0).then_inc(s_set, 1)


def stage_s(nc, io, cat, kT, o_all):
    with Stage(nc, "S") as st:
        sb, ps, sem = st.sb, st.ps, st.sem
        GB = 4
        GROUPS = DB // GB
        RING = 8
        NK = PAST + NS
        PB = 4
        JB = NPG // PB
        n_phys = io["cache_k"].shape[1]
        table = sb("table", [1, DB * NPG], I32)
        ident = sb("ident", [P, P])
        mask_new = sb("mask_new", [P, GROUPS * NS])
        own_head = sb("own_head", [P, W0])
        to_token = sb("to_token", [P, GROUPS * NS])
        row_head = sb("row_head", [P, P])
        bias_h = sb("bias_h", [H0, 1])
        bias = sb("bias", [P, 2])
        qT = sb("qT", [P, 4, NS])
        qz = sb("qz", [P, GB, 4, NS])
        v_new = sb("v_new", [NS, W0])
        kp = sb("kp", [P, RING, W0])
        vp = sb("vp", [P, RING, W0])
        kpT = sb("kpT", [P, 2, 4, P])
        keep = sb("keep", [P, NK])
        take = sb("take", [P, NK])
        z_new = sb("z_new", [P, NS])
        left = sb("left", [P, NK + 1])
        a = sb("a", [P, NK])
        aT = sb("aT", [P, NPG + 1, P])
        own = sb("own", [P, GROUPS, W0])
        p_t = [ps(f"t{i}") for i in range(2)]
        p_z, p_n, p_o, p_m = ps("z"), ps("n"), ps("o"), ps("m")
        p_a = [ps(f"a{i}") for i in range(2)]
        s_in, s_set, s_bias, s_b1, s_b2 = (sem(n) for n in ("loaded", "set", "bias_ps", "bias_neg", "bias_pos"))
        s_kp = [sem(f"k_page{i}") for i in range(RING)]
        s_vp = [sem(f"v_page{i}") for i in range(RING)]
        s_qz, s_tr, s_sc, s_nsc = (sem(n) for n in ("q_spread", "page_turned", "page_scored", "new_scored"))
        s_kT = [sem(f"kT_ready{i}") for i in range(2)]
        s_zn, s_keep, s_take, s_scan, s_a = (sem(n) for n in ("new_masked", "keep", "take", "scanned", "weighed"))
        s_at, s_aT, s_av, s_own, s_tok, s_out = (sem(n) for n in (
            "a_turned", "aT_ready", "a_times_v", "own_kept", "by_token", "o_written"))
        s_pe = sem("tensor_waits_settled")
        block = st.block()
        AT = NPG // 4 + 1

        def const(name):
            return io["consts"][:, cat[name][0]:cat[name][1]]

        loads = [(table[:, :], io["page_table"].rearrange("b n -> (b n)").unsqueeze(0)),
                 (ident[:, :], const("ident")), (mask_new[:, :], const("mask_new")),
                 (own_head[:, :], const("own_head")), (to_token[:, :], const("to_token")),
                 (row_head[:, :], const("row_head")), (bias_h[:, :], io["sb_bias"].rearrange("o h -> h o")),
                 (qT[:, :, :], io["q_turned"][4 * NT:4 * NT + 4, :, 0:NS].rearrange("q p n -> p q n")),
                 (v_new[:, :], io["v_sample"].rearrange("o b t h d -> (o b t) (h d)"))]

        @block.sync
        def _(sp):
            n_in = load_all(sp, s_in, loads)
            sp.wait_ge(s_in, n_in)

            def page(cache, ring, slot, s_page, g, bb, j):
                phys = sp.value_load(table[0:1, bass.ds(g * (GB * NPG) + j + bb * NPG, 1)], min_val=0, max_val=n_phys - 1)
                sp.dma_start(ring[:, slot, :], io[cache][0, bass.ds(phys, 1), :, :, :].rearrange(
                    "o p h d -> p (o h d)")).then_inc(s_page, 16)

            with sp.Fori(0, GROUPS) as g:
                with sp.Fori(0, JB) as jb:
                    for m in range(PB * GB):
                        sp.wait_ge(s_tr, g * (NPG * GB) + jb * (PB * GB) + (m + 1))
                        page("cache_k", kp, m % RING, s_kp[m % RING], g, m % GB, jb * PB + m // GB)
                for m in range(NPG * GB):
                    if m >= RING:
                        sp.wait_ge(s_av, g * (NPG * GB + GB) + (m - RING + 1))
                    page("cache_v", vp, m % RING, s_vp[m % RING], g, m % GB, m // GB)

        @block.tensor
        def _(pe):
            pe.wait_ge(s_in, 16 * len(loads))
            pe.matmul(p_m[:, 0:1], row_head[0:H0, :], bias_h[:, :], start=True, stop=True).then_inc(s_bias, 1)
            with pe.Fori(0, GROUPS) as g:
                pe.wait_ge(s_qz, g * 8 + 8)
                settle(pe, s_pe)
                with pe.Fori(0, JB) as jb:
                    n0 = g * (NPG * GB) + jb * (PB * GB)
                    for m in range(PB * GB + 1):
                        if m < PB * GB:
                            pe.wait_ge(s_kp[m % RING], (g * (NPG * GB) + jb * (PB * GB) + (m - m % RING)) * (16 // RING) + 16)
                            pe.wait_ge(s_kT[m % 2], g * (NPG * GB // 2) + jb * (PB * GB // 2) + m // 2)
                            for q in range(4):
                                mm = pe.transpose(p_t[m % 2][:, q * P:(q + 1) * P], kp[:, m % RING, q * P:(q + 1) * P],
                                                  ident[:, :])
                            mm.then_inc(s_tr, 1)
                        if m >= 1:
                            k = m - 1
                            j, bb = k // GB, k % GB
                            pe.wait_ge(s_kT[k % 2], g * (NPG * GB // 2) + jb * (PB * GB // 2) + (k // 2 + 1))
                            if k == 0:
                                pe.wait_ge(s_take, g * (JB + 1) + jb)
                            for q in range(4):
                                mm = pe.matmul(p_z[NS * bb:NS * bb + NS, j * P:(j + 1) * P], qz[:, bb, q, :],
                                               kpT[:, k % 2, q, :], start=(q == 0), stop=(q == 3))
                            mm.then_inc(s_sc, 1)
                for bb in range(GB):
                    for q in range(4):
                        mm = pe.matmul(p_n[NS * bb:NS * bb + NS, 0:NS], qz[:, bb, q, :], kT[:, q, PAST:PAST + NS],
                                       start=(q == 0), stop=(q == 3))
                mm.then_inc(s_nsc, 1)
                pe.wait_ge(s_a, g + 1)
                for k in range(AT):
                    pe.wait_ge(s_aT, g * AT + k - 1) if k >= 2 else pe.wait_ge(s_own, g)
                    if k < AT - 1:
                        for q in range(4):
                            c = (4 * k + q) * P
                            mm = pe.transpose(p_a[k % 2][:, q * P:(q + 1) * P], a[:, c:c + P], ident[:, :])
                    else:
                        mm = pe.transpose(p_a[k % 2][0:NS, 0:P], a[:, PAST:NK], ident[:, :])
                    mm.then_inc(s_at, 1)
                for m in range(NPG * GB):
                    j, bb = m // GB, m % GB
                    if m % (4 * GB) == 0:
                        pe.wait_ge(s_aT, g * AT + j // 4 + 1)
                    pe.wait_ge(s_vp[m % RING], g * (NPG * GB // RING * 16) + m // RING * 16 + 16)
                    pe.matmul(p_o[NS * bb:NS * bb + NS, :], aT[:, j, NS * bb:NS * bb + NS], vp[:, m % RING, :],
                              start=(j == 0), stop=False, skip_group_check=True).then_inc(s_av, 1)
                pe.wait_ge(s_aT, g * AT + AT)
                settle(pe, s_pe)
                for bb in range(GB):
                    pe.matmul(p_o[NS * bb:NS * bb + NS, :], aT[0:NS, NPG, NS * bb:NS * bb + NS], v_new[:, :],
                              start=False, stop=True, skip_group_check=True).then_inc(s_av, 1)
            pe.wait_ge(s_own, GROUPS)
            for g in range(GROUPS):
                mm = pe.matmul(p_m[0:NS, :], to_token[:, g * NS:(g + 1) * NS], own[:, g, :], start=(g == 0),
                               stop=(g == GROUPS - 1))
            mm.then_inc(s_tok, 1)

        @block.scalar
        def _(act):
            act.wait_ge(s_bias, 1)
            act.activation(bias[:, 0:1], p_m[:, 0:1], ACT.Copy).then_inc(s_b2, 1)
            act.activation(bias[:, 1:2], p_m[:, 0:1], ACT.Copy, scale=-1.0).then_inc(s_b2, 1)
            act.wait_ge(s_b2, 2)

            def both(cols, src, free):
                act.wait_ge(s_scan, free)
                act.activation(keep[:, cols], src, ACT.Sigmoid, scale=-(HD ** -0.5), bias=bias[:, 1:2]).then_inc(s_keep, 1)
                act.wait_ge(s_a, free)
                act.activation(take[:, cols], src, ACT.Sigmoid, scale=HD ** -0.5, bias=bias[:, 0:1]).then_inc(s_take, 1)

            with act.Fori(0, GROUPS) as g:
                with act.Fori(0, JB) as jb:
                    for m in range(0, PB * GB, 2):
                        act.wait_ge(s_tr, g * (NPG * GB) + jb * (PB * GB) + (RING + m + 1))
                        if m >= 2:
                            act.wait_ge(s_sc, g * (NPG * GB) + jb * (PB * GB) + (m - 1))
                        act.activation(kpT[:, 0, :, :], p_t[0][:, :].rearrange("p (q i) -> p q i", q=4),
                                       ACT.Copy).then_inc(s_kT[0], 1)
                    act.wait_ge(s_sc, g * (NPG * GB) + jb * (PB * GB) + PB * GB)
                    both(bass.ds(jb * (PB * P), PB * P), p_z[:, :], g)
                act.wait_ge(s_zn, g + 1)
                both(slice(PAST, NK), z_new[:, :], g)
                for k in range(AT):
                    act.wait_ge(s_at, g * AT + (k + 1))
                    act.wait_ge(s_av, g * (NPG * GB + GB))
                    if k < AT - 1:
                        act.activation(aT[:, 4 * k:4 * k + 4, :], p_a[k % 2][:, :].rearrange("p (q i) -> p q i", q=4),
                                       ACT.Copy).then_inc(s_aT, 1)
                    else:
                        act.activation(aT[0:NS, NPG, :], p_a[k % 2][0:NS, 0:P], ACT.Copy).then_inc(s_aT, 1)

        @block.vector
        def _(dve):
            dve.wait_ge(s_in, 16 * len(loads))
            dve.wait_ge(s_set, 2)
            dve.wait_ge(s_tr, RING)
            with dve.Fori(0, GROUPS) as g:
                dve.wait_ge(s_nsc, g)
                for q in range(4):
                    for hh in range(2):
                        h = 2 * q + hh
                        rows = slice(64 * hh, 64 * hh + 64)
                        dve.tensor_copy(qz[rows, :, q, h * DS:(h + 1) * DS],
                                        qT[rows, q, bass.ds(g * (GB * DS), GB * DS)].rearrange(
                                            "p (b t) -> p b t", t=DS)).then_inc(s_qz, 1)
                with dve.Fori(0, JB) as jb:
                    for m in range(1, PB * GB, 2):
                        dve.wait_ge(s_tr, g * (NPG * GB) + jb * (PB * GB) + (RING + m + 1))
                        if m >= 3:
                            dve.wait_ge(s_sc, g * (NPG * GB) + jb * (PB * GB) + (m - 1))
                        dve.tensor_copy(kpT[:, 1, :, :], p_t[1][:, :].rearrange("p (q i) -> p q i", q=4)).then_inc(s_kT[1], 1)
                dve.wait_ge(s_nsc, g + 1)
                dve.wait_ge(s_take, g * (JB + 1))
                dve.tensor_tensor(z_new[:, :], p_n[:, 0:NS], mask_new[:, bass.ds(g * NS, NS)], ALU.add).then_inc(s_zn, 1)
                dve.wait_ge(s_keep, g * (JB + 1) + JB + 1)
                dve.wait_ge(s_a, g)
                dve.tensor_tensor_scan(left[:, 0:NK][:, ::-1], keep[:, ::-1], keep[:, ::-1], 1.0,
                                       ALU.mult, ALU.bypass).then_inc(s_scan, 1)
                dve.wait_ge(s_scan, g + 1)
                dve.wait_ge(s_take, g * (JB + 1) + JB + 1)
                dve.wait_ge(s_at, g * AT)
                dve.tensor_tensor(a[:, :], take[:, :], left[:, 1:NK + 1], ALU.mult).then_inc(s_a, 1)
                dve.wait_ge(s_av, g * (NPG * GB + GB) + NPG * GB + GB)
                dve.tensor_tensor(own[:, bass.ds(g, 1), :].rearrange("p o n -> p (o n)"), p_o[:, :], own_head[:, :],
                                  ALU.mult).then_inc(s_own, 1)
            dve.wait_ge(s_tok, 1)
            dve.tensor_copy(o_all[0:NS, NT, :], p_m[0:NS, :]).then_inc(s_out, 1)

        @block.gpsimd
        def _(pool):
            pool.memset(qz[:, :, :, :], 0.0).then_inc(s_tr, RING)
            pool.memset(left[:, NK:NK + 1], 1.0).then_inc(s_set, 1)
            pool.memset(o_all[:, NT, :], 0.0).then_inc(s_set, 1)


def stage_c(nc, io, cat, o_all, ba):
    with Stage(nc, "C") as st:
        sb, ps, sem = st.sb, st.ps, st.sem
        w_raw = sb("w_raw", [P, 2, DM])
        w_hi, w_lo = (sb(n, [P, KC, DM], F32R) for n in ("w_hi", "w_lo"))
        wb_raw = sb("wb_raw", [P, KC, 2 * H1])
        wb_hi, wb_lo = (sb(n, [P, KC, 2 * H1], F32R) for n in ("wb_hi", "wb_lo"))
        g_odd = sb("g_odd", [P, KC])
        ident = sb("ident", [P, P])
        half = sb("half", [P, 1])
        mix = sb("mix", [P, 2, DM])
        x = sb("x", [P, 2, DM])
        mT_hi, mT_lo = (sb(n, [P, KC, P], F32R) for n in ("mT_hi", "mT_lo"))
        h1 = sb("h1", [P, DM])
        xn = sb("xn", [P, DM])
        ss, ms, rstd = (sb(n, [P, 1]) for n in ("ss", "ms", "rstd"))
        xT_hi, xT_lo = (sb(n, [P, KC, P], F32R) for n in ("xT_hi", "xT_lo"))
        p_m = [ps(f"m{i}") for i in range(2)]
        p_y = [ps(f"y{i}") for i in range(2)]
        p_h = [ps(f"h{i}") for i in range(2)]
        p_b = ps("b")
        s_in, s_half, s_zero = sem("loaded"), sem("half_set"), sem("pad_zeroed")
        s_w = [sem(f"w_in{i}") for i in range(2)]
        s_mix_in = [sem(f"mix_in{i}") for i in range(2)]
        s_x = [sem(f"x_in{i}") for i in range(2)]
        s_whi, s_wlo, s_wg, s_wb = (sem(n) for n in ("w_hi_ready", "w_lo_ready", "wb_scaled", "wb_ready"))
        s_mix, s_mt, s_mhi, s_mlo, s_y = (sem(n) for n in ("mix_ready", "mix_turned", "mT_hi", "mT_lo", "projected"))
        s_h, s_ho, s_ss, s_ms, s_rs = (sem(n) for n in ("h1_ready", "h1_stored", "squares", "mean_square", "rstd"))
        s_xn, s_ht, s_xhi, s_xlo, s_xo = (sem(n) for n in ("normed", "h1_turned", "xT_hi", "xT_lo", "xT_stored"))
        s_b, s_bo = sem("b_projected"), sem("b_ready")
        s_sp, s_pool = sem("sync_waits_settled"), sem("pool_waits_settled")
        block = st.block()
        loads = [(ident[:, :], io["consts"][:, cat["ident"][0]:cat["ident"][1]]),
                 (g_odd[:, :], io["norm_odd"].rearrange("o (k p) -> p (o k)", p=P)),
                 (wb_raw[:, :, :], io["w_in_odd"].rearrange("o (k p) n -> p (o k) n", p=P)[:, :, ODD_IN - 2 * H1:ODD_IN])]

        @block.sync
        def _(sp):
            def load(t, slot):
                last = isinstance(t, int) and t == NT
                sp.dma_start(mix[:, slot, :], io["mixgate"][bass.ds(t, 1), :, :].rearrange("o p n -> p (o n)")).then_inc(
                    s_mix_in[slot], 16)
                if last:
                    sp.wait_ge(s_zero, 1)
                    sp.dma_start(x[0:NS, slot, :], io["x_sample"].rearrange("b t d -> (b t) d")).then_inc(s_x[slot], 16)
                else:
                    sp.dma_start(x[:, slot, :], io["x_prompt"][0, bass.ds(t * P, P), :]).then_inc(s_x[slot], 16)

            load_all(sp, s_in, loads)
            load(0, 0)
            for k in range(KC):
                if k >= 2:
                    sp.wait_ge(s_wlo, k - 1)
                sp.dma_start(w_raw[:, k % 2, :], io["w_out_even"][0, k * P:(k + 1) * P, :]).then_inc(s_w[k % 2], 16)

            def body(t, slot, nth):
                first = isinstance(t, int) and t == 0
                if not (isinstance(t, int) and t == NT):
                    if not first:
                        sp.wait_ge(s_mt, t)
                        settle(sp, s_sp)
                        sp.wait_ge(s_h, t * 2)
                    load(t + 1, 1 - slot)
                sp.wait_ge(s_h, t * 2 + 2)
                settle(sp, s_sp)
                sp.dma_start(io["h1"][bass.ds(t, 1), :, :].rearrange("o p n -> p (o n)"), h1[:, :]).then_inc(s_ho, 16)
                sp.wait_ge(s_xlo, t * 2 + 2)
                settle(sp, s_sp)
                for part, src in (("xT_hi", xT_hi), ("xT_lo", xT_lo)):
                    sp.dma_start(io[part][:, :, bass.ds(t * P, P)], src[:, :, :].bitcast(F32)).then_inc(s_xo, 16)

            tiles_in_order(sp, body)
            sp.wait_ge(s_ho, 16 * (NT + 1))
            sp.wait_ge(s_xo, 32 * (NT + 1))

        @block.tensor
        def _(pe):
            def split(out, l_hi, l_lo, r_hi, r_lo, first, last):
                pe.matmul(out, l_hi, r_hi, start=first, stop=False)
                pe.matmul(out, l_hi, r_lo, start=False, stop=False)
                return pe.matmul(out, l_lo, r_hi, start=False, stop=last)

            def post(t):
                pe.wait_ge(s_xn, t + 1)
                at_least(pe, s_xlo, t * 2)
                for k in range(KC):
                    mm = pe.transpose(p_h[k // 4][:, k % 4 * P:(k % 4 + 1) * P], xn[:, k * P:(k + 1) * P], ident[:, :])
                mm.then_inc(s_ht, 1)

            def post_b(t):
                pe.wait_ge(s_xlo, t * 2 + 2)
                pe.wait_ge(s_wb, 2)
                at_least(pe, s_bo, t)
                for k in range(KC):
                    mm = split(p_b[:, 0:2 * H1], xT_hi[:, k, :], xT_lo[:, k, :], wb_hi[:, k, :], wb_lo[:, k, :],
                               k == 0, k == KC - 1)
                mm.then_inc(s_b, 1)

            def body(t, slot, nth):
                first = isinstance(t, int) and t == 0
                if first:
                    pe.wait_ge(s_in, 16 * len(loads))
                pe.wait_ge(s_mix, t + 1)
                at_least(pe, s_mlo, t * 2)
                for k in range(KC):
                    mm = pe.transpose(p_m[k // 4][:, k % 4 * P:(k % 4 + 1) * P], mix[:, slot, k * P:(k + 1) * P],
                                      ident[:, :])
                mm.then_inc(s_mt, 1)
                if not first:
                    post(t - 1)
                pe.wait_ge(s_mlo, t * 2 + 2)
                at_least(pe, s_h, t * 2)
                if first:
                    pe.wait_ge(s_wlo, KC)
                for n in range(2):
                    for k in range(KC):
                        mm = split(p_y[n][:, :], mT_hi[:, k, :], mT_lo[:, k, :], w_hi[:, k, n * 512:(n + 1) * 512],
                                   w_lo[:, k, n * 512:(n + 1) * 512], k == 0, k == KC - 1)
                    mm.then_inc(s_y, 1)
                if not first:
                    post_b(t - 1)

            tiles_in_order(pe, body)
            post(NT)
            post_b(NT)

        @block.scalar
        def _(act):
            for k in range(KC):
                act.wait_ge(s_w[k % 2], k // 2 * 16 + 16)
                act.activation(w_hi[:, k, :], w_raw[:, k % 2, :], ACT.Copy).then_inc(s_whi, 1)

            def post(t):
                act.wait_ge(s_ht, t + 1)
                at_least(act, s_xo, t * 32)
                at_least(act, s_b, t)
                for n in range(2):
                    act.activation(xT_hi[:, 4 * n:4 * n + 4, :], p_h[n][:, :].rearrange("p (k i) -> p k i", k=4),
                                   ACT.Copy).then_inc(s_xhi, 1)

            def body(t, slot, nth):
                first = isinstance(t, int) and t == 0
                act.wait_ge(s_mt, t + 1)
                at_least(act, s_y, t * 2)
                for n in range(2):
                    act.activation(mT_hi[:, 4 * n:4 * n + 4, :], p_m[n][:, :].rearrange("p (k i) -> p k i", k=4),
                                   ACT.Copy).then_inc(s_mhi, 1)
                if not first:
                    post(t - 1)
                act.wait_ge(s_h, t * 2 + 2)
                at_least(act, s_ms, t)
                at_least(act, s_ht, t)
                act.activation(xn[:, :], h1[:, :], ACT.Square, accum_out=ss[:, :]).then_inc(s_ss, 1)
                act.wait_ge(s_ss, t + 1)
                act.wait_ge(s_rs, t + 1)
                act.activation(xn[:, :], h1[:, :], ACT.Copy, scale=rstd[:, :]).then_inc(s_xn, 1)

            tiles_in_order(act, body)
            post(NT)

        @block.vector
        def _(dve):
            dve.wait_ge(s_in, 16 * len(loads))
            dve.tensor_tensor(wb_raw[:, :, :], wb_raw[:, :, :], g_odd[:, :].unsqueeze(2).to_broadcast([P, KC, 2 * H1]),
                              ALU.mult).then_inc(s_wg, 1)
            dve.wait_ge(s_wg, 1)
            dve.tensor_copy(wb_hi[:, :, :], wb_raw[:, :, :]).then_inc(s_wb, 1)
            dve.wait_ge(s_wb, 1)
            dve.tensor_tensor(wb_lo[:, :, :], wb_raw[:, :, :], wb_hi[:, :, :].bitcast(F32), ALU.subtract).then_inc(s_wb, 1)
            for k in range(KC):
                dve.wait_ge(s_whi, k + 1)
                dve.wait_ge(s_w[k % 2], k // 2 * 16 + 16)
                dve.tensor_tensor(w_lo[:, k, :], w_raw[:, k % 2, :], w_hi[:, k, :].bitcast(F32), ALU.subtract).then_inc(s_wlo, 1)

            def post(t):
                dve.wait_ge(s_xhi, t * 2 + 2)
                at_least(dve, s_xo, t * 32)
                at_least(dve, s_b, t)
                for n in range(2):
                    dve.tensor_tensor(xT_lo[:, 4 * n:4 * n + 4, :], p_h[n][:, :].rearrange("p (k i) -> p k i", k=4),
                                      xT_hi[:, 4 * n:4 * n + 4, :].bitcast(F32), ALU.subtract).then_inc(s_xlo, 1)

            def post_b(t):
                dve.wait_ge(s_b, t + 1)
                dve.tensor_copy(ba[:, bass.ds(t, 1), :].rearrange("p o n -> p (o n)"), p_b[:, 0:2 * H1]).then_inc(s_bo, 1)

            def body(t, slot, nth):
                first = isinstance(t, int) and t == 0
                dve.wait_ge(s_mix_in[slot], nth * 16 + 16)
                dve.tensor_tensor(mix[:, slot, W0:DM], mix[:, slot, W0:DM],
                                  o_all[:, bass.ds(t, 1), :].rearrange("p o n -> p (o n)"), ALU.mult).then_inc(s_mix, 1)
                dve.wait_ge(s_mhi, t * 2 + 2)
                at_least(dve, s_y, t * 2)
                for n in range(2):
                    dve.tensor_tensor(mT_lo[:, 4 * n:4 * n + 4, :], p_m[n][:, :].rearrange("p (k i) -> p k i", k=4),
                                      mT_hi[:, 4 * n:4 * n + 4, :].bitcast(F32), ALU.subtract).then_inc(s_mlo, 1)
                if not first:
                    post(t - 1)
                dve.wait_ge(s_x[slot], nth * 16 + 16)
                at_least(dve, s_ho, t * 16)
                at_least(dve, s_xn, t)
                for n in range(2):
                    dve.wait_ge(s_y, t * 2 + (n + 1))
                    dve.tensor_tensor(h1[:, n * 512:(n + 1) * 512], p_y[n][:, :], x[:, slot, n * 512:(n + 1) * 512],
                                      ALU.add).then_inc(s_h, 1)
                if not first:
                    post_b(t - 1)

            tiles_in_order(dve, body)
            post(NT)
            post_b(NT)

        @block.gpsimd
        def _(pool):
            pool.memset(half[:, :], -0.5).then_inc(s_half, 1)
            pool.wait_ge(s_half, 1)

            def body(t, slot, nth):
                if isinstance(t, int) and t == NT - 1:
                    pool.wait_ge(s_h, 2 * (NT - 1))
                    pool.memset(x[:, 0, :], 0.0).then_inc(s_zero, 1)
                pool.wait_ge(s_ss, t + 1)
                at_least(pool, s_xn, t)
                settle(pool, s_pool)
                pool.tensor_scalar(ms[:, :], ss[:, :], 1.0 / DM, EPS, ALU.mult, ALU.add).then_inc(s_ms, 1)
                pool.wait_ge(s_ms, t + 1)
                pool.tensor_tensor(rstd[:, :], ms[:, :], half[:, :], ALU.pow).then_inc(s_rs, 1)

            tiles_in_order(pool, body)


def stage_g(nc, io, cat, ba, gd):
    with Stage(nc, "G") as st:
        sb, ps, sem = st.sb, st.ps, st.sem
        T = NT + 1
        consts = {n: sb(n, [P, P]) for n in ("tri", "tri_samp", "last_samp")}
        ones = sb("ones", [P, P])
        own = sb("own", [P, DB])
        rate, dt = sb("rate", [P, H1]), sb("dt", [P, H1])
        y, e, sp_, g = (sb(n, [P, T, H1]) for n in ("y", "e", "sp", "g"))
        gb = sb("gb", [P, DB, H1])
        gap = sb("gap", [P, T, H1])
        p_c, p_t = ps("c"), ps("t")
        s_in, s_one = sem("loaded"), sem("ones_set")
        s_v, s_a, s_p = sem("vector_step"), sem("scalar_step"), sem("sums")
        block = st.block()
        loads = [(consts[n][:, :], io["consts"][:, cat[n][0]:cat[n][1]]) for n in consts]
        loads += [(own[:, :], io["consts"][:, cat["own_batch"][0]:cat["own_batch"][1]]),
                  (rate[:, :], io["a_log"].to_broadcast([P, H1])), (dt[:, :], io["dt_bias"].to_broadcast([P, H1]))]
        n_in = 16 * len(loads)
        over = lambda v: v[:, :].unsqueeze(1).to_broadcast([P, T, H1])

        @block.sync
        def _(sp):
            load_all(sp, s_in, loads)

        @block.gpsimd
        def _(pool):
            pool.memset(ones[:, :], 1.0).then_inc(s_one, 1)

        @block.vector
        def _(dve):
            dve.wait_ge(s_in, n_in)
            dve.tensor_tensor(y[:, :, :], ba[:, :, H1:2 * H1], over(dt), ALU.add).then_inc(s_v, 1)
            dve.wait_ge(s_v, 1)
            dve.tensor_scalar(sp_[:, :, :], y[:, :, :], 0.0, None, ALU.max).then_inc(s_v, 1)
            dve.wait_ge(s_a, 5)
            dve.wait_ge(s_v, 2)
            dve.tensor_tensor(sp_[:, :, :], sp_[:, :, :], e[:, :, :], ALU.add).then_inc(s_v, 1)
            dve.tensor_scalar(rate[:, :], rate[:, :], -1.0, None, ALU.mult).then_inc(s_v, 1)
            dve.wait_ge(s_v, 4)
            dve.tensor_tensor(g[:, :, :], sp_[:, :, :], over(rate), ALU.mult).then_inc(s_v, 1)
            dve.wait_ge(s_v, 5)
            dve.tensor_tensor(gb[:, :, :], g[:, NT, :].unsqueeze(1).to_broadcast([P, DB, H1]),
                              own[:, :].unsqueeze(2).to_broadcast([P, DB, H1]), ALU.mult).then_inc(s_v, 1)
            dve.wait_ge(s_p, 1)
            dve.tensor_copy(gd[:, 1, :, :], p_c[:, 0:T * H1].rearrange("p (t h) -> p t h", h=H1)).then_inc(s_v, 1)
            dve.wait_ge(s_v, 7)
            dve.wait_ge(s_p, 2)
            dve.tensor_tensor(gap[:, :, :], p_t[:, 0:T * H1].rearrange("p (t h) -> p t h", h=H1), gd[:, 1, :, :],
                              ALU.subtract).then_inc(s_v, 1)

        @block.scalar
        def _(act):
            act.activation(gd[:, 0, :, :], ba[:, :, 0:H1], ACT.Sigmoid).then_inc(s_a, 1)
            act.wait_ge(s_v, 1)
            act.activation(e[:, :, :], y[:, :, :], ACT.Abs).then_inc(s_a, 1)
            act.wait_ge(s_a, 2)
            act.activation(e[:, :, :], e[:, :, :], ACT.Exp, scale=-1.0).then_inc(s_a, 1)
            act.wait_ge(s_a, 3)
            act.wait_ge(s_one, 1)
            act.activation(e[:, :, :], e[:, :, :], ACT.Ln, bias=ones[:, 0:1]).then_inc(s_a, 1)
            act.wait_ge(s_in, n_in)
            act.activation(rate[:, :], rate[:, :], ACT.Exp).then_inc(s_a, 1)
            act.wait_ge(s_v, 8)
            act.activation(gd[:, 2, :, :], gd[:, 1, :, :], ACT.Exp).then_inc(s_a, 1)
            act.activation(gd[:, 3, :, :], gap[:, :, :], ACT.Exp).then_inc(s_a, 1)
            act.activation(gd[:, 4, :, :], p_t[:, 0:T * H1].rearrange("p (t h) -> p t h", h=H1), ACT.Exp).then_inc(s_a, 1)
            act.wait_ge(s_p, 3)
            act.activation(gd[:, 5, 0:DB, :], p_c[:, T * H1:(T + DB) * H1].rearrange("p (t h) -> p t h", h=H1),
                           ACT.Exp).then_inc(s_a, 1)

        @block.tensor
        def _(pe):
            pe.wait_ge(s_v, 5)
            pe.wait_ge(s_one, 1)
            flat = g[:, :, :].rearrange("p t h -> p (t h)")
            n = NT * H1
            pe.matmul(p_c[:, 0:n], consts["tri"][:, :], flat[:, 0:n], start=True, stop=True)
            pe.matmul(p_c[:, n:n + H1], consts["tri_samp"][:, :], flat[:, n:n + H1], start=True, stop=True).then_inc(s_p, 1)
            pe.matmul(p_t[:, 0:n], ones[:, :], flat[:, 0:n], start=True, stop=True)
            pe.matmul(p_t[:, n:n + H1], consts["last_samp"][:, :], flat[:, n:n + H1], start=True, stop=True).then_inc(s_p, 1)
            pe.wait_ge(s_v, 7)
            pe.matmul(p_c[:, n + H1:n + H1 + DB * H1], ones[:, :], gb[:, :, :].rearrange("p b h -> p (b h)"),
                      start=True, stop=True).then_inc(s_p, 1)


def stage_d(nc, io, cat):
    with Stage(nc, "D") as st:
        sb, ps, sem = st.sb, st.ps, st.sem
        NB = 4
        BT = SEQ // NB
        NCV = CONV // P
        NST = NCV + H1
        TOK = SEQ + NS
        HB = DB * (CW - 1)
        xT_hi, xT_lo = (sb(n, [P, KC, TOK], F32R) for n in ("xT_hi", "xT_lo"))
        w_raw = sb("w_raw", [P, 2, KC, P])
        w_hi, w_lo = (sb(n, [P, 2, KC, P], F32R) for n in ("w_hi", "w_lo"))
        g_odd = sb("g_odd", [P, KC])
        ident = sb("ident", [P, P])
        ext = sb("ext", [P, 2, CW - 1 + SEQ])
        ext_s = sb("ext_s", [P, 2, DB, CW - 1 + DS])
        last_s = sb("last_s", [P, 2, HB])
        out = sb("out", [P, 2, TOK])
        taps = sb("taps", [P, NCV, CW])
        hist = sb("hist", [P, NCV, HB])
        tap = sb("tap", [P, 2, CW])
        rows_p = sb("rows_p", [CW - 1, P])
        rows_s = sb("rows_s", [HB, P])
        p_y = [ps(f"y{i}") for i in range(NB)]
        p_s = [ps("s0")]
        p_r = ps("r")
        s_in, s_set, s_pre, s_prc = sem("loaded"), sem("set"), sem("small_turned"), sem("small_out")
        s_xt = [sem(f"xT_in{i}") for i in range(NB)]
        s_w = [sem(f"w_in{i}") for i in range(2)]
        s_wg, s_whi, s_wlo = sem("w_scaled"), sem("w_hi"), sem("w_lo")
        s_y = [sem(f"projected{i}") for i in range(NB + 1)]
        s_ev = [sem(f"block_out{i}") for i in range(NB + 1)]
        s_tap, s_cv, s_sl, s_r, s_ro = (sem(n) for n in ("tap_ready", "conv_step", "silu_done", "rows_turned", "rows_ready"))
        s_o = [sem(f"stored{i}") for i in range(2)]
        s_rs, s_last = sem("rows_stored"), sem("last_rows")
        block = st.block()
        STEPS = 2 * CW

        @block.sync
        def _(sp):
            sp.dma_start(g_odd[:, :], io["norm_odd"].rearrange("o (k p) -> p (o k)", p=P),
                         allow_slow_non_contiguous=True).then_inc(s_in, 16)
            sp.dma_start(ident[:, :], io["consts"][:, cat["ident"][0]:cat["ident"][1]]).then_inc(s_in, 16)
            sp.dma_start(out[0:CW, 0, 0:SEQ], io["conv_w"][0, :, 0:SEQ]).then_inc(s_in, 16)
            sp.dma_start(out[0:CW, 1, 0:CONV - SEQ], io["conv_w"][0, :, SEQ:CONV]).then_inc(s_in, 16)
            sp.dma_start(ext[0:HB, 0, 0:SEQ], io["state_conv"].rearrange("o b r c -> (o b r) c")[:, 0:SEQ]).then_inc(s_in, 16)
            sp.dma_start(ext[0:HB, 1, 0:CONV - SEQ], io["state_conv"].rearrange("o b r c -> (o b r) c")[:, SEQ:CONV]).then_inc(
                s_in, 16)

            def load_w(c, slot):
                sp.dma_start(w_raw[:, slot, :, :], io["w_in_odd"].rearrange("o (k p) n -> p (o k) n", p=P)[
                    :, :, bass.ds(c * P, P)]).then_inc(s_w[slot], 16)

            load_w(0, 0)
            load_w(1, 1)
            for n in range(NB):
                cols = slice(n * BT, (n + 1) * BT if n < NB - 1 else TOK)
                for part, dst in (("xT_hi", xT_hi), ("xT_lo", xT_lo)):
                    sp.dma_start(dst[:, :, cols].bitcast(F32), io[part][:, :, cols]).then_inc(s_xt[n], 16)

            def rows(c):
                sp.wait_ge(s_ro, c * 2 + 2)
                sp.dma_start(io["conv_prompt"][0, 0, :, bass.ds(c * P, P)], rows_p[:, :]).then_inc(s_rs, 16)
                sp.dma_start(io["conv_sample"].rearrange("o b r c -> (o b r) c")[:, bass.ds(c * P, P)],
                             rows_s[:, :]).then_inc(s_rs, 16)

            def body(c, slot, nth, more=True):
                if more:
                    sp.wait_ge(s_wlo, c + 1)
                    load_w(c + 2, slot)
                if isinstance(c, int) and (c == 0 or c > NCV):
                    pass
                else:
                    rows(c - 1)
                sp.wait_ge(s_sl, c + 1)
                sp.dma_start(io["strips"][bass.ds(c, 1), :, :].rearrange("o p n -> p (o n)"),
                             out[:, slot, :]).then_inc(s_o[slot], 16)

            body(0, 0, 0)
            body(1, 1, 0)
            with sp.Fori(1, NCV // 2) as i:
                body(i * 2, 0, i)
                body(i * 2 + 1, 1, i)
            for c in range(NCV, NST):
                body(c, c % 2, c // 2, more=c + 2 < NST)
            for s in s_o:
                sp.wait_ge(s, 16 * NST // 2)
            sp.wait_ge(s_rs, 32 * NCV)

        @block.tensor
        def _(pe):
            pe.wait_ge(s_in, 16 * 6)
            for c in range(NCV):
                half, at = divmod(c * P, SEQ)
                mm = pe.transpose(p_r[:, c * CW:(c + 1) * CW], out[0:CW, half, at:at + P], ident[0:CW, 0:CW])
            mm.then_inc(s_pre, 1)
            for c in range(NCV):
                half, at = divmod(c * P, SEQ)
                mm = pe.transpose(p_y[c // 12][:, c % 12 * HB:(c % 12 + 1) * HB], ext[0:HB, half, at:at + P],
                                  ident[0:HB, 0:HB])
            mm.then_inc(s_pre, 1)
            pe.wait_ge(s_prc, 3)

            def body(c, slot, nth, first=False):
                pe.wait_ge(s_wlo, c + 1)
                for n in range(NB + 1):
                    if first and n < NB:
                        pe.wait_ge(s_xt[n], 32)
                    at_least(pe, s_ev[n], c)
                    dst = p_y[n][:, :] if n < NB else p_s[0][:, 0:NS]
                    cols = slice(n * BT, (n + 1) * BT) if n < NB else slice(SEQ, TOK)
                    for k in range(KC):
                        pe.matmul(dst, w_hi[:, slot, k, :], xT_hi[:, k, cols], start=(k == 0), stop=False)
                        pe.matmul(dst, w_hi[:, slot, k, :], xT_lo[:, k, cols], start=False, stop=False)
                        mm = pe.matmul(dst, w_lo[:, slot, k, :], xT_hi[:, k, cols], start=False, stop=(k == KC - 1))
                    mm.then_inc(s_y[n], 1)
                if isinstance(c, int) and (c == 0 or c > NCV):
                    return
                pe.wait_ge(s_last, c)
                pe.wait_ge(s_ev[NB - 1], c)
                at_least(pe, s_ro, (c - 1) * 2)
                pe.transpose(p_r[0:CW - 1, 0:P], ext[:, 1 - slot, SEQ:SEQ + CW - 1], ident[:, :])
                pe.transpose(p_r[0:HB, P:2 * P], last_s[:, 1 - slot, :], ident[:, :]).then_inc(s_r, 1)

            for c in range(2):
                body(c, c, 0, first=(c == 0))
            with pe.Fori(1, NCV // 2) as i:
                body(i * 2, 0, i)
                body(i * 2 + 1, 1, i)
            for c in range(NCV, NST):
                body(c, c % 2, c // 2)

        @block.scalar
        def _(act):
            def body(c, slot, nth, conv=True, first=False):
                if conv and not first:
                    act.wait_ge(s_cv, c * STEPS - STEPS)
                    act.wait_ge(s_r, c - 1)
                for n in range(NB + 1):
                    act.wait_ge(s_y[n], c + 1)
                    if not conv:
                        act.wait_ge(s_o[slot], nth * 16)
                        dst = out[:, slot, n * BT:(n + 1) * BT] if n < NB else out[:, slot, SEQ:TOK]
                        src = p_y[n][:, :] if n < NB else p_s[0][:, 0:NS]
                        mm = act.activation(dst, src, ACT.Silu)
                    elif n < NB:
                        mm = act.activation(ext[:, slot, CW - 1 + n * BT:CW - 1 + (n + 1) * BT], p_y[n][:, :], ACT.Copy)
                    else:
                        mm = act.activation(ext_s[:, slot, :, CW - 1:CW - 1 + DS],
                                            p_s[0][:, 0:NS].rearrange("p (b t) -> p b t", t=DS), ACT.Copy)
                    mm.then_inc(s_ev[n], 1)
                if conv:
                    act.wait_ge(s_cv, c * STEPS + STEPS)
                    act.activation(out[:, slot, :], out[:, slot, :], ACT.Silu).then_inc(s_sl, 1)
                else:
                    for n in range(NB + 1):
                        act.wait_ge(s_ev[n], c + 1)
                    act.sem_inc(s_sl, 1)

            act.wait_ge(s_prc, 3)
            act.wait_ge(s_set, 1)
            body(0, 0, 0, first=True)
            body(1, 1, 0, first=True)
            with act.Fori(1, NCV // 2) as i:
                body(i * 2, 0, i)
                body(i * 2 + 1, 1, i)
            for c in range(NCV, NST):
                body(c, c % 2, c // 2, conv=False)

        @block.vector
        def _(dve):
            dve.wait_ge(s_pre, 1)
            dve.tensor_copy(taps[:, :, :], p_r[:, 0:NCV * CW].rearrange("p (c j) -> p c j", j=CW)).then_inc(s_prc, 1)
            dve.wait_ge(s_pre, 2)
            for n in range(2):
                dve.tensor_copy(hist[:, 12 * n:12 * n + 12, :], p_y[n][:, 0:12 * HB].rearrange(
                    "p (c j) -> p c j", j=HB)).then_inc(s_prc, 1)
            dve.wait_ge(s_prc, 3)
            dve.memset(ext[:, :, 0:CW - 1], 0.0).then_inc(s_set, 1)

            def split_w(c, slot, nth):
                dve.wait_ge(s_w[slot], nth * 16 + 16)
                dve.tensor_tensor(w_raw[:, slot, :, :], w_raw[:, slot, :, :],
                                  g_odd[:, :].unsqueeze(2).to_broadcast([P, KC, P]), ALU.mult).then_inc(s_wg, 1)
                dve.wait_ge(s_wg, c + 1)
                if not (isinstance(c, int) and c < 2):
                    dve.wait_ge(s_y[NB], c - 1)
                dve.tensor_copy(w_hi[:, slot, :, :], w_raw[:, slot, :, :]).then_inc(s_whi, 1)
                dve.wait_ge(s_whi, c + 1)
                dve.tensor_tensor(w_lo[:, slot, :, :], w_raw[:, slot, :, :], w_hi[:, slot, :, :].bitcast(F32),
                                  ALU.subtract).then_inc(s_wlo, 1)

            def rows(c):
                dve.wait_ge(s_r, c + 1)
                at_least(dve, s_rs, c * 32)
                dve.tensor_copy(rows_p[:, :], p_r[0:CW - 1, 0:P]).then_inc(s_ro, 1)
                dve.tensor_copy(rows_s[:, :], p_r[0:HB, P:2 * P]).then_inc(s_ro, 1)

            def body(c, slot, nth):
                if not (isinstance(c, int) and c < 2):
                    dve.wait_ge(s_sl, c - 1)
                    dve.wait_ge(s_r, c - 1)
                dve.tensor_copy(tap[:, slot, :], taps[:, bass.ds(c, 1), :].rearrange("p o j -> p (o j)")).then_inc(s_tap, 1)
                dve.tensor_copy(ext_s[:, slot, :, 0:CW - 1], hist[:, bass.ds(c, 1), :].rearrange(
                    "p o (b r) -> p (o b) r", r=CW - 1)).then_inc(s_tap, 1)
                split_w(c + 1, 1 - slot, nth + slot)
                dve.wait_ge(s_tap, c * 2 + 2)
                dve.wait_ge(s_o[slot], nth * 16)
                for n in range(NB + 1):
                    dve.wait_ge(s_ev[n], c + 1)
                dve.tensor_copy(last_s[:, slot, :].rearrange("p (b r) -> p b r", r=CW - 1),
                                ext_s[:, slot, :, DS:DS + CW - 1]).then_inc(s_last, 1)
                y, ys = out[:, slot, 0:SEQ], out[:, slot, SEQ:TOK].rearrange("p (b t) -> p b t", t=DS)
                for j in range(CW):
                    if j == 0:
                        dve.tensor_scalar(y, ext[:, slot, 0:SEQ], tap[:, slot, 0:1], None, ALU.mult).then_inc(s_cv, 1)
                        dve.tensor_scalar(ys, ext_s[:, slot, :, 0:DS], tap[:, slot, 0:1], None, ALU.mult).then_inc(s_cv, 1)
                    else:
                        dve.wait_ge(s_cv, c * STEPS + 2 * j)
                        dve.scalar_tensor_tensor(y, ext[:, slot, j:j + SEQ], tap[:, slot, j:j + 1], y, ALU.mult,
                                                 ALU.add).then_inc(s_cv, 1)
                        dve.scalar_tensor_tensor(ys, ext_s[:, slot, :, j:j + DS], tap[:, slot, j:j + 1], ys, ALU.mult,
                                                 ALU.add).then_inc(s_cv, 1)
                if not (isinstance(c, int) and c == 0):
                    rows(c - 1)

            split_w(0, 0, 0)
            body(0, 0, 0)
            body(1, 1, 0)
            with dve.Fori(1, NCV // 2) as i:
                body(i * 2, 0, i)
                body(i * 2 + 1, 1, i)
            split_w(NCV + 1, 1, NCV // 2)
            rows(NCV - 1)
            for c in range(NCV + 2, NST):
                split_w(c, c % 2, c // 2)


def stage_e(nc, io, cat, gd):
    with Stage(nc, "E") as st:
        sb, ps, sem = st.sb, st.ps, st.sem
        CH = 4
        NU = NT // CH
        LAST = NU * H1
        ident = sb("ident", [P, P])
        ident_b = sb("ident_b", [P, P], BF16)
        mask_f = sb("mask_f", [P, CH * P])
        mask = sb("mask", [P, CH * P], BF16)
        levels = sb("levels", [P, LEVELS, P])
        g_o = sb("g_o", [P, 1])
        half = sb("half", [P, 2 * CH])
        src = sb("src", [P, 2, 4, CH * P])
        sm = sb("sm", [P, 2, 5, CH])
        k_tok = sb("k_tok", [P, CH, P])
        sq = sb("sq", [P, 2, CH, P])
        ss, sse, rn = (sb(n, [P, 2 * CH]) for n in ("ss", "sse", "rn"))
        lnk, nb, brk, kwf, ktf = (sb(n, [P, CH]) for n in ("lnk", "nb", "brk", "kwf", "ktf"))
        rq = sb("rq", [P, 2, CH])
        erow = sb("erow", [P, CH, P])
        dec = sb("dec", [P, CH, P])
        kbT = sb("kbT", [P, CH, P])
        lt = sb("lt", [P, CH, P])
        nbs = sb("nbs", [P, LEVELS, CH, P])
        ut = sb("ut", [P, 2, 2, 2, 2, P])
        gm = sb("gm", [P, 2, 2, P])
        kw = sb("kw", [P, CH, P])
        uf, vb, nwT, qe, attT, kt = (sb(n, [P, 2, CH, P]) for n in ("uf", "vb", "nwT", "qe", "attT", "kt"))
        state = sb("state", [P, 2, P])
        vn = sb("vn", [P, 2, P])
        o_sb, on = (sb(n, [P, CH, P]) for n in ("o_sb", "on"))
        junk = sb("junk", [P, P])
        oss, ose, orn = (sb(n, [P, CH]) for n in ("oss", "ose", "orn"))
        oT = sb("oT", [P, CH, P])
        p1 = [ps(f"i{i}") for i in range(4)]
        p_v, p_o, p_s, p_t = ps("v"), ps("o"), ps("s"), ps("t")
        s_in, s_cst, s_half = sem("loaded"), sem("cast"), sem("half_set")
        s_src = [sem(f"src_in{i}") for i in range(2)]
        s_sm = sem("columns")
        s_ktr, s_vtr, s_qtr, s_g, s_gm, s_br, s_kq, s_kk, s_t0 = (sem(n) for n in (
            "k_turned", "v_turned", "q_turned", "gc_rows", "gc_masked", "b_rows", "kq", "kk", "u_turned"))
        s_ktok, s_sq, s_er, s_ln, s_dec = (sem(n) for n in ("k_tok", "squares", "exp_rows", "log_norm", "decay"))
        s_vb, s_ss, s_kb, s_qe, s_att, s_lt = (sem(n) for n in ("vb", "sums", "kbT", "qe", "att", "lt"))
        s_sse, s_rn, s_brk, s_kwf, s_nb, s_rq, s_kw, s_ktw = (sem(n) for n in (
            "sums_eps", "norm", "b_norm", "kw_factor", "neg_bias", "q_norm", "kw", "kt"))
        s_nbs, s_u0, s_t1 = sem("level_masked"), sem("u_first"), sem("t_first")
        s_x = [sem(f"lt_t{i}") for i in range(2)]
        s_gr = [sem(f"g_ready{i}") for i in range(2)]
        s_y = [sem(f"ut_product{i}") for i in range(2)]
        s_ut = [sem(f"ut_ready{i}") for i in range(2)]
        s_w, s_wn = sem("w_product"), sem("w_ready")
        s_v, s_vn, s_o, s_ds, s_st = (sem(n) for n in ("v_product", "v_new", "o_product", "state_product", "state_ready"))
        s_os, s_oss, s_ose, s_orn, s_on, s_ot, s_oT = (sem(n) for n in (
            "o_out", "o_squares", "o_mean", "o_norm", "o_normed", "o_turned", "oT_ready"))
        s_fin = sem("state_stored")
        s_oo = sem("oT_stored")
        s_pool = sem("pool_waits_settled")
        block = st.block()
        n_in = 16 * 4
        ORDER = ["turns", "v0", "decay", "rows", "s0", "scores", "v1", "first", "s1", 1, "v2", 2, "s2", 3, "v3", 4, "s3",
                 5, "out", 6, "w"]

        def run(eng, step1, step2):
            def unit(h, g, more=True):
                for name in ORDER:
                    if isinstance(name, str) and (name[0] in "vs" and name[1:].isdigit() or name == "out"):
                        step2(name, h * NU + g, g, h)
                    elif more:
                        nxt = (g + 1) % NU
                        step1(name, h * NU + g + 1, (g + 1) % 2, nxt, h if g < NU - 1 else h + 1, h * 2 + (g + 1) // 2)

            for name in ORDER:
                if not (isinstance(name, str) and (name[0] in "vs" and name[1:].isdigit() or name == "out")):
                    step1(name, 0, 0, 0, 0, 0)
            with eng.Fori(0, H1 - 1) as h:
                for g in range(NU):
                    unit(h, g)
            for g in range(NU):
                unit(H1 - 1, g, more=g < NU - 1)

        def halves(a):
            return a.rearrange("p (c i) -> p c i", c=CH)

        @block.sync
        def _(sp):
            def const(name):
                return io["consts"][:, cat[name][0]:cat[name][1]]

            lv = (cat["level0"][0], cat[f"level{LEVELS - 1}"][1])
            for dst, s in ((ident[:, :], const("ident")), (mask_f[:, :], const("mask_tri")),
                           (levels[:, :, :], io["consts"][:, lv[0]:lv[1]].rearrange("p (l i) -> p l i", i=P)),
                           (g_o[:, :], io["o_norm"].rearrange("o e -> e o"))):
                sp.dma_start(dst, s, allow_slow_non_contiguous=True).then_inc(s_in, 16)

            def load(w, slot, g, h):
                at_least(sp, s_oT, w - 1)
                for n in range(4):
                    sp.dma_start(src[:, slot, n, :], io["strips"][bass.ds(h + n * H1, 1), :, g * CH * P:(g + 1) * CH * P]
                                 .rearrange("o p n -> p (o n)")).then_inc(s_src[slot], 16)

            def unit(h, g, more=True):
                w = h * NU + g
                if more:
                    load(w + 1, (g + 1) % 2, (g + 1) % NU, h if g < NU - 1 else h + 1)
                if g == NU - 1:
                    sp.wait_ge(s_st, h * NT + NT)
                    sp.dma_start(io["delta_prompt"][0, 0, bass.ds(h, 1), :, :].rearrange("o p n -> p (o n)"),
                                 state[:, 0, :]).then_inc(s_fin, 16)
                sp.wait_ge(s_oT, w + 1)
                sp.dma_start(io["oT"][bass.ds(h, 1), :, g * CH * P:(g + 1) * CH * P].rearrange("o p n -> p (o n)"),
                             oT[:, :, :].rearrange("p c i -> p (c i)")).then_inc(s_oo, 16)

            load(0, 0, 0, 0)
            with sp.Fori(0, H1 - 1) as h:
                for g in range(NU):
                    unit(h, g)
            for g in range(NU):
                unit(H1 - 1, g, more=g < NU - 1)
            sp.wait_ge(s_fin, 16 * H1)
            sp.wait_ge(s_oo, 16 * LAST)

        @block.tensor
        def _(pe):
            pe.wait_ge(s_in, n_in)
            pe.wait_ge(s_cst, 2)

            def step1(name, w, slot, g, h, nth):
                q_, k_, v_ = (src[:, slot, n, :] for n in range(3))
                cs = [slice(c * P, (c + 1) * P) for c in range(CH)]
                if name == "turns":
                    pe.wait_ge(s_src[slot], nth * 64 + 64)
                    at_least(pe, s_wn, w * 2)
                    at_least(pe, s_ut[0], w * (LEVELS - 1))
                    at_least(pe, s_ut[1], w * (LEVELS - 1))
                    for bank, t, s in ((0, k_, s_ktr), (1, v_, s_vtr), (2, q_, s_qtr)):
                        for c in range(CH):
                            mm = pe.transpose(p1[bank][:, cs[c]], t[:, cs[c]], ident[:, :])
                        mm.then_inc(s, 1)
                    pe.wait_ge(s_sm, w + 1)
                    for c in range(CH):
                        mm = pe.matmul(p1[3][:, cs[c]], sm[:, slot, 1, c:c + 1].to_broadcast([P, P]), ident[:, :],
                                       start=(c == 0), stop=True, skip_group_check=True)
                    mm.then_inc(s_g, 1)
                elif name == "decay":
                    pe.wait_ge(s_er, w + 1)
                    pe.matmul(p1[3][:, :], ident_b[:, :], mask[:, :], start=False, stop=True,
                              skip_group_check=True).then_inc(s_gm, 1)
                elif name == "rows":
                    pe.wait_ge(s_brk, w + 1)
                    pe.wait_ge(s_sq, w * 2 + 2)
                    pe.wait_ge(s_ktok, w + 1)
                    for c in range(CH):
                        mm = pe.matmul(p1[0][:, cs[c]], brk[:, c:c + 1].to_broadcast([P, P]), ident[:, :],
                                       start=True, stop=True)
                    mm.then_inc(s_br, 1)
                elif name == "scores":
                    for c in range(CH):
                        mm = pe.matmul(p1[2][:, cs[c]], k_[:, cs[c]], q_[:, cs[c]], start=True, stop=True)
                    mm.then_inc(s_kq, 1)
                    pe.wait_ge(s_kb, w + 1)
                    pe.wait_ge(s_vb, w + 1)
                    for c in range(CH):
                        mm = pe.matmul(p1[1][:, cs[c]], k_[:, cs[c]], kbT[:, c, :], start=True, stop=True)
                    mm.then_inc(s_kk, 1)
                elif name == "first":
                    pe.wait_ge(s_u0, w + 1)
                    pe.wait_ge(s_att, w + 1)
                    for hf in range(2):
                        for c in range(2):
                            mm = pe.transpose(p1[2 * hf][:, cs[c]], ut[:, 0, hf, 0, c, :], ident[:, :])
                        mm.then_inc(s_t0, 1)
                elif name == "w":
                    pe.wait_ge(s_kw, w + 1)
                    for hf in range(2):
                        pe.wait_ge(s_ut[hf], w * (LEVELS - 1) + LEVELS - 1)
                        for c in range(2):
                            mm = pe.matmul(p1[2 * hf][:, cs[c]], kw[:, 2 * hf + c, :], uf[:, slot, 2 * hf + c, :],
                                           start=True, stop=True)
                        mm.then_inc(s_w, 1)
                else:
                    n = name
                    old = (n - 1) % 2
                    for hf in range(2):
                        if n == 1:
                            pe.wait_ge(s_t1, w * 2 + hf + 1)
                        else:
                            pe.wait_ge(s_ut[hf], w * (LEVELS - 1) + n - 1)
                        pe.wait_ge(s_nbs, w * LEVELS + n + 1)
                        for c in range(2):
                            mm = pe.matmul(p1[2 * hf][:, cs[c]], nbs[:, n, 2 * hf + c, :], ut[:, old, hf, 1, c, :],
                                           start=True, stop=True)
                        mm.then_inc(s_x[hf], 1)
                    for hf in range(2):
                        pe.wait_ge(s_gr[hf], w * (LEVELS - 1) + n)
                        for c in range(2):
                            mm = pe.matmul(p1[2 * hf + 1][:, cs[c]], gm[:, hf, c, :], ut[:, old, hf, 0, c, :],
                                           start=True, stop=True)
                        if n < LEVELS - 1:
                            for c in range(2):
                                mm = pe.matmul(p1[2 * hf + 1][:, cs[2 + c]], ut[:, old, hf, 0, c, :], gm[:, hf, c, :],
                                               start=True, stop=True)
                        mm.then_inc(s_y[hf], 1)

            def step2(name, w, g, h):
                slot = g % 2
                if name == "out":
                    pe.wait_ge(s_on, w + 1)
                    for c in range(CH):
                        mm = pe.transpose(p_t[:, c * P:(c + 1) * P], on[:, c, :], ident[:, :])
                    mm.then_inc(s_ot, 1)
                    return
                c = int(name[1])
                n = w * CH + c
                head_start = g == 0 and c == 0
                old = c % 2
                if name[0] == "v":
                    if c == 0:
                        pe.wait_ge(s_wn, w * 2 + 2)
                    pe.wait_ge(s_vn, n)
                    pe.matmul(p_v[:, 0:P], uf[:, slot, c, :], vb[:, slot, c, :], start=True, stop=head_start).then_inc(
                        s_v, 1) if head_start else pe.matmul(p_v[:, 0:P], uf[:, slot, c, :], vb[:, slot, c, :],
                                                             start=True, stop=False)
                    if not head_start:
                        pe.wait_ge(s_st, n)
                        pe.matmul(p_v[:, 0:P], nwT[:, slot, c, :], state[:, old, :], start=False, stop=True).then_inc(s_v, 1)
                else:
                    pe.wait_ge(s_oss, n)
                    if not head_start:
                        pe.matmul(p_o[:, 0:P], qe[:, slot, c, :], state[:, old, :], start=True, stop=False)
                    pe.wait_ge(s_vn, n + 1)
                    pe.matmul(p_s[:, 0:P], kt[:, slot, c, :], vn[:, c % 2, :], start=True, stop=True).then_inc(s_ds, 1)
                    pe.matmul(p_o[:, 0:P], attT[:, slot, c, :], vn[:, c % 2, :], start=head_start, stop=True).then_inc(s_o, 1)

            run(pe, step1, step2)

        @block.scalar
        def _(act):
            def step1(name, w, slot, g, h, nth):
                if name == "turns":
                    act.wait_ge(s_ktr, w + 1)
                    at_least(act, s_kw, w)
                    at_least(act, s_ktw, w)
                    act.activation(k_tok[:, :, :], halves(p1[0][:, :]), ACT.Copy).then_inc(s_ktok, 1)
                    at_least(act, s_ss, w)
                    act.activation(sq[:, 1, :, :], halves(p1[0][:, :]), ACT.Square).then_inc(s_sq, 1)
                    act.wait_ge(s_qtr, w + 1)
                    act.activation(sq[:, 0, :, :], halves(p1[2][:, :]), ACT.Square).then_inc(s_sq, 1)
                    act.wait_ge(s_g, w + 1)
                    at_least(act, s_qe, w)
                    act.activation(erow[:, :, :], halves(p1[3][:, :]), ACT.Exp).then_inc(s_er, 1)
                elif name == "decay":
                    act.wait_ge(s_sse, w + 1)
                    at_least(act, s_nb, w)
                    act.activation(lnk[:, :], sse[:, CH:2 * CH], ACT.Ln).then_inc(s_ln, 1)
                    act.wait_ge(s_gm, w + 1)
                    act.wait_ge(s_nb, w + 1)
                    at_least(act, s_lt, w)
                    for c in range(CH):
                        act.activation(dec[:, c, :], p1[3][:, c * P:(c + 1) * P], ACT.Exp, bias=nb[:, c:c + 1]).then_inc(s_dec, 1)
                elif name == "first":
                    for hf in range(2):
                        act.wait_ge(s_t0, w * 2 + hf + 1)
                        act.activation(ut[:, 0, hf, 1, :, :], p1[2 * hf][:, 0:2 * P].rearrange("p (c i) -> p c i", c=2),
                                       ACT.Copy).then_inc(s_t1, 1)
                elif name == "w":
                    for hf in range(2):
                        act.wait_ge(s_w, w * 2 + hf + 1)
                        act.activation(nwT[:, slot, 2 * hf:2 * hf + 2, :], p1[2 * hf][:, 0:2 * P].rearrange(
                            "p (c i) -> p c i", c=2), ACT.Copy, scale=-1.0).then_inc(s_wn, 1)
                elif isinstance(name, int):
                    n = name
                    for hf in range(2):
                        act.wait_ge(s_y[hf], w * (LEVELS - 1) + n)
                        if n < LEVELS - 1:
                            act.activation(ut[:, n % 2, hf, :, :, :].rearrange("p a c i -> p (a c) i"),
                                           halves(p1[2 * hf + 1][:, :]), ACT.Copy).then_inc(s_ut[hf], 1)
                        else:
                            at_least(act, s_ot, w - 1)
                            act.activation(uf[:, slot, 2 * hf:2 * hf + 2, :], p1[2 * hf + 1][:, 0:2 * P].rearrange(
                                "p (c i) -> p c i", c=2), ACT.Copy).then_inc(s_ut[hf], 1)

            def step2(name, w, g, h):
                slot = g % 2
                if name[0] == "s" and name != "out":
                    c = int(name[1])
                    n = w * CH + c
                    act.wait_ge(s_o, n + 1)
                    if c == 0:
                        at_least(act, s_on, w)
                        at_least(act, s_ose, w)
                    act.activation(o_sb[:, c, :], p_o[:, 0:P], ACT.Copy, scale=rq[:, slot, c:c + 1]).then_inc(s_os, 1)
                    at_least(act, s_oss, n)
                    act.activation(junk[:, :], p_o[:, 0:P], ACT.Square, scale=rq[:, slot, c:c + 1],
                                   accum_out=oss[:, c:c + 1]).then_inc(s_oss, 1)

            run(act, step1, step2)

        @block.vector
        def _(dve):
            dve.wait_ge(s_in, n_in)
            dve.tensor_copy(ident_b[:, :], ident[:, :]).then_inc(s_cst, 1)
            dve.tensor_copy(mask[:, :], mask_f[:, :]).then_inc(s_cst, 1)

            def step1(name, w, slot, g, h, nth):
                if name == "turns":
                    dve.wait_ge(s_vtr, w + 1)
                    dve.wait_ge(s_sm, w + 1)
                    at_least(dve, s_ot, w - 1)
                    dve.tensor_tensor(vb[:, slot, :, :], halves(p1[1][:, :]),
                                      sm[:, slot, 0, :].unsqueeze(2).to_broadcast([P, CH, P]), ALU.mult).then_inc(s_vb, 1)
                    dve.wait_ge(s_sq, w * 2 + 2)
                    at_least(dve, s_sse, w)
                    dve.tensor_reduce(ss[:, :], sq[:, :, :, :].rearrange("p a c i -> p (a c) i"), AX.X, ALU.add).then_inc(s_ss, 1)
                elif name == "decay":
                    dve.wait_ge(s_er, w + 1)
                    dve.tensor_tensor(qe[:, slot, :, :], halves(src[:, slot, 0, :]), erow[:, :, :], ALU.mult).then_inc(s_qe, 1)
                elif name == "rows":
                    dve.wait_ge(s_br, w + 1)
                    dve.tensor_tensor(kbT[:, :, :], halves(src[:, slot, 1, :]), halves(p1[0][:, :]), ALU.mult).then_inc(s_kb, 1)
                elif name == "scores":
                    dve.wait_ge(s_dec, w * CH + CH)
                    dve.wait_ge(s_kq, w + 1)
                    dve.tensor_tensor(attT[:, slot, :, :], halves(p1[2][:, :]), dec[:, :, :], ALU.mult).then_inc(s_att, 1)
                    dve.wait_ge(s_kk, w + 1)
                    at_least(dve, s_nbs, w * LEVELS)
                    dve.tensor_tensor(lt[:, :, :], halves(p1[1][:, :]), dec[:, :, :], ALU.mult).then_inc(s_lt, 1)
                elif name == "first":
                    dve.wait_ge(s_nbs, w * LEVELS + 1)
                    at_least(dve, s_y[1], w * (LEVELS - 1))
                    for hf in range(2):
                        mm = dve.tensor_tensor(ut[:, 0, hf, 0, :, :], nbs[:, 0, 2 * hf:2 * hf + 2, :],
                                               ident[:, :].unsqueeze(1).to_broadcast([P, 2, P]), ALU.add)
                    mm.then_inc(s_u0, 1)
                elif isinstance(name, int):
                    n = name
                    for hf in range(2):
                        dve.wait_ge(s_x[hf], w * (LEVELS - 1) + n)
                        dve.tensor_tensor(gm[:, hf, :, :], p1[2 * hf][:, 0:2 * P].rearrange("p (c i) -> p c i", c=2),
                                          ident[:, :].unsqueeze(1).to_broadcast([P, 2, P]), ALU.add).then_inc(s_gr[hf], 1)

            def step2(name, w, g, h):
                slot = g % 2
                if name == "out":
                    dve.wait_ge(s_orn, w + 1)
                    dve.wait_ge(s_os, w * CH + CH)
                    at_least(dve, s_ot, w)
                    dve.tensor_tensor(on[:, :, :], o_sb[:, :, :], orn[:, :].unsqueeze(2).to_broadcast([P, CH, P]),
                                      ALU.mult).then_inc(s_on, 1)
                    dve.wait_ge(s_ot, w + 1)
                    at_least(dve, s_oo, w * 16)
                    dve.scalar_tensor_tensor(oT[:, :, :], halves(p_t[:, :]), g_o[:, 0:1], halves(src[:, slot, 3, :]),
                                             ALU.mult, ALU.mult).then_inc(s_oT, 1)
                    return
                c = int(name[1])
                n = w * CH + c
                if name[0] == "v":
                    dve.wait_ge(s_v, n + 1)
                    at_least(dve, s_o, n if c == 0 else n - 1)
                    dve.tensor_copy(vn[:, c % 2, :], p_v[:, 0:P]).then_inc(s_vn, 1)
                else:
                    dve.wait_ge(s_ds, n + 1)
                    new = (c + 1) % 2
                    if g == 0 and c == 0:
                        dve.tensor_copy(state[:, new, :], p_s[:, 0:P]).then_inc(s_st, 1)
                    else:
                        if g == 0 and c == 1:
                            at_least(dve, s_fin, h * 16)
                        dve.wait_ge(s_st, n)
                        dve.scalar_tensor_tensor(state[:, new, :], state[:, c % 2, :], sm[:, slot, 4, c:c + 1],
                                                 p_s[:, 0:P], ALU.mult, ALU.add).then_inc(s_st, 1)

            run(dve, step1, step2)

        @block.gpsimd
        def _(pool):
            pool.memset(half[:, :], -0.5).then_inc(s_half, 1)

            def step1(name, w, slot, g, h, nth):
                if name == "turns":
                    at_least(pool, s_oT, w - 1)
                    pool.tensor_copy(sm[:, slot, :, :], gd[:, 0:5, g * CH:(g + 1) * CH, bass.ds(h, 1)].rearrange(
                        "p f c o -> p f (c o)")).then_inc(s_sm, 1)
                    pool.wait_ge(s_ss, w + 1)
                    at_least(pool, s_ln, w)
                    settle(pool, s_pool)
                    pool.tensor_scalar(sse[:, :], ss[:, :], EPS, None, ALU.add).then_inc(s_sse, 1)
                    pool.wait_ge(s_sse, w + 1)
                    pool.tensor_tensor(rn[:, :], sse[:, :], half[:, :], ALU.pow).then_inc(s_rn, 1)
                    pool.wait_ge(s_rn, w + 1)
                    pool.wait_ge(s_sm, w + 1)
                    at_least(pool, s_br, w)
                    pool.tensor_tensor(brk[:, :], sm[:, slot, 0, :], rn[:, CH:2 * CH], ALU.mult).then_inc(s_brk, 1)
                elif name == "decay":
                    pool.wait_ge(s_ln, w + 1)
                    at_least(pool, s_dec, w * CH)
                    settle(pool, s_pool)
                    pool.tensor_scalar(lnk[:, :], lnk[:, :], -0.5, None, ALU.mult).then_inc(s_kwf, 1)
                    pool.wait_ge(s_kwf, w * 2 + 1)
                    pool.tensor_tensor(nb[:, :], lnk[:, :], sm[:, slot, 1, :], ALU.subtract).then_inc(s_nb, 1)
                    at_least(pool, s_kw, w)
                    pool.wait_ge(s_brk, w + 1)
                    pool.tensor_tensor(kwf[:, :], brk[:, :], sm[:, slot, 2, :], ALU.mult).then_inc(s_kwf, 1)
                    at_least(pool, s_ktw, w)
                    at_least(pool, s_oss, (w - 1) * CH)
                    pool.tensor_tensor(ktf[:, :], rn[:, CH:2 * CH], sm[:, slot, 3, :], ALU.mult).then_inc(s_rq, 1)
                    pool.tensor_scalar(rq[:, slot, :], rn[:, 0:CH], D1 ** -0.5, None, ALU.mult).then_inc(s_rq, 1)
                elif name == "scores":
                    pool.wait_ge(s_lt, w + 1)
                    at_least(pool, s_x[1], w * (LEVELS - 1))
                    for n in range(LEVELS):
                        pool.tensor_tensor(nbs[:, n, :, :], lt[:, :, :], levels[:, n, :].unsqueeze(1).to_broadcast([P, CH, P]),
                                           ALU.mult).then_inc(s_nbs, 1)
                    pool.wait_ge(s_ktok, w + 1)
                    pool.wait_ge(s_kwf, w * 2 + 2)
                    at_least(pool, s_w, w * 2)
                    pool.tensor_tensor(kw[:, :, :], k_tok[:, :, :], kwf[:, :].unsqueeze(2).to_broadcast([P, CH, P]),
                                       ALU.mult).then_inc(s_kw, 1)
                    pool.wait_ge(s_rq, w * 2 + 2)
                    at_least(pool, s_ds, (w - 1) * CH)
                    pool.tensor_tensor(kt[:, slot, :, :], k_tok[:, :, :], ktf[:, :].unsqueeze(2).to_broadcast([P, CH, P]),
                                       ALU.mult).then_inc(s_ktw, 1)

            def step2(name, w, g, h):
                if name == "s3":
                    pool.wait_ge(s_oss, w * CH + CH)
                    at_least(pool, s_orn, w)
                    settle(pool, s_pool)
                    pool.tensor_scalar(ose[:, :], oss[:, :], 1.0 / D1, EPS, ALU.mult, ALU.add).then_inc(s_ose, 1)
                    pool.wait_ge(s_ose, w + 1)
                    at_least(pool, s_on, w)
                    pool.tensor_tensor(orn[:, :], ose[:, :], half[:, 0:CH], ALU.pow).then_inc(s_orn, 1)

            pool.wait_ge(s_in, n_in)
            pool.wait_ge(s_half, 1)
            run(pool, step1, step2)


def stage_h(nc, io, cat, gd):
    with Stage(nc, "H") as st:
        sb, ps, sem = st.sb, st.ps, st.sem
        ident = sb("ident", [P, P])
        own = sb("own", [P, DB])
        own_cols = sb("own_cols", [P, DB, NS])
        mask = sb("mask", [NS, NS])
        strict = sb("strict", [NS, NS])
        g_o = sb("g_o", [P, 1])
        half = sb("half", [NS, 2 * H1])
        src = sb("src", [P, 4, H1, NS])
        state = sb("state", [P, DB, H1, D1])
        faded = sb("faded", [P, DB, H1, D1])
        k_tok, q_tok, kb, kt, kw, vb, vn, sq_k, sq_q, qe = (sb(n, [NS, H1, D1]) for n in (
            "k_tok", "q_tok", "kb", "kt", "kw", "vb", "vn", "sq_k", "sq_q", "qe"))
        ss, sse, rn = (sb(n, [NS, 2, H1]) for n in ("ss", "sse", "rn"))
        oss, ose, orn = (sb(n, [NS, H1]) for n in ("oss", "ose", "orn"))
        gap = sb("gap", [NS, H1, NS])
        dec = sb("dec", [NS, H1, NS])
        turned = sb("turned", [P, 3, H1, NS])
        qnT = sb("qnT", [P, H1, NS])
        att, m, n_, r, u = (sb(x, [NS, H1, NS]) for x in ("att", "m", "n", "r", "u"))
        mi = sb("mi", [NS, H1, NS])
        wz, qz = (sb(n, [P, H1, DB, NS]) for n in ("wz", "qz"))
        vx = sb("vx", [NS, 2, DB, D1])
        oT = sb("oT", [P, H1, NS])
        p = [ps(f"b{i}") for i in range(8)]
        s_in, s_src, s_state, s_half = sem("loaded"), sem("src_in"), sem("state_in"), sem("half_set")
        s_tr, s_qk, s_sq, s_ss, s_sse, s_rn = (sem(n) for n in ("turned", "qk_out", "squares", "sums", "sums_eps", "norms"))
        s_vb, s_kn, s_qn, s_kb, s_kw, s_kt, s_qe = (sem(n) for n in ("vb", "k_normed", "q_normed", "kb", "kw", "kt", "q_exp"))
        s_g, s_gap1, s_gap2, s_dec = (sem(n) for n in ("gc_rows", "gc_masked", "gap", "decay"))
        s_bt, s_bT, s_kk, s_m1, s_m, s_mi, s_att = (sem(n) for n in (
            "back_turned", "back_ready", "scores", "m_decayed", "m_ready", "m_plus_i", "att_ready"))
        s_nt, s_n, s_nn, s_r, s_up, s_u, s_wp, s_wz, s_qz = (sem(n) for n in (
            "m_turned", "n_ready", "n_squared", "r_ready", "u_product", "u_ready", "w_product", "w_spread", "q_spread"))
        s_v, s_vn, s_vx, s_ds, s_new, s_o = (sem(n) for n in (
            "v_product", "v_new", "v_spread", "state_product", "state_ready", "o_product"))
        s_osq, s_oss, s_ose, s_orn, s_on, s_ot, s_oT = (sem(n) for n in (
            "o_squares", "o_sums", "o_mean", "o_norm", "o_normed", "o_turned", "oT_ready"))
        s_fade, s_out = sem("faded"), sem("stored")
        block = st.block()
        loads = [(ident[:, :], io["consts"][:, cat["ident"][0]:cat["ident"][1]]),
                 (own[:, :], io["consts"][:, cat["own_batch"][0]:cat["own_batch"][1]]),
                 (own_cols[:, :, :], io["consts"][:, cat["own_cols"][0]:cat["own_cols"][1]].rearrange(
                     "p (b t) -> p b t", t=NS)),
                 (mask[:, :], io["consts"][0:NS, cat["mask_tri_samp"][0]:cat["mask_tri_samp"][0] + NS]),
                 (strict[:, :], io["consts"][0:NS, cat["strict_samp"][0]:cat["strict_samp"][0] + NS]),
                 (g_o[:, :], io["o_norm"].rearrange("o e -> e o"))]
        n_in = 16 * len(loads)
        col = lambda a: a.unsqueeze(2).to_broadcast([NS, H1, D1])
        beta, gc, egc, erest = (gd[0:NS, f, NT, :] for f in range(4))

        def heads(bank, n):
            return p[bank + n][0:NS, :].rearrange("p (h d) -> p h d", d=D1)

        @block.sync
        def _(sp):
            for n in range(4):
                sp.dma_start(src[:, n, :, :], io["strips"][n * H1:(n + 1) * H1, :, SEQ:SEQ + NS].rearrange(
                    "h p t -> p h t")).then_inc(s_src, 16)
            load_all(sp, s_in, loads)
            for b in range(DB):
                sp.dma_start(state[:, b, :, :], io["state_delta"][0, b, :, :, :].rearrange("h k v -> k h v")).then_inc(
                    s_state, 16)
            for h in range(H1):
                sp.wait_ge(s_new, 2 * h + 2)
                sp.dma_start(io["delta_sample"][0, :, h, :, :].rearrange("b k v -> k b v"), faded[:, :, h, :]).then_inc(
                    s_out, 16)
            sp.wait_ge(s_oT, 1)
            sp.dma_start(io["oT"][:, :, SEQ:SEQ + NS].rearrange("h p t -> p h t"), oT[:, :, :]).then_inc(s_out, 16)
            sp.wait_ge(s_out, 16 * (H1 + 1))

        @block.tensor
        def _(pe):
            pe.wait_ge(s_in, n_in)
            pe.wait_ge(s_src, 64)
            for bank, n in ((0, 1), (2, 0), (4, 2)):
                for h in range(H1):
                    mm = pe.transpose(p[bank + h // 4][0:NS, h % 4 * D1:(h % 4 + 1) * D1], src[:, n, h, :], ident[:, :])
                mm.then_inc(s_tr, 1)
            for h in range(H1):
                mm = pe.matmul(p[6][0:NS, h * NS:(h + 1) * NS], gd[0:NS, 1, NT, h:h + 1].to_broadcast([NS, NS]),
                               ident[0:NS, 0:NS], start=True, stop=True)
            mm.then_inc(s_g, 1)
            for n, (ready, t) in enumerate(((s_kn, k_tok), (s_kb, kb), (s_qe, qe), (s_qn, q_tok))):
                pe.wait_ge(ready, 1)
                for h in range(H1):
                    mm = pe.transpose(p[n][:, h * NS:(h + 1) * NS], t[:, h, :], ident[0:NS, 0:NS])
                mm.then_inc(s_bt, 1)
            pe.wait_ge(s_bT, 4)
            pe.wait_ge(s_vb, 2)
            for bank, t in ((4, turned[:, 1]), (5, qnT)):
                for h in range(H1):
                    mm = pe.matmul(p[bank][0:NS, h * NS:(h + 1) * NS], turned[:, 0, h, :], t[:, h, :], start=True, stop=True)
                mm.then_inc(s_kk, 1)
            pe.wait_ge(s_m, 1)
            for h in range(H1):
                mm = pe.transpose(p[7][0:NS, h * NS:(h + 1) * NS], m[:, h, :], ident[0:NS, 0:NS])
            mm.then_inc(s_nt, 1)
            pe.wait_ge(s_n, 1)
            for h in range(H1):
                mm = pe.matmul(p[0][0:NS, h * NS:(h + 1) * NS], m[:, h, :], n_[:, h, :], start=True, stop=True)
            mm.then_inc(s_nn, 1)
            pe.wait_ge(s_r, 1)
            pe.wait_ge(s_mi, 1)
            for h in range(H1):
                mm = pe.matmul(p[1][0:NS, h * NS:(h + 1) * NS], r[:, h, :], mi[:, h, :], start=True, stop=True)
            mm.then_inc(s_up, 1)
            pe.wait_ge(s_u, 1)
            pe.wait_ge(s_kw, 1)
            for h in range(H1):
                mm = pe.matmul(p[6][:, h * NS:(h + 1) * NS], kw[:, h, :], u[:, h, :], start=True, stop=True)
            mm.then_inc(s_wp, 1)
            pe.wait_ge(s_wz, 1)
            pe.wait_ge(s_state, 16 * DB)
            pe.wait_ge(s_vb, 2)
            for h in range(H1):
                out = p[h // 4][0:NS, h % 4 * D1:(h % 4 + 1) * D1]
                pe.matmul(out, u[:, h, :], vb[:, h, :], start=True, stop=False)
                for b in range(DB):
                    mm = pe.matmul(out, wz[:, h, b, :], state[:, b, h, :], start=False, stop=(b == DB - 1))
                if h % 4 == 3:
                    mm.then_inc(s_v, 1)
            pe.wait_ge(s_qz, 1)
            pe.wait_ge(s_att, 1)
            for h in range(H1):
                out = p[2 + h // 4][0:NS, h % 4 * D1:(h % 4 + 1) * D1]
                for b in range(DB):
                    pe.matmul(out, qz[:, h, b, :], state[:, b, h, :], start=(b == 0), stop=False)
                pe.wait_ge(s_vn, h // 4 + 1)
                mm = pe.matmul(out, att[:, h, :], vn[:, h, :], start=False, stop=True)
                if h % 4 == 3:
                    mm.then_inc(s_o, 1)
            pe.wait_ge(s_kt, 1)
            for h in range(H1):
                pe.wait_ge(s_vx, h + 1)
                for n in range(2):
                    if h >= 2:
                        pe.wait_ge(s_new, 2 * (h - 2) + n + 1)
                    pe.matmul(p[4 + h % 2 * 2 + n][:, :], kt[:, h, :], vx[:, h % 2, 4 * n:4 * n + 4, :].rearrange(
                        "p b d -> p (b d)"), start=True, stop=True).then_inc(s_ds, 1)
            pe.wait_ge(s_on, 1)
            for h in range(H1):
                mm = pe.transpose(p[0][:, h * NS:(h + 1) * NS], sq_k[:, h, :], ident[0:NS, 0:NS])
            mm.then_inc(s_ot, 1)

        @block.scalar
        def _(act):
            act.wait_ge(s_tr, 1)
            for n in range(2):
                act.activation(sq_k[:, 4 * n:4 * n + 4, :], heads(0, n), ACT.Square).then_inc(s_sq, 1)
            act.wait_ge(s_tr, 2)
            for n in range(2):
                act.activation(sq_q[:, 4 * n:4 * n + 4, :], heads(2, n), ACT.Square).then_inc(s_sq, 1)
            act.wait_ge(s_gap2, 1)
            act.activation(dec[:, :, :], gap[:, :, :], ACT.Exp).then_inc(s_dec, 1)
            for n, dst in enumerate((turned[:, 0], turned[:, 1], turned[:, 2], qnT[:, :, :])):
                act.wait_ge(s_bt, n + 1)
                act.activation(dst, p[n][:, 0:H1 * NS].rearrange("p (h t) -> p h t", t=NS),
                               ACT.Copy).then_inc(s_bT, 1)
            act.wait_ge(s_nt, 1)
            act.activation(n_[:, :, :], p[7][0:NS, 0:H1 * NS].rearrange("p (h t) -> p h t", t=NS), ACT.Copy).then_inc(s_n, 1)
            act.wait_ge(s_up, 1)
            act.activation(u[:, :, :], p[1][0:NS, 0:H1 * NS].rearrange("p (h t) -> p h t", t=NS), ACT.Copy).then_inc(s_u, 1)
            for n in range(2):
                act.wait_ge(s_v, n + 1)
                act.activation(vn[:, 4 * n:4 * n + 4, :], heads(0, n), ACT.Copy).then_inc(s_vn, 1)
            act.wait_ge(s_ss, 1)
            for n in range(2):
                act.wait_ge(s_o, n + 1)
                act.activation(sq_q[:, 4 * n:4 * n + 4, :], heads(2, n), ACT.Square).then_inc(s_osq, 1)

        def grow(dve, h):
            dve.wait_ge(s_fade, h + 1)
            for n in range(2):
                dve.wait_ge(s_ds, 2 * h + n + 1)
                dve.tensor_tensor(faded[:, 4 * n:4 * n + 4, h, :], faded[:, 4 * n:4 * n + 4, h, :],
                                  p[4 + h % 2 * 2 + n][:, :].rearrange("p (b d) -> p b d", d=D1),
                                  ALU.add).then_inc(s_new, 1)

        @block.vector
        def _(dve):
            dve.wait_ge(s_tr, 3)
            for n in range(2):
                dve.tensor_tensor(vb[:, 4 * n:4 * n + 4, :], heads(4, n), col(beta)[:, 4 * n:4 * n + 4, :],
                                  ALU.mult).then_inc(s_vb, 1)
            dve.wait_ge(s_g, 1)
            dve.wait_ge(s_in, n_in)
            dve.tensor_tensor(gap[:, :, :], p[6][0:NS, 0:H1 * NS].rearrange("p (h t) -> p h t", t=NS),
                              mask[:, :].unsqueeze(1).to_broadcast([NS, H1, NS]), ALU.add).then_inc(s_gap1, 1)
            dve.wait_ge(s_gap1, 1)
            dve.tensor_tensor(gap[:, :, :], gap[:, :, :], gc.unsqueeze(2).to_broadcast([NS, H1, NS]),
                              ALU.subtract).then_inc(s_gap2, 1)
            dve.wait_ge(s_sq, 4)
            dve.tensor_reduce(ss[:, 0, :], sq_k[:, :, :], AX.X, ALU.add)
            dve.tensor_reduce(ss[:, 1, :], sq_q[:, :, :], AX.X, ALU.add).then_inc(s_ss, 1)
            dve.wait_ge(s_rn, 1)
            for n in range(2):
                mm = dve.tensor_tensor(k_tok[:, 4 * n:4 * n + 4, :], heads(0, n), col(rn[:, 0, :])[:, 4 * n:4 * n + 4, :],
                                       ALU.mult)
            mm.then_inc(s_kn, 1)
            dve.wait_ge(s_kn, 1)
            dve.tensor_tensor(kb[:, :, :], k_tok[:, :, :], col(beta), ALU.mult).then_inc(s_kb, 1)
            for n in range(2):
                mm = dve.scalar_tensor_tensor(q_tok[:, 4 * n:4 * n + 4, :], heads(2, n), D1 ** -0.5,
                                              col(rn[:, 1, :])[:, 4 * n:4 * n + 4, :], ALU.mult, ALU.mult)
            mm.then_inc(s_qn, 1)
            dve.wait_ge(s_qn, 1)
            dve.tensor_tensor(qe[:, :, :], q_tok[:, :, :], col(egc), ALU.mult).then_inc(s_qe, 1)
            dve.wait_ge(s_kb, 1)
            dve.scalar_tensor_tensor(kw[:, :, :], kb[:, :, :], -1.0, col(egc), ALU.mult, ALU.mult).then_inc(s_kw, 1)
            dve.tensor_tensor(kt[:, :, :], k_tok[:, :, :], col(erest), ALU.mult).then_inc(s_kt, 1)
            dve.wait_ge(s_bT, 3)
            dve.tensor_tensor(qz[:, :, :, :], turned[:, 2].unsqueeze(2).to_broadcast([P, H1, DB, NS]),
                              own_cols[:, :, :].unsqueeze(1).to_broadcast([P, H1, DB, NS]), ALU.mult).then_inc(s_qz, 1)
            dve.wait_ge(s_dec, 1)
            dve.wait_ge(s_kk, 2)
            dve.tensor_tensor(m[:, :, :], p[4][0:NS, 0:H1 * NS].rearrange("p (h t) -> p h t", t=NS), dec[:, :, :],
                              ALU.mult).then_inc(s_m1, 1)
            dve.wait_ge(s_m1, 1)
            dve.tensor_tensor(m[:, :, :], m[:, :, :], strict[:, :].unsqueeze(1).to_broadcast([NS, H1, NS]),
                              ALU.mult).then_inc(s_m, 1)
            eye = ident[0:NS, 0:NS].unsqueeze(1).to_broadcast([NS, H1, NS])
            dve.tensor_tensor(att[:, :, :], p[5][0:NS, 0:H1 * NS].rearrange("p (h t) -> p h t", t=NS), dec[:, :, :],
                              ALU.mult).then_inc(s_att, 1)
            dve.wait_ge(s_m, 1)
            dve.tensor_tensor(mi[:, :, :], m[:, :, :], eye, ALU.add).then_inc(s_mi, 1)
            dve.wait_ge(s_nn, 1)
            dve.tensor_tensor(r[:, :, :], p[0][0:NS, 0:H1 * NS].rearrange("p (h t) -> p h t", t=NS), eye,
                              ALU.add).then_inc(s_r, 1)
            dve.wait_ge(s_wp, 1)
            dve.tensor_tensor(wz[:, :, :, :], p[6][:, 0:H1 * NS].rearrange("p (h t) -> p h t", t=NS).unsqueeze(
                2).to_broadcast([P, H1, DB, NS]), own_cols[:, :, :].unsqueeze(1).to_broadcast([P, H1, DB, NS]),
                ALU.mult).then_inc(s_wz, 1)
            for h in range(H1):
                dve.wait_ge(s_vn, h // 4 + 1)
                if h >= 2:
                    dve.wait_ge(s_ds, 2 * h - 2)
                dve.tensor_tensor(vx[:, h % 2, :, :], vn[:, h, :].unsqueeze(1).to_broadcast([NS, DB, D1]),
                                  own[0:NS, :].unsqueeze(2).to_broadcast([NS, DB, D1]), ALU.mult).then_inc(s_vx, 1)
                if h >= 1:
                    grow(dve, h - 1)
            grow(dve, H1 - 1)
            dve.wait_ge(s_osq, 2)
            dve.tensor_reduce(oss[:, :], sq_q[:, :, :], AX.X, ALU.add).then_inc(s_oss, 1)
            dve.wait_ge(s_orn, 1)
            for n in range(2):
                mm = dve.tensor_tensor(sq_k[:, 4 * n:4 * n + 4, :], heads(2, n), col(orn[:, :])[:, 4 * n:4 * n + 4, :],
                                       ALU.mult)
            mm.then_inc(s_on, 1)
            dve.wait_ge(s_ot, 1)
            dve.scalar_tensor_tensor(oT[:, :, :], p[0][:, 0:H1 * NS].rearrange("p (h t) -> p h t", t=NS), g_o[:, 0:1],
                                     src[:, 3, :, :], ALU.mult, ALU.mult).then_inc(s_oT, 1)

        @block.gpsimd
        def _(pool):
            pool.memset(half[:, :], -0.5).then_inc(s_half, 1)
            pool.wait_ge(s_half, 1)
            pool.wait_ge(s_ss, 1)
            pool.tensor_scalar(sse[:, :, :], ss[:, :, :], EPS, None, ALU.add).then_inc(s_sse, 1)
            pool.wait_ge(s_sse, 1)
            pool.tensor_tensor(rn[:, :, :], sse[:, :, :], half[:, :].rearrange("p (a h) -> p a h", a=2),
                               ALU.pow).then_inc(s_rn, 1)
            pool.wait_ge(s_state, 16 * DB)
            for h in range(H1):
                pool.tensor_tensor(faded[:, :, h, :], state[:, :, h, :], gd[:, 5, 0:DB, h].unsqueeze(2).to_broadcast(
                    [P, DB, D1]), ALU.mult).then_inc(s_fade, 1)
            pool.wait_ge(s_oss, 1)
            pool.tensor_scalar(ose[:, :], oss[:, :], 1.0 / D1, EPS, ALU.mult, ALU.add).then_inc(s_ose, 1)
            pool.wait_ge(s_ose, 1)
            pool.tensor_tensor(orn[:, :], ose[:, :], half[:, 0:H1], ALU.pow).then_inc(s_orn, 1)


def stage_f(nc, io, cat):
    with Stage(nc, "F") as st:
        sb, ps, sem = st.sb, st.ps, st.sem
        w_raw = sb("w_raw", [P, H1, DM])
        w_hi, w_lo = (sb(n, [P, H1, DM], F32R) for n in ("w_hi", "w_lo"))
        o = sb("o", [P, 2, H1, P])
        h1 = sb("h1", [P, 2, DM])
        o_hi, o_lo = (sb(n, [P, 2, H1, P], F32R) for n in ("o_hi", "o_lo"))
        y = sb("y", [P, 2, DM])
        p_y = [ps(f"y{i}") for i in range(4)]
        s_w = [sem(f"w_in{k}") for k in range(H1)]
        s_whi, s_wlo = sem("w_hi"), sem("w_lo")
        s_o = [sem(f"o_in{i}") for i in range(2)]
        s_h = [sem(f"h1_in{i}") for i in range(2)]
        s_ohi, s_olo, s_p, s_y = (sem(n) for n in ("o_hi", "o_lo", "projected", "y_ready"))
        s_st = [sem(f"stored{i}") for i in range(2)]
        s_sp = sem("sync_waits_settled")
        block = st.block()

        def tiles(eng, body):
            for t in range(2):
                body(t, t, 0)
            with eng.Fori(1, NT // 2 - 1) as i:
                body(i * 2, 0, i)
                body(i * 2 + 1, 1, i)
            for t in range(NT - 2, NT + 1):
                body(t, t % 2, t // 2)

        @block.sync
        def _(sp):
            def load(t, slot):
                n = NS if isinstance(t, int) and t == NT else P
                sp.dma_start(o[:, slot, :, 0:n], io["oT"][:, :, bass.ds(t * P, n)].rearrange("h p n -> p h n")).then_inc(
                    s_o[slot], 16)
                sp.dma_start(h1[0:n, slot, :], io["h1"][bass.ds(t, 1), 0:n, :].rearrange("o p n -> p (o n)")).then_inc(
                    s_h[slot], 16)

            for k in range(H1):
                sp.dma_start(w_raw[:, k, :], io["w_out_odd"][0, k * P:(k + 1) * P, :]).then_inc(s_w[k], 16)
                if k == 0:
                    load(0, 0)
                    load(1, 1)

            def body(t, slot, nth):
                sp.wait_ge(s_y, t * 2 + 2)
                settle(sp, s_sp)
                if isinstance(t, int) and t == NT:
                    sp.dma_start(io["y_sample"].rearrange("b t d -> (b t) d"), y[0:NS, slot, :]).then_inc(s_st[slot], 16)
                else:
                    sp.dma_start(io["y_prompt"][0, bass.ds(t * P, P), :], y[:, slot, :]).then_inc(s_st[slot], 16)
                if not (isinstance(t, int) and t >= NT - 1):
                    load(t + 2, slot)

            tiles(sp, body)
            sp.wait_ge(s_st[0], 16 * (NT // 2 + 1))
            sp.wait_ge(s_st[1], 16 * (NT // 2))

        @block.tensor
        def _(pe):
            def body(t, slot, nth):
                m = NS if isinstance(t, int) and t == NT else P
                pe.wait_ge(s_olo, t + 1)
                at_least(pe, s_y, t * 2 - 2)
                for n in range(2):
                    cols = slice(n * 512, (n + 1) * 512)
                    out = p_y[2 * slot + n][0:m, :]
                    for k in range(H1):
                        if isinstance(t, int) and t == 0:
                            pe.wait_ge(s_wlo, k + 1)
                        pe.matmul(out, o_hi[:, slot, k, 0:m], w_hi[:, k, cols], start=(k == 0), stop=False)
                        pe.matmul(out, o_hi[:, slot, k, 0:m], w_lo[:, k, cols], start=False, stop=False)
                        mm = pe.matmul(out, o_lo[:, slot, k, 0:m], w_hi[:, k, cols], start=False, stop=(k == H1 - 1))
                    mm.then_inc(s_p, 1)

            tiles(pe, body)

        @block.scalar
        def _(act):
            def body(t, slot, nth):
                n = NS if isinstance(t, int) and t == NT else P
                act.wait_ge(s_o[slot], nth * 16 + 16)
                at_least(act, s_p, t * 2 - 2)
                act.activation(o_hi[:, slot, :, 0:n], o[:, slot, :, 0:n], ACT.Copy).then_inc(s_ohi, 1)
                if isinstance(t, int) and t == 0:
                    for k in range(H1):
                        act.wait_ge(s_w[k], 16)
                        act.activation(w_hi[:, k, :], w_raw[:, k, :], ACT.Copy).then_inc(s_whi, 1)

            tiles(act, body)

        @block.vector
        def _(dve):
            def split_o(t, slot, nth):
                n = NS if isinstance(t, int) and t == NT else P
                dve.wait_ge(s_ohi, t + 1)
                dve.wait_ge(s_o[slot], nth * 16 + 16)
                at_least(dve, s_p, t * 2 - 2)
                dve.tensor_tensor(o_lo[:, slot, :, 0:n], o[:, slot, :, 0:n], o_hi[:, slot, :, 0:n].bitcast(F32),
                                  ALU.subtract).then_inc(s_olo, 1)

            def body(t, slot, nth):
                if isinstance(t, int) and t == 0:
                    split_o(0, 0, 0)
                    for k in range(H1):
                        dve.wait_ge(s_whi, k + 1)
                        dve.tensor_tensor(w_lo[:, k, :], w_raw[:, k, :], w_hi[:, k, :].bitcast(F32),
                                          ALU.subtract).then_inc(s_wlo, 1)
                m = NS if isinstance(t, int) and t == NT else P
                if not (isinstance(t, int) and t == NT):
                    split_o(t + 1, 1 - slot, nth + slot)
                dve.wait_ge(s_h[slot], nth * 16 + 16)
                dve.wait_ge(s_st[slot], nth * 16) if not (isinstance(t, int) and t < 2) else None
                for n in range(2):
                    dve.wait_ge(s_p, t * 2 + (n + 1))
                    dve.tensor_tensor(y[0:m, slot, n * 512:(n + 1) * 512], p_y[2 * slot + n][0:m, :],
                                      h1[0:m, slot, n * 512:(n + 1) * 512], ALU.add).then_inc(s_y, 1)

            tiles(dve, body)


OUTS = [("y_prompt", (1, SEQ, DM)), ("y_sample", (DB, DS, DM)),
        ("pool_prompt", (1, 1, BUF, W0)), ("pool_sample", (1, DB, BUF, W0)),
        ("k_prompt", (1, 1, SEQ, H0, HD)), ("v_prompt", (1, 1, SEQ, H0, HD)),
        ("k_sample", (1, DB, DS, H0, HD)), ("v_sample", (1, DB, DS, H0, HD)),
        ("conv_prompt", (1, 1, CW - 1, CONV)), ("conv_sample", (1, DB, CW - 1, CONV)),
        ("delta_prompt", (1, 1, H1, D1, D1)), ("delta_sample", (1, DB, H1, D1, D1))]
SCRATCH = [("mixgate", (NT + 1, P, DM)),
           ("q_turned", ((NT + 1) * 4, P, P)),
           ("h1", (NT + 1, P, DM)),
           ("xT_hi", (P, KC, (NT + 1) * P)), ("xT_lo", (P, KC, (NT + 1) * P)),
           ("strips", (4 * H1, P, SEQ + NS)),
           ("oT", (H1, P, (NT + 1) * P))]


def build(nc, io, cat):
    with nc.sbuf_tensor("ba", [P, NT + 1, 2 * H1], F32) as ba, nc.sbuf_tensor("gd", [P, 6, NT + 1, H1], F32) as gd:
        with nc.sbuf_tensor("kT", [P, 4, (NT + 1) * P], F32) as kT:
            stage_a(nc, io, cat, kT)
            with nc.sbuf_tensor("o_all", [P, NT + 1, W0], F32) as o_all:
                stage_b(nc, io, cat, kT, o_all)
                stage_s(nc, io, cat, kT, o_all)
                stage_c(nc, io, cat, o_all, ba)
        stage_g(nc, io, cat, ba, gd)
        stage_d(nc, io, cat)
        stage_e(nc, io, cat, gd)
        stage_h(nc, io, cat, gd)
        stage_f(nc, io, cat)


def kernel(**inputs):
    import concourse.bacc as bacc
    from concourse.bass_utils import run_bass_kernel_spmd

    nc = bacc.Bacc("TRN2", target_bir_lowering=False, num_devices=1)
    consts, cat = constants()
    arrays = {name: np.ascontiguousarray(a) for name, a in inputs.items()}
    arrays["consts"] = consts
    io = {}
    for name, a in arrays.items():
        io[name] = nc.dram_tensor(f"in_{name}", a.shape, mybir.dt.from_np(a.dtype), kind="ExternalInput").ap()
    for name, shape in OUTS:
        io[name] = nc.dram_tensor(f"out_{name}", shape, F32, kind="ExternalOutput").ap()
    for name, shape in SCRATCH:
        io[name] = nc.dram_tensor(f"scratch_{name}", shape, F32, kind="Internal").ap()
    build(nc, io, cat)
    r = run_bass_kernel_spmd(nc, [{f"in_{name}": a for name, a in arrays.items()}], core_ids=[0])
    return tuple(r.results[0][f"out_{name}"] for name, _ in OUTS)
```

```python
from contextlib import ExitStack

import numpy as np

import concourse.bass as bass
import concourse.mybir as mybir

F32 = mybir.dt.float32
F32R = mybir.dt.float32r
BF16 = mybir.dt.bfloat16
I32 = mybir.dt.int32
ALU = mybir.AluOpType
ACT = mybir.ActivationFunctionType
AX = mybir.AxisListType

P = 128
DM = 1024
KC = DM // P
SEQ = 2048
NT = SEQ // P
DB, DS = 8, 4
NS = DB * DS
PAST = 2048
PAGE = 128
NPG = PAST // PAGE
EPS = 1e-6
H0, HD = 8, 64
W0 = H0 * HD
NG, WIN = 4, (2, 4, 8, 16)
BUF = max(WIN) - 1
EVEN_IN = W0 + 3 * W0 + DM
H1, D1 = 8, 128
QK = H1 * D1
CONV = 3 * QK
CW = 4
ODD_IN = CONV + QK + 2 * H1
LEVELS = 7
NEG = -1e30



def constants():
    j, i = np.arange(P)[:, None], np.arange(P)[None, :]
    out = {"ident": (j == i)}
    first, cur, prev, samp, samp_buf = ([] for _ in range(5))
    for w in WIN:
        own = (i - j >= 0) & (i - j < w)
        first.append(own / np.minimum(i + 1, w) - (i == j))
        cur.append(own / w - (i == j))
        prev.append((i + P - j < w) / w)
        same = (i // DS == j // DS) & (i < NS) & (j < NS)
        samp.append((same & own) / w - ((i == j) & (i < NS)))
        dist = i % DS + BUF - j % BUF
        samp_buf.append(((j // BUF == i // DS) & (i < NS) & (j < DB * BUF) & (dist < w)) / w)
    for name, band in (("band_first", first), ("band", cur), ("band_prev", prev), ("band_samp", samp),
                       ("band_buf", samp_buf)):
        out[name] = np.concatenate(band, 1)
    y = np.arange(7 * P)[None, :]
    out["mask_q"] = np.where(y - 3 * P >= j, NEG, 0.0)
    key = np.arange(2 * NS)[None, :]
    g, kb, kt = key // NS, key % NS // DS, key % DS
    out["mask_new"] = np.where((kb == 4 * g + j // NS) & (kt < j % DS), 0.0, NEG)
    out["own_head"] = (np.arange(W0)[None, :] // HD == (j % NS) // DS)
    out["to_token"] = ((kb == 4 * g + j // NS) & (kt == j % DS))
    out["row_head"] = (j == i % NS // DS)
    out["tri"] = (j <= i)
    out["mask_tri"] = np.tile(np.where(j <= i, 0.0, NEG), (1, 4))
    same = (i // DS == j // DS)
    out["tri_samp"] = (j <= i) & same
    out["mask_tri_samp"] = np.where((j <= i) & same, 0.0, NEG)
    out["last_samp"] = (i // DS == j // DS) * 1.0
    for n in range(LEVELS):
        s = 1 << n
        out[f"level{n}"] = -1.0 * ((i // (2 * s) == j // (2 * s)) & (i // s % 2 == 1) & (j // s % 2 == 0))
    out["strict_samp"] = -1.0 * ((j < i) & same)
    out["own_cols"] = (np.arange(DB * NS)[None, :] // NS == np.arange(DB * NS)[None, :] % NS // DS)
    out["own_batch"] = (np.arange(DB)[None, :] == j // DS)
    at, parts = {}, []
    n = 0
    for name, a in out.items():
        a = np.ascontiguousarray(np.broadcast_to(a, (P, a.shape[1])), dtype=np.float32)
        at[name] = (n, n + a.shape[1])
        n += a.shape[1]
        parts.append(a)
    return np.concatenate(parts, 1), at


def load_all(eng, sem, pairs):
    for dst, src in pairs:
        eng.dma_start(dst, src, allow_slow_non_contiguous=True).then_inc(sem, 16)
    return 16 * len(pairs)


def at_least(eng, sem, value):
    if not isinstance(value, int) or value > 0:
        eng.wait_ge(sem, value)


def settle(eng, sem):
    eng.sem_inc(sem, 1)


class Stage:

    def __init__(self, nc, tag):
        self.nc, self.tag, self.ctx = nc, tag, ExitStack()
        self.sems = []

    def __enter__(self):
        self.ctx.__enter__()
        return self

    def __exit__(self, *a):
        self.ctx.__exit__(*a)
        self.nc.clear_and_free_semaphores(self.sems)
        self.nc.all_engine_barrier()

    def sb(self, name, shape, dt=F32):
        return self.ctx.enter_context(self.nc.sbuf_tensor(f"{self.tag}_{name}", shape, dt))

    def ps(self, name, shape=(P, 512)):
        return self.ctx.enter_context(self.nc.psum_tensor(f"{self.tag}_ps_{name}", list(shape), F32))

    def sem(self, name):
        self.sems.append(self.nc.alloc_semaphore(name=f"{self.tag}_{name}"))
        return self.sems[-1]

    def block(self):
        return self.ctx.enter_context(self.nc.Block())


def tiles(eng, body):
    for t in range(2):
        body(t, t, 0)
    with eng.Fori(1, NT // 2 - 1) as i:
        body(i * 2, 0, i)
        body(i * 2 + 1, 1, i)
    for t in range(NT - 2, NT + 1):
        body(t, t % 2, t // 2)


def stage_a(nc, io, cat, heads):
    with Stage(nc, "Q" if heads else "A") as st:
        sb, ps, sem = st.sb, st.ps, st.sem
        NB = 3
        cols = [W0, 2 * W0, 3 * W0] if heads else [0, 4 * W0, 5 * W0]
        w_raw = sb("w_raw", [P, 2, NB, W0])
        w_hi, w_lo = (sb(n, [P, KC, NB, W0], F32R) for n in ("w_hi", "w_lo"))
        ident = sb("ident", [P, P])
        g_in = sb("g_in", [P, KC])
        x = sb("x", [P, 2, DM])
        xT_hi, xT_lo = (sb(n, [P, 2, KC, P], F32R) for n in ("xT_hi", "xT_lo"))
        junk = sb("junk", [P, DM])
        ss, ms, rstd = (sb(n, [P, 2]) for n in ("ss", "ms", "rstd"))
        half = sb("half", [P, 16])
        p_x = [ps(f"x{i}") for i in range(2)]
        p_pj = [ps(f"pj{i}") for i in range(NB)]
        s_c, s_half, s_zero = sem("const_in"), sem("half_set"), sem("pad_zeroed")
        s_w = [sem(f"w_in{k}") for k in range(2)]
        s_whi, s_wlo = sem("w_hi"), sem("w_lo")
        s_x = [sem(f"x_in{p}") for p in range(2)]
        s_xp, s_xhi, s_xlo = sem("x_turned"), sem("xT_hi"), sem("xT_lo")
        s_ss, s_ms, s_rs = sem("squares_summed"), sem("mean_square"), sem("rstd_ready")
        s_pj = [sem(f"projected{n}") for n in range(NB)]
        s_ev = [sem(f"block_out{n}") for n in range(NB)]
        s_go_on, s_sp = sem("pool_waits_settled"), sem("sync_waits_settled")

        def const(name):
            a, b = cat[name]
            return io["consts"][:, a:b]

        singles = [(ident[:, :], const("ident")),
                   (g_in[:, :], io["norm_even"].rearrange("o (k p) -> p (o k)", p=P))]
        if heads:
            g_qk = sb("g_qk", [P, 2, HD])
            qk, qkn = (sb(n, [P, 2 * W0]) for n in ("qk", "qkn"))
            hss, hms, hr = (sb(n, [P, 16]) for n in ("hss", "hms", "hr"))
            v = sb("v", [P, 2, W0])
            qT, kT = (sb(n, [P, 4, P]) for n in ("qT", "kT"))
            p_q, p_k = ps("q"), ps("k")
            s_sq, s_hs, s_hm, s_hr = sem("head_squares"), sem("head_sums"), sem("head_means"), sem("head_rstd")
            s_qk1, s_qkn = sem("qk_scaled"), sem("qk_normed")
            s_qt, s_kt, s_qT, s_kT = sem("q_turned"), sem("k_turned"), sem("qT_ready"), sem("kT_ready")
            s_ko, s_qo, s_kTo = sem("k_stored"), sem("q_stored"), sem("kT_stored")
            s_vo = [sem(f"v_stored{i}") for i in range(2)]
            singles += [(g_qk[:, 0], io["q_norm"].to_broadcast([P, HD])),
                        (g_qk[:, 1], io["k_norm"].to_broadcast([P, HD]))]
        else:
            w_pool = sb("w_pool", [P, NG, P])
            scale = sb("scale", [P, NG * P])
            bands = {n: sb(n, [P, NG, P]) for n in ("band_first", "band", "band_prev", "band_samp", "band_buf")}
            buf_in = sb("buf_in", [P, W0])
            u = sb("u", [P, 2, W0])
            gate = sb("gate", [P, 2, DM])
            dT = sb("dT", [P, NG, P])
            mix = sb("mix", [P, W0])
            p_d, p_m = ps("d"), ps("m")
            s_wp, s_d, s_dT, s_y, s_mix = (sem(n) for n in ("w_pool_scaled", "pooled", "dT_ready", "pool_out", "mix_ready"))
            s_mo, s_uo = sem("mix_stored"), sem("u_stored")
            s_go = [sem(f"gate_stored{i}") for i in range(2)]
            singles += [(scale[:, :], io["pool_scale"].to_broadcast([P, NG * P])),
                        (w_pool[:, :, :], io["w_pool"].rearrange("o g c d -> c (o g) d")),
                        (buf_in[0:DB * BUF, :], io["cache_pool"].rearrange("o b r c -> (o b r) c"))]
            singles += [(bands[n][:, :, :], const(n).rearrange("p (g i) -> p g i", g=NG)) for n in bands]
        n_c = 16 * len(singles)
        block = st.block()

        @block.sync
        def _(sp):
            def load_x(t, slot, samples=False):
                if samples:
                    sp.wait_ge(s_zero, 1)
                    sp.dma_start(x[0:NS, slot, :], io["x_sample"].rearrange("b t d -> (b t) d")).then_inc(s_x[slot], 16)
                else:
                    sp.dma_start(x[:, slot, :], io["x_prompt"][0, bass.ds(t * P, P), :]).then_inc(s_x[slot], 16)

            load_x(0, 0)
            load_all(sp, s_c, singles[:2])
            for k in range(KC):
                if k >= 2:
                    sp.wait_ge(s_wlo, k - 1)
                rows = io["w_in_even"][0, k * P:(k + 1) * P, :]
                if heads:
                    sp.dma_start(w_raw[:, k % 2, :, :].rearrange("p n c -> p (n c)"), rows[:, cols[0]:cols[0] + NB * W0]).then_inc(
                        s_w[k % 2], 16)
                else:
                    sp.dma_start(w_raw[:, k % 2, 0, :], rows[:, 0:W0]).then_inc(s_w[k % 2], 16)
                    sp.dma_start(w_raw[:, k % 2, 1:NB, :].rearrange("p n c -> p (n c)"), rows[:, cols[1]:cols[1] + 2 * W0]).then_inc(
                        s_w[k % 2], 16)
                if k == 1:
                    load_x(1, 1)
            load_all(sp, s_c, singles[2:])

            def body(t, slot, nth):
                last = isinstance(t, int) and t == NT
                n = NS if last else P
                row0 = 0 if last else t * P
                if not (isinstance(t, int) and t >= NT - 1):
                    sp.wait_ge(s_xp, t + 1)
                    sp.wait_ge(s_ss, t + 1)
                    settle(sp, s_sp)
                    load_x(t + 2, slot, samples=isinstance(t, int) and t == NT - 2)
                if heads:
                    k_out, v_out = (io[a].rearrange("o b t h d -> (o b t) (h d)")
                                    for a in (("k_sample", "v_sample") if last else ("k_prompt", "v_prompt")))
                    sp.wait_ge(s_ev[2], t + 1)
                    settle(sp, s_sp)
                    sp.dma_start(v_out[bass.ds(row0, n), :], v[0:n, slot, :]).then_inc(s_vo[slot], 16)
                    sp.wait_ge(s_qkn, t + 1)
                    settle(sp, s_sp)
                    sp.dma_start(k_out[bass.ds(row0, n), :], qkn[0:n, W0:2 * W0]).then_inc(s_ko, 16)
                else:
                    if isinstance(t, int) and t >= NT - 1:
                        sp.wait_ge(s_ev[0], t + 1)
                        if last:
                            for b in range(DB):
                                sp.dma_start(io["pool_sample"][0, b, BUF - DS:BUF, :],
                                             u[b * DS:(b + 1) * DS, slot, :]).then_inc(s_uo, 16)
                        else:
                            sp.dma_start(io["pool_prompt"][0, 0, :, :], u[P - BUF:P, slot, :]).then_inc(s_uo, 16)
                    sp.wait_ge(s_ev[2], t + 1)
                    settle(sp, s_sp)
                    sp.dma_start(io["mixgate"][bass.ds(t, 1), :, W0:DM].rearrange("o p n -> p (o n)"),
                                 gate[:, slot, W0:DM]).then_inc(s_go[slot], 16)
                if not (isinstance(t, int) and t == 0):
                    post(t - 1)

            def post(t):
                sp.wait_ge(s_qT if heads else s_mix, t + 1)
                settle(sp, s_sp)
                if heads:
                    sp.dma_start(io["q_turned"][bass.ds(t * 4, 4), :, :].rearrange("q p n -> p q n"),
                                 qT[:, :, :]).then_inc(s_qo, 16)
                    sp.wait_ge(s_kT, t + 1)
                    settle(sp, s_sp)
                    sp.dma_start(io["k_turned"][:, :, bass.ds(t * P, P)], kT[:, :, :]).then_inc(s_kTo, 16)
                else:
                    sp.dma_start(io["mixgate"][bass.ds(t, 1), :, 0:W0].rearrange("o p n -> p (o n)"),
                                 mix[:, :]).then_inc(s_mo, 16)

            tiles(sp, body)
            post(NT)
            if not heads:
                for b in range(DB):
                    sp.dma_start(io["pool_sample"][0, b, 0:BUF - DS, :], io["cache_pool"][0, b, DS:BUF, :]).then_inc(s_uo, 16)
                sp.wait_ge(s_uo, 16 * (2 * DB + 1))
                sp.wait_ge(s_mo, 16 * (NT + 1))
            else:
                sp.wait_ge(s_ko, 16 * (NT + 1))
                sp.wait_ge(s_qo, 16 * (NT + 1))
                sp.wait_ge(s_kTo, 16 * (NT + 1))
            for slot, s in enumerate(s_vo if heads else s_go):
                sp.wait_ge(s, 16 * (NT // 2 + 1 - slot))

        @block.tensor
        def _(pe):
            def turn_x(t, slot, nth):
                pe.wait_ge(s_x[slot], nth * 16 + 16)
                at_least(pe, s_xlo, t * 2)
                for k in range(KC):
                    mm = pe.transpose(p_x[k // 4][:, k % 4 * P:(k % 4 + 1) * P], x[:, slot, k * P:(k + 1) * P],
                                      ident[:, :])
                mm.then_inc(s_xp, 1)

            def pooled(t, slot, kind):
                pe.wait_ge(s_ev[0], t + 1)
                at_least(pe, s_dT, t)
                band = bands[{"first": "band_first", "samples": "band_samp"}.get(kind, "band")]
                for g in range(NG):
                    out = p_d[:, g * P:(g + 1) * P]
                    mm = pe.matmul(out, u[:, slot, g * P:(g + 1) * P], band[:, g, :], start=True, stop=(kind == "first"))
                    if kind == "samples":
                        n = DB * BUF
                        mm = pe.matmul(out, buf_in[0:n, g * P:(g + 1) * P], bands["band_buf"][0:n, g, :], start=False,
                                       stop=True)
                    elif kind != "first":
                        mm = pe.matmul(out, u[:, 1 - slot, g * P:(g + 1) * P], bands["band_prev"][:, g, :], start=False,
                                       stop=True)
                mm.then_inc(s_d, 1)

            def mixed(t):
                pe.wait_ge(s_dT, t + 1)
                at_least(pe, s_mix, t)
                for g in range(NG):
                    mm = pe.matmul(p_m[:, g * P:(g + 1) * P], dT[:, g, :], w_pool[:, g, :], start=True, stop=True)
                mm.then_inc(s_y, 1)

            def turn_qk(t):
                pe.wait_ge(s_qkn, t + 1)
                for bank, at, copied, s in ((p_q, 0, s_qT, s_qt), (p_k, W0, s_kT, s_kt)):
                    at_least(pe, copied, t)
                    for q in range(4):
                        mm = pe.transpose(bank[:, q * P:(q + 1) * P], qkn[:, at + q * P:at + (q + 1) * P], ident[:, :])
                    mm.then_inc(s, 1)

            def body(t, slot, nth):
                first = isinstance(t, int) and t == 0
                if first:
                    pe.wait_ge(s_c, 32)
                    turn_x(0, 0, 0)
                if not (isinstance(t, int) and t == NT):
                    turn_x(t + 1, 1 - slot, nth + slot)
                if not heads and not first:
                    if isinstance(t, int) and t == 1:
                        pe.wait_ge(s_c, n_c)
                        pe.wait_ge(s_wp, 1)
                    pooled(t - 1, 1 - slot, "first" if isinstance(t, int) and t == 1 else "mid")
                pe.wait_ge(s_xlo, t * 2 + 2)
                for n in range(NB):
                    at_least(pe, s_ev[n], t)
                    for k in range(KC):
                        if first and n == 0:
                            pe.wait_ge(s_wlo, k + 1)
                        out = p_pj[n][:, :]
                        pe.matmul(out, xT_hi[:, slot, k, :], w_hi[:, k, n, :], start=(k == 0), stop=False)
                        pe.matmul(out, xT_hi[:, slot, k, :], w_lo[:, k, n, :], start=False, stop=False)
                        mm = pe.matmul(out, xT_lo[:, slot, k, :], w_hi[:, k, n, :], start=False, stop=(k == KC - 1))
                    mm.then_inc(s_pj[n], 1)
                if not first:
                    turn_qk(t - 1) if heads else mixed(t - 1)

            tiles(pe, body)
            if heads:
                turn_qk(NT)
            else:
                pooled(NT, 0, "samples")
                mixed(NT)

        @block.vector
        def _(dve):
            def split_x(t, slot):
                dve.wait_ge(s_xhi, t * 2 + 2)
                at_least(dve, s_pj[NB - 1], t - 1)
                for hf in range(2):
                    dve.tensor_tensor(xT_lo[:, slot, 4 * hf:4 * hf + 4, :], p_x[hf][:, :].rearrange("p (k i) -> p k i", k=4),
                                      xT_hi[:, slot, 4 * hf:4 * hf + 4, :].bitcast(F32), ALU.subtract).then_inc(s_xlo, 1)

            def norm_qk(t):
                dve.wait_ge(s_ev[0], t + 1)
                dve.wait_ge(s_ev[1], t + 1)
                at_least(dve, s_ko, t * 16)
                at_least(dve, s_kt, t)
                dve.tensor_tensor(qkn[:, :], qk[:, :], qk[:, :], ALU.mult).then_inc(s_sq, 1)
                dve.wait_ge(s_sq, t + 1)
                dve.tensor_reduce(hss[:, :], qkn[:, :].rearrange("p (h d) -> p h d", d=HD), AX.X,
                                  ALU.add).then_inc(s_hs, 1)
                dve.wait_ge(s_hr, t + 1)
                dve.wait_ge(s_hs, t + 1)
                dve.tensor_tensor(qkn[:, :].rearrange("p (h d) -> p h d", d=HD),
                                  qk[:, :].rearrange("p (h d) -> p h d", d=HD),
                                  hr[:, :].unsqueeze(2).to_broadcast([P, 16, HD]), ALU.mult).then_inc(s_qk1, 1)
                dve.wait_ge(s_qk1, t + 1)
                q4 = qkn[:, :].rearrange("p (a h d) -> p a h d", a=2, d=HD)
                dve.tensor_tensor(q4, q4, g_qk[:, :, :].unsqueeze(2).to_broadcast([P, 2, H0, HD]),
                                  ALU.mult).then_inc(s_qkn, 1)

            def pool_out(t, slot):
                dve.wait_ge(s_y, t + 1)
                dve.wait_ge(s_ev[1], t + 1)
                at_least(dve, s_mo, t * 16)
                dve.tensor_tensor(mix[:, :], p_m[:, :], gate[:, slot, 0:W0], ALU.mult).then_inc(s_mix, 1)

            def pool_d(t):
                dve.wait_ge(s_d, t + 1)
                at_least(dve, s_y, t)
                dve.tensor_copy(dT[:, :, :], p_d[:, :].rearrange("p (g i) -> p g i", g=NG)).then_inc(s_dT, 1)

            def body(t, slot, nth):
                first = isinstance(t, int) and t == 0
                if first:
                    split_x(0, 0)
                    dve.wait_ge(s_c, 32)
                    for k in range(KC):
                        dve.wait_ge(s_whi, k + 1)
                        dve.scalar_tensor_tensor(w_lo[:, k, :, :], w_raw[:, k % 2, :, :], g_in[:, k:k + 1],
                                                 w_hi[:, k, :, :].bitcast(F32), ALU.mult, ALU.subtract).then_inc(s_wlo, 1)
                    dve.wait_ge(s_c, n_c)
                    if not heads:
                        dve.tensor_tensor(w_pool[:, :, :], w_pool[:, :, :], scale[:, :].rearrange("p (g i) -> p g i", g=NG),
                                          ALU.mult).then_inc(s_wp, 1)
                if not (isinstance(t, int) and t == NT):
                    split_x(t + 1, 1 - slot)
                if heads:
                    norm_qk(t)
                elif not first:
                    pool_d(t - 1)
                    pool_out(t - 1, 1 - slot)

            tiles(dve, body)
            if not heads:
                pool_d(NT)
                pool_out(NT, 0)

        @block.scalar
        def _(act):
            def square(t, slot, nth):
                act.wait_ge(s_x[slot], nth * 16 + 16)
                at_least(act, s_ss, t)
                at_least(act, s_ms, t - 1)
                act.activation(junk[:, :], x[:, slot, :], ACT.Square, accum_out=ss[:, slot:slot + 1]).then_inc(s_ss, 1)

            def x_hi(t, slot):
                act.wait_ge(s_xp, t + 1)
                at_least(act, s_pj[NB - 1], t - 1)
                for hf in range(2):
                    act.activation(xT_hi[:, slot, 4 * hf:4 * hf + 4, :], p_x[hf][:, :].rearrange("p (k i) -> p k i", k=4),
                                   ACT.Copy).then_inc(s_xhi, 1)

            def copy_qk(t):
                act.wait_ge(s_qt, t + 1)
                at_least(act, s_qo, t * 16)
                act.activation(qT[:, :, :], p_q[:, :].rearrange("p (q i) -> p q i", q=4), ACT.Copy).then_inc(s_qT, 1)
                act.wait_ge(s_kt, t + 1)
                at_least(act, s_kTo, t * 16)
                act.activation(kT[:, :, :], p_k[:, :].rearrange("p (q i) -> p q i", q=4), ACT.Copy).then_inc(s_kT, 1)

            def body(t, slot, nth):
                first = isinstance(t, int) and t == 0
                if first:
                    square(0, 0, 0)
                    x_hi(0, 0)
                    act.wait_ge(s_c, 32)
                    for k in range(KC):
                        act.wait_ge(s_w[k % 2], (k // 2 + 1) * (16 if heads else 32))
                        act.activation(w_hi[:, k, :, :], w_raw[:, k % 2, :, :], ACT.Copy, scale=g_in[:, k:k + 1]).then_inc(s_whi, 1)
                if not (isinstance(t, int) and t == NT):
                    square(t + 1, 1 - slot, nth + slot)
                    x_hi(t + 1, 1 - slot)
                act.wait_ge(s_rs, t + 1)
                dst = [qk[:, 0:W0], qk[:, W0:2 * W0], v[:, slot, :]] if heads else [
                    u[:, slot, :], gate[:, slot, 0:W0], gate[:, slot, W0:DM]]
                for n in range(NB):
                    act.wait_ge(s_pj[n], t + 1)
                    if heads and n < 2:
                        at_least(act, s_qk1, t)
                    elif heads:
                        at_least(act, s_vo[slot], nth * 16)
                    elif n == 0:
                        at_least(act, s_d, t)
                    elif n == 1:
                        at_least(act, s_mix, t - 1)
                    else:
                        at_least(act, s_go[slot], nth * 16)
                    act.activation(dst[n], p_pj[n][:, :], ACT.Silu if not heads and n > 0 else ACT.Copy,
                                   scale=rstd[:, slot:slot + 1]).then_inc(s_ev[n], 1)
                if heads and not first:
                    copy_qk(t - 1)

            tiles(act, body)
            if heads:
                copy_qk(NT)

        @block.gpsimd
        def _(pool):
            pool.memset(half[:, :], -0.5).then_inc(s_half, 1)
            pool.wait_ge(s_half, 1)

            def norm(t, slot):
                pool.wait_ge(s_ss, t + 1)
                at_least(pool, s_ev[NB - 1], t - 1)
                settle(pool, s_go_on)
                pool.tensor_scalar(ms[:, slot:slot + 1], ss[:, slot:slot + 1], 1.0 / DM, EPS, ALU.mult,
                                   ALU.add).then_inc(s_ms, 1)
                pool.wait_ge(s_ms, t + 1)
                pool.tensor_tensor(rstd[:, slot:slot + 1], ms[:, slot:slot + 1], half[:, 0:1],
                                   ALU.pow).then_inc(s_rs, 1)

            def body(t, slot, nth):
                if isinstance(t, int) and t == 0:
                    norm(0, 0)
                if isinstance(t, int) and t == NT - 2:
                    pool.wait_ge(s_xp, NT - 1)
                    pool.wait_ge(s_ss, NT - 1)
                    pool.memset(x[:, 0, :], 0.0).then_inc(s_zero, 1)
                if not (isinstance(t, int) and t == NT):
                    norm(t + 1, 1 - slot)
                if heads:
                    pool.wait_ge(s_hs, t + 1)
                    at_least(pool, s_qk1, t)
                    settle(pool, s_go_on)
                    pool.tensor_scalar(hms[:, :], hss[:, :], 1.0 / HD, EPS, ALU.mult, ALU.add).then_inc(s_hm, 1)
                    pool.wait_ge(s_hm, t + 1)
                    pool.tensor_tensor(hr[:, :], hms[:, :], half[:, :], ALU.pow).then_inc(s_hr, 1)

            tiles(pool, body)


def stage_b(nc, io, cat, o_all):
    with Stage(nc, "B") as st:
        sb, ps, sem = st.sb, st.ps, st.sem
        KB = 4
        RING = 4
        v_all = sb("v", [P, NT, W0])
        ident = sb("ident", [P, P])
        ident_b = sb("ident_b", [P, P], BF16)
        mask_f = sb("mask_f", [P, 7 * P])
        mask = sb("mask", [P, 7 * P], BF16)
        bias = sb("bias", [P, 2, H0])
        qz = sb("qz", [P, 2, 4, 2, P])
        q_hi, q_lo = (sb(n, [P, 2, 4, 2, P], F32R) for n in ("q_hi", "q_lo"))
        k_hi, k_lo = (sb(n, [P, 4, SEQ], F32R) for n in ("k_hi", "k_lo"))
        keep = sb("keep", [P, RING, KB * P])
        take = sb("take", [P, RING, KB * P])
        left = sb("left", [P, 2, NT * P + 1])
        a = sb("a", [P, 2, KB * P])
        aT = sb("aT", [P, 2, KB, P])
        p_z = [ps(f"z{i}") for i in range(RING)]
        p_a = [ps(f"a{i}") for i in range(2)]
        p_o = [ps(f"o{i}") for i in range(2)]
        s_in, s_set, s_cast = sem("loaded"), sem("set"), sem("cast")
        s_q = [sem(f"q_in{s}") for s in range(2)]
        s_k = [sem(f"k_in{kb}") for kb in range(NT // KB)]
        s_v = [sem(f"v_in{kb}") for kb in range(NT // KB)]
        s_qhi, s_qlo, s_khi, s_klo = (sem(n) for n in ("q_hi", "q_lo", "k_hi", "k_lo"))
        s_z, s_keep, s_take, s_scan, s_a = (sem(n) for n in ("scored", "keep", "take", "scanned", "weighed"))
        s_at, s_aT, s_av, s_o = (sem(n) for n in ("a_turned", "aT_ready", "a_times_v", "o_ready"))
        block = st.block()
        END = NT * P
        SPLITS = {(0, 8): 1, (0, 12): 2, (2, 8): 3}

        def const(name):
            return io["consts"][:, cat[name][0]:cat[name][1]]

        loads = [(ident[:, :], const("ident")), (mask_f[:, :], const("mask_q")),
                 (bias[:, 0, :], io["sb_bias"].to_broadcast([P, H0]))]

        def bodies(eng, body):
            body(0, 0, 1)
            body(2, 1, 1)
            for c in range(2, 5):
                with eng.Fori(0, 2) as i:
                    body(i * 2 + 4 * (c - 1), i + 2 * (c - 1), c)

        def block_list(t, c):
            base = sum(32 * k for k in range(1, c))
            n0 = (t - 4 * (c - 1)) * 8 * c + base
            return n0, [(s, h, j) for s in range(2) for h in range(H0) for j in range(c)]

        @block.sync
        def _(sp):
            def load_k(kb):
                keys = slice(kb * KB * P, (kb + 1) * KB * P)
                sp.dma_start(k_lo[:, :, keys].bitcast(F32), io["k_turned"][:, :, keys]).then_inc(s_k[kb], 16)

            load_k(0)
            load_all(sp, s_in, loads)
            sp.wait_ge(s_set, 2)

            def body(t, nth, c):
                for s in range(2):
                    at_least(sp, s_o, t * 8 + 8 * (s - 1))
                    for hh in range(2):
                        sp.dma_start(qz[64 * hh:64 * hh + 64, s, :, hh, :],
                                     io["q_turned"][bass.ds(t * 4 + 4 * s, 4), 64 * hh:64 * hh + 64, :].rearrange(
                                         "q p n -> p q n")).then_inc(s_q[s], 16)
                if isinstance(t, int) and t == 0:
                    for kb in range(NT // KB):
                        if kb > 0:
                            load_k(kb)
                        sp.dma_start(v_all[:, kb * KB:(kb + 1) * KB, :],
                                     io["v_prompt"].rearrange("o b (t p) h d -> p (o b t) (h d)", p=P)[
                                         :, kb * KB:(kb + 1) * KB, :]).then_inc(s_v[kb], 16)

            bodies(sp, body)

        @block.tensor
        def _(pe):
            pe.wait_ge(s_in, 16 * len(loads))
            pe.wait_ge(s_cast, 2)

            def body(t, nth, c):
                n0, blocks = block_list(t, c)
                pe.wait_ge(s_klo, c)
                for kb in range(c):
                    pe.wait_ge(s_v[kb], 16)
                for m in range(len(blocks) + 4):
                    if m < len(blocks):
                        s, h, j = blocks[m]
                        if h == 0 and j == 0:
                            pe.wait_ge(s_qlo, t + (s + 1))
                        at_least(pe, s_take, n0 + (m - 3))
                        kb = c - 1 - j
                        keys = slice(kb * KB * P, (kb + 1) * KB * P)
                        qh, ql = (q[:, s, h // 2, h % 2, :] for q in (q_hi, q_lo))
                        kh, kl = k_hi[:, h // 2, keys], k_lo[:, h // 2, keys]
                        pe.matmul(p_z[m % RING][:, :], qh, kh, start=True, stop=False)
                        pe.matmul(p_z[m % RING][:, :], qh, kl, start=False, stop=False)
                        mm = pe.matmul(p_z[m % RING][:, :], ql, kh, start=False, stop=(j > 0))
                        if j == 0:
                            off = (t - 4 * (c - 1)) * -P + (3 - s) * P
                            mm = pe.matmul(p_z[m % RING][:, :], ident_b[:, :], mask[:, bass.ds(off, KB * P)],
                                           start=False, stop=True)
                        mm.then_inc(s_z, 1)
                    if 3 <= m < len(blocks) + 3:
                        k = m - 3
                        pe.wait_ge(s_a, n0 + (k + 1))
                        at_least(pe, s_aT, n0 + (k - 1))
                        for q in range(KB):
                            mm = pe.transpose(p_a[k % 2][:, q * P:(q + 1) * P], a[:, k % 2, q * P:(q + 1) * P],
                                              ident[:, :])
                        mm.then_inc(s_at, 1)
                    if m >= 4:
                        k = m - 4
                        s, h, j = blocks[k]
                        pe.wait_ge(s_aT, n0 + (k + 1))
                        if j == 0:
                            at_least(pe, s_o, t * 8 + (8 * s + h - 1))
                        kb = c - 1 - j
                        for q in range(KB):
                            mm = pe.matmul(p_o[h % 2][:, 0:HD], aT[:, k % 2, q, :],
                                           v_all[:, kb * KB + q, h * HD:(h + 1) * HD],
                                           start=(j == 0 and q == 0), stop=(j == c - 1 and q == KB - 1))
                        mm.then_inc(s_av, 1)

            bodies(pe, body)

        @block.scalar
        def _(act):
            act.wait_ge(s_cast, 3)
            act.wait_ge(s_set, 2)

            def split_k(kb):
                keys = slice(kb * KB * P, (kb + 1) * KB * P)
                act.wait_ge(s_k[kb], 16)
                act.activation(k_hi[:, :, keys], k_lo[:, :, keys].bitcast(F32), ACT.Copy).then_inc(s_khi, 1)

            def split_q(t, s, nth):
                act.wait_ge(s_q[s], nth * 32 + 32)
                act.activation(q_hi[:, s, :, :, :], qz[:, s, :, :, :], ACT.Copy).then_inc(s_qhi, 1)

            split_k(0)

            def body(t, nth, c):
                n0, blocks = block_list(t, c)
                split_q(t, 0, nth)
                for m in range(len(blocks) + 3):
                    if isinstance(t, int) and (t, m) in SPLITS:
                        split_k(SPLITS[t, m])
                    if m == 4 * c:
                        split_q(t, 1, nth)
                    if m < len(blocks):
                        s, h, j = blocks[m]
                        act.wait_ge(s_z, n0 + (m + 1))
                        at_least(act, s_scan, n0 + (m - 3))
                        act.activation(keep[:, m % RING, :], p_z[m % RING][:, :], ACT.Sigmoid,
                                       scale=-(HD ** -0.5), bias=bias[:, 1, h:h + 1]).then_inc(s_keep, 1)
                        at_least(act, s_a, n0 + (m - 3))
                        act.activation(take[:, m % RING, :], p_z[m % RING][:, :], ACT.Sigmoid,
                                       scale=HD ** -0.5, bias=bias[:, 0, h:h + 1]).then_inc(s_take, 1)
                    if m >= 3:
                        k = m - 3
                        act.wait_ge(s_at, n0 + (k + 1))
                        at_least(act, s_av, n0 + (k - 1))
                        act.activation(aT[:, k % 2, :, :], p_a[k % 2][:, :].rearrange("p (q i) -> p q i", q=KB),
                                       ACT.Copy).then_inc(s_aT, 1)

            bodies(act, body)

        @block.vector
        def _(dve):
            dve.wait_ge(s_in, 16 * len(loads))
            dve.tensor_copy(ident_b[:, :], ident[:, :]).then_inc(s_cast, 1)
            dve.tensor_copy(mask[:, :], mask_f[:, :]).then_inc(s_cast, 1)
            dve.tensor_scalar(bias[:, 1, :], bias[:, 0, :], -1.0, None, ALU.mult).then_inc(s_cast, 1)
            dve.wait_ge(s_set, 2)

            def split_k(kb):
                keys = slice(kb * KB * P, (kb + 1) * KB * P)
                dve.wait_ge(s_khi, kb + 1)
                dve.tensor_tensor(k_lo[:, :, keys], k_lo[:, :, keys].bitcast(F32), k_hi[:, :, keys].bitcast(F32),
                                  ALU.subtract).then_inc(s_klo, 1)

            def split_q(t, s, nth):
                dve.wait_ge(s_qhi, t + (s + 1))
                dve.wait_ge(s_q[s], nth * 32 + 32)
                dve.tensor_tensor(q_lo[:, s, :, :, :], qz[:, s, :, :, :], q_hi[:, s, :, :, :].bitcast(F32),
                                  ALU.subtract).then_inc(s_qlo, 1)

            split_k(0)

            def body(t, nth, c):
                n0, blocks = block_list(t, c)
                split_q(t, 0, nth)

                def out(k):
                    s, h, j = blocks[k]
                    if j == c - 1:
                        dve.wait_ge(s_av, n0 + (k + 1))
                        dve.tensor_copy(o_all[:, bass.ds(t + s, 1), h * HD:(h + 1) * HD].rearrange(
                            "p o d -> p (o d)"), p_o[h % 2][:, 0:HD]).then_inc(s_o, 1)

                for m in range(len(blocks)):
                    if isinstance(t, int) and (t, m) in SPLITS:
                        split_k(SPLITS[t, m])
                    if m == 4 * c:
                        split_q(t, 1, nth)
                    s, h, j = blocks[m]
                    lo = END - (j + 1) * KB * P
                    buf = left[:, h % 2, :]
                    dve.wait_ge(s_keep, n0 + (m + 1))
                    at_least(dve, s_a, n0 + m)
                    dve.tensor_tensor_scan(buf[:, lo:lo + KB * P][:, ::-1], keep[:, m % RING, ::-1],
                                           keep[:, m % RING, ::-1], buf[:, lo + KB * P:lo + KB * P + 1],
                                           ALU.mult, ALU.bypass).then_inc(s_scan, 1)
                    dve.wait_ge(s_scan, n0 + (m + 1))
                    dve.wait_ge(s_take, n0 + (m + 1))
                    at_least(dve, s_at, n0 + (m - 1))
                    dve.tensor_tensor(a[:, m % 2, :], take[:, m % RING, :], buf[:, lo + 1:lo + 1 + KB * P],
                                      ALU.mult).then_inc(s_a, 1)
                    if m >= 5:
                        out(m - 5)
                for k in range(len(blocks) - 5, len(blocks)):
                    out(k)

            bodies(dve, body)

        @block.gpsimd
        def _(pool):
            pool.memset(qz[:, :, :, :, :], 0.0).then_inc(s_set, 1)
            pool.memset(left[:, :, END:END + 1], 1.0).then_inc(s_set, 1)


def stage_s(nc, io, cat, o_all):
    with Stage(nc, "S") as st:
        sb, ps, sem = st.sb, st.ps, st.sem
        GB = 4
        GROUPS = DB // GB
        RING = 8
        NK = PAST + NS
        PB = 4
        JB = NPG // PB
        n_phys = io["cache_k"].shape[1]
        table = sb("table", [1, DB * NPG], I32)
        ident = sb("ident", [P, P])
        mask_new = sb("mask_new", [P, GROUPS * NS])
        own_head = sb("own_head", [P, W0])
        to_token = sb("to_token", [P, GROUPS * NS])
        row_head = sb("row_head", [P, P])
        bias_h = sb("bias_h", [H0, 1])
        bias = sb("bias", [P, 2])
        qT = sb("qT", [P, 4, NS])
        qz = sb("qz", [P, GB, 4, NS])
        v_new = sb("v_new", [NS, W0])
        k_new = sb("k_new", [P, 4, NS])
        kp = sb("kp", [P, RING, W0])
        vp = sb("vp", [P, RING, W0])
        kpT = sb("kpT", [P, 2, 4, P])
        keep = sb("keep", [P, NK])
        take = sb("take", [P, NK])
        z_new = sb("z_new", [P, NS])
        left = sb("left", [P, NK + 1])
        a = sb("a", [P, NK])
        aT = sb("aT", [P, NPG + 1, P])
        own = sb("own", [P, GROUPS, W0])
        p_t = [ps(f"t{i}") for i in range(2)]
        p_z, p_n, p_o, p_m = ps("z"), ps("n"), ps("o"), ps("m")
        p_a = [ps(f"a{i}") for i in range(2)]
        s_in, s_set, s_bias, s_b1, s_b2 = (sem(n) for n in ("loaded", "set", "bias_ps", "bias_neg", "bias_pos"))
        s_kp = [sem(f"k_page{i}") for i in range(RING)]
        s_vp = [sem(f"v_page{i}") for i in range(RING)]
        s_qz, s_tr, s_sc, s_nsc = (sem(n) for n in ("q_spread", "page_turned", "page_scored", "new_scored"))
        s_kT = [sem(f"kT_ready{i}") for i in range(2)]
        s_zn, s_keep, s_take, s_scan, s_a = (sem(n) for n in ("new_masked", "keep", "take", "scanned", "weighed"))
        s_at, s_aT, s_av, s_own, s_tok, s_out = (sem(n) for n in (
            "a_turned", "aT_ready", "a_times_v", "own_kept", "by_token", "o_written"))
        s_pe = sem("tensor_waits_settled")
        block = st.block()
        AT = NPG // 4 + 1

        def const(name):
            return io["consts"][:, cat[name][0]:cat[name][1]]

        loads = [(table[:, :], io["page_table"].rearrange("b n -> (b n)").unsqueeze(0)),
                 (ident[:, :], const("ident")), (mask_new[:, :], const("mask_new")),
                 (own_head[:, :], const("own_head")), (to_token[:, :], const("to_token")),
                 (row_head[:, :], const("row_head")), (bias_h[:, :], io["sb_bias"].rearrange("o h -> h o")),
                 (qT[:, :, :], io["q_turned"][4 * NT:4 * NT + 4, :, 0:NS].rearrange("q p n -> p q n")),
                 (k_new[:, :, :], io["k_turned"][:, :, NT * P:NT * P + NS]),
                 (v_new[:, :], io["v_sample"].rearrange("o b t h d -> (o b t) (h d)"))]

        def pages(eng, odd):
            def page(cache, ring, slot, s_page, g, bb, j):
                phys = eng.value_load(table[0:1, bass.ds(g * (GB * NPG) + j + bb * NPG, 1)], min_val=0, max_val=n_phys - 1)
                eng.dma_start(ring[:, slot, :], io[cache][0, bass.ds(phys, 1), :, :, :].rearrange(
                    "o p h d -> p (o h d)")).then_inc(s_page, 16)

            for g in range(GROUPS):
                with eng.Fori(0, JB) as jb:
                    for m in range(odd, PB * GB, 2):
                        at_least(eng, s_tr, g * (NPG * GB) + jb * (PB * GB) + (m + 1))
                        page("cache_k", kp, m % RING, s_kp[m % RING], g, m % GB, jb * PB + m // GB)
                for m in range(odd, NPG * GB, 2):
                    if m >= RING:
                        at_least(eng, s_av, g * (NPG * GB + GB) + (m - RING + 1))
                    page("cache_v", vp, m % RING, s_vp[m % RING], g, m % GB, m // GB)

        @block.sync
        def _(sp):
            sp.wait_ge(s_in, load_all(sp, s_in, loads))
            pages(sp, 0)

        @block.tensor
        def _(pe):
            pe.wait_ge(s_in, 16 * len(loads))
            pe.matmul(p_m[:, 0:1], row_head[0:H0, :], bias_h[:, :], start=True, stop=True).then_inc(s_bias, 1)
            for g in range(GROUPS):
                at_least(pe, s_qz, g * 8 + 8)
                settle(pe, s_pe)
                with pe.Fori(0, JB) as jb:
                    n0 = g * (NPG * GB) + jb * (PB * GB)
                    for m in range(PB * GB + 1):
                        if m < PB * GB:
                            pe.wait_ge(s_kp[m % RING], (g * (NPG * GB) + jb * (PB * GB) + (m - m % RING)) * (16 // RING) + 16)
                            pe.wait_ge(s_kT[m % 2], g * (NPG * GB // 2) + jb * (PB * GB // 2) + (m // 2 + 1))
                            for q in range(4):
                                mm = pe.transpose(p_t[m % 2][:, q * P:(q + 1) * P], kp[:, m % RING, q * P:(q + 1) * P],
                                                  ident[:, :])
                            mm.then_inc(s_tr, 1)
                        if m >= 1:
                            k = m - 1
                            j, bb = k // GB, k % GB
                            pe.wait_ge(s_kT[k % 2], g * (NPG * GB // 2) + jb * (PB * GB // 2) + (k // 2 + 2))
                            if k == 0:
                                pe.wait_ge(s_take, g * (JB + 1) + jb + 1)
                            for q in range(4):
                                mm = pe.matmul(p_z[NS * bb:NS * bb + NS, j * P:(j + 1) * P], qz[:, bb, q, :],
                                               kpT[:, k % 2, q, :], start=(q == 0), stop=(q == 3))
                            mm.then_inc(s_sc, 1)
                for bb in range(GB):
                    for q in range(4):
                        mm = pe.matmul(p_n[NS * bb:NS * bb + NS, 0:NS], qz[:, bb, q, :], k_new[:, q, :],
                                       start=(q == 0), stop=(q == 3))
                mm.then_inc(s_nsc, 1)
                pe.wait_ge(s_a, g + 1)
                for k in range(AT):
                    at_least(pe, s_aT, g * AT + k - 1) if k >= 2 else pe.wait_ge(s_own, g)
                    if k < AT - 1:
                        for q in range(4):
                            c = (4 * k + q) * P
                            mm = pe.transpose(p_a[k % 2][:, q * P:(q + 1) * P], a[:, c:c + P], ident[:, :])
                    else:
                        mm = pe.transpose(p_a[k % 2][0:NS, 0:P], a[:, PAST:NK], ident[:, :])
                    mm.then_inc(s_at, 1)
                for m in range(NPG * GB):
                    j, bb = m // GB, m % GB
                    if m % (4 * GB) == 0:
                        at_least(pe, s_aT, g * AT + j // 4 + 1)
                    at_least(pe, s_vp[m % RING], g * (NPG * GB // RING * 16) + m // RING * 16 + 16)
                    pe.matmul(p_o[NS * bb:NS * bb + NS, :], aT[:, j, NS * bb:NS * bb + NS], vp[:, m % RING, :],
                              start=(j == 0), stop=False, skip_group_check=True).then_inc(s_av, 1)
                at_least(pe, s_aT, g * AT + AT)
                settle(pe, s_pe)
                for bb in range(GB):
                    pe.matmul(p_o[NS * bb:NS * bb + NS, :], aT[0:NS, NPG, NS * bb:NS * bb + NS], v_new[:, :],
                              start=False, stop=True, skip_group_check=True).then_inc(s_av, 1)
            pe.wait_ge(s_own, GROUPS)
            for g in range(GROUPS):
                mm = pe.matmul(p_m[0:NS, :], to_token[:, g * NS:(g + 1) * NS], own[:, g, :], start=(g == 0),
                               stop=(g == GROUPS - 1))
            mm.then_inc(s_tok, 1)

        @block.scalar
        def _(act):
            act.wait_ge(s_bias, 1)
            act.activation(bias[:, 0:1], p_m[:, 0:1], ACT.Copy).then_inc(s_b2, 1)
            act.activation(bias[:, 1:2], p_m[:, 0:1], ACT.Copy, scale=-1.0).then_inc(s_b2, 1)
            act.wait_ge(s_b2, 2)
            act.sem_inc(s_kT[0], 1)
            act.sem_inc(s_take, 1)

            def both(cols, src, free):
                at_least(act, s_scan, free)
                act.activation(keep[:, cols], src, ACT.Sigmoid, scale=-(HD ** -0.5), bias=bias[:, 1:2]).then_inc(s_keep, 1)
                at_least(act, s_a, free)
                act.activation(take[:, cols], src, ACT.Sigmoid, scale=HD ** -0.5, bias=bias[:, 0:1]).then_inc(s_take, 1)

            for g in range(GROUPS):
                with act.Fori(0, JB) as jb:
                    for m in range(0, PB * GB, 2):
                        at_least(act, s_tr, g * (NPG * GB) + jb * (PB * GB) + (RING + m + 1))
                        if m >= 2:
                            at_least(act, s_sc, g * (NPG * GB) + jb * (PB * GB) + (m - 1))
                        act.activation(kpT[:, 0, :, :], p_t[0][:, :].rearrange("p (q i) -> p q i", q=4),
                                       ACT.Copy).then_inc(s_kT[0], 1)
                    at_least(act, s_sc, g * (NPG * GB) + jb * (PB * GB) + PB * GB)
                    both(bass.ds(jb * (PB * P), PB * P), p_z[:, :], g)
                act.wait_ge(s_zn, g + 1)
                both(slice(PAST, NK), z_new[:, :], g)
                for k in range(AT):
                    at_least(act, s_at, g * AT + (k + 1))
                    at_least(act, s_av, g * (NPG * GB + GB))
                    if k < AT - 1:
                        act.activation(aT[:, 4 * k:4 * k + 4, :], p_a[k % 2][:, :].rearrange("p (q i) -> p q i", q=4),
                                       ACT.Copy).then_inc(s_aT, 1)
                    else:
                        act.activation(aT[0:NS, NPG, :], p_a[k % 2][0:NS, 0:P], ACT.Copy).then_inc(s_aT, 1)

        @block.vector
        def _(dve):
            dve.wait_ge(s_in, 16 * len(loads))
            dve.wait_ge(s_set, 2)
            dve.wait_ge(s_tr, RING)
            dve.sem_inc(s_kT[1], 1)
            for g in range(GROUPS):
                at_least(dve, s_nsc, g)
                for q in range(4):
                    for hh in range(2):
                        h = 2 * q + hh
                        rows = slice(64 * hh, 64 * hh + 64)
                        dve.tensor_copy(qz[rows, :, q, h * DS:(h + 1) * DS],
                                        qT[rows, q, bass.ds(g * (GB * DS), GB * DS)].rearrange(
                                            "p (b t) -> p b t", t=DS)).then_inc(s_qz, 1)
                with dve.Fori(0, JB) as jb:
                    for m in range(1, PB * GB, 2):
                        at_least(dve, s_tr, g * (NPG * GB) + jb * (PB * GB) + (RING + m + 1))
                        if m >= 3:
                            at_least(dve, s_sc, g * (NPG * GB) + jb * (PB * GB) + (m - 1))
                        dve.tensor_copy(kpT[:, 1, :, :], p_t[1][:, :].rearrange("p (q i) -> p q i", q=4)).then_inc(s_kT[1], 1)
                dve.wait_ge(s_nsc, g + 1)
                dve.wait_ge(s_take, g * (JB + 1) + 1)
                dve.tensor_tensor(z_new[:, :], p_n[:, 0:NS], mask_new[:, bass.ds(g * NS, NS)], ALU.add).then_inc(s_zn, 1)
                at_least(dve, s_keep, g * (JB + 1) + JB + 1)
                at_least(dve, s_a, g)
                dve.tensor_tensor_scan(left[:, 0:NK][:, ::-1], keep[:, ::-1], keep[:, ::-1], 1.0,
                                       ALU.mult, ALU.bypass).then_inc(s_scan, 1)
                dve.wait_ge(s_scan, g + 1)
                dve.wait_ge(s_take, g * (JB + 1) + JB + 2)
                at_least(dve, s_at, g * AT)
                dve.tensor_tensor(a[:, :], take[:, :], left[:, 1:NK + 1], ALU.mult).then_inc(s_a, 1)
                at_least(dve, s_av, g * (NPG * GB + GB) + NPG * GB + GB)
                dve.tensor_tensor(own[:, bass.ds(g, 1), :].rearrange("p o n -> p (o n)"), p_o[:, :], own_head[:, :],
                                  ALU.mult).then_inc(s_own, 1)
            dve.wait_ge(s_tok, 1)
            dve.tensor_copy(o_all[0:NS, NT, :], p_m[0:NS, :]).then_inc(s_out, 1)

        @block.gpsimd
        def _(pool):
            pool.memset(qz[:, :, :, :], 0.0).then_inc(s_tr, RING)
            pool.memset(left[:, NK:NK + 1], 1.0).then_inc(s_set, 1)
            pool.memset(o_all[:, NT, :], 0.0).then_inc(s_set, 1)
            pool.wait_ge(s_in, 16 * len(loads))
            pages(pool, 1)


def stage_c(nc, io, cat, o_all):
    with Stage(nc, "C") as st:
        sb, ps, sem = st.sb, st.ps, st.sem
        w_hi, w_lo = (sb(n, [P, KC, DM], F32R) for n in ("w_hi", "w_lo"))
        ident = sb("ident", [P, P])
        half = sb("half", [P, 1])
        mix = sb("mix", [P, 2, DM])
        x = sb("x", [P, 2, DM])
        mT_hi, mT_lo = (sb(n, [P, 2, KC, P], F32R) for n in ("mT_hi", "mT_lo"))
        h1 = sb("h1", [P, 2, DM])
        w_raw = h1
        xn = sb("xn", [P, DM])
        ss, ms, rstd = (sb(n, [P, 1]) for n in ("ss", "ms", "rstd"))
        xT = sb("xT", [P, KC, P])
        p_m = [ps(f"m{i}") for i in range(2)]
        p_y = [ps(f"y{i}") for i in range(2)]
        p_h = [ps(f"h{i}") for i in range(2)]
        s_in, s_half, s_zero = sem("loaded"), sem("half_set"), sem("pad_zeroed")
        s_w = [sem(f"w_in{i}") for i in range(2)]
        s_mix_in = [sem(f"mix_in{i}") for i in range(2)]
        s_x = [sem(f"x_in{i}") for i in range(2)]
        s_whi, s_wlo = sem("w_hi_ready"), sem("w_lo_ready")
        s_mix, s_mt, s_mhi, s_mlo, s_y = (sem(n) for n in ("mix_ready", "mix_turned", "mT_hi", "mT_lo", "projected"))
        s_h, s_ss, s_ms, s_rs = (sem(n) for n in ("h1_ready", "squares", "mean_square", "rstd"))
        s_ho = [sem(f"h1_stored{i}") for i in range(2)]
        s_xn, s_ht, s_xr, s_xo = (sem(n) for n in ("normed", "h1_turned", "xT_ready", "xT_stored"))
        s_sp, s_pool = sem("sync_waits_settled"), sem("pool_waits_settled")
        block = st.block()
        loads = [(ident[:, :], io["consts"][:, cat["ident"][0]:cat["ident"][1]])]

        @block.sync
        def _(sp):
            def load_mix(t, slot):
                sp.dma_start(mix[:, slot, :], io["mixgate"][bass.ds(t, 1), :, :].rearrange("o p n -> p (o n)")).then_inc(
                    s_mix_in[slot], 16)

            def load_x(t, slot):
                if isinstance(t, int) and t == NT:
                    sp.wait_ge(s_zero, 1)
                    sp.dma_start(x[0:NS, slot, :], io["x_sample"].rearrange("b t d -> (b t) d")).then_inc(s_x[slot], 16)
                else:
                    sp.dma_start(x[:, slot, :], io["x_prompt"][0, bass.ds(t * P, P), :]).then_inc(s_x[slot], 16)

            def post(t):
                sp.wait_ge(s_xr, t * 2 + 2)
                settle(sp, s_sp)
                sp.dma_start(io["xT"][:, :, bass.ds(t * P, P)], xT[:, :, :]).then_inc(s_xo, 16)

            load_mix(0, 0)
            load_all(sp, s_in, loads)
            for k in range(KC):
                if k >= 2:
                    sp.wait_ge(s_wlo, k - 1)
                sp.dma_start(w_raw[:, k % 2, :], io["w_out_even"][0, k * P:(k + 1) * P, :]).then_inc(s_w[k % 2], 16)
                if k == 1:
                    load_mix(1, 1)
                    load_x(0, 0)
                    load_x(1, 1)

            def body(t, slot, nth):
                more = not (isinstance(t, int) and t >= NT - 1)
                if more:
                    sp.wait_ge(s_mt, t + 1)
                    settle(sp, s_sp)
                    load_mix(t + 2, slot)
                sp.wait_ge(s_h, t * 2 + 2)
                settle(sp, s_sp)
                sp.dma_start(io["h1"][bass.ds(t, 1), :, :].rearrange("o p n -> p (o n)"), h1[:, slot, :]).then_inc(
                    s_ho[slot], 16)
                if more:
                    load_x(t + 2, slot)
                if not (isinstance(t, int) and t == 0):
                    post(t - 1)

            tiles(sp, body)
            post(NT)
            for slot, sem_o in enumerate(s_ho):
                sp.wait_ge(sem_o, 16 * (NT // 2 + 1 - slot))
            sp.wait_ge(s_xo, 16 * (NT + 1))

        @block.tensor
        def _(pe):
            def split(out, l_hi, l_lo, r_hi, r_lo, first, last):
                pe.matmul(out, l_hi, r_hi, start=first, stop=False)
                pe.matmul(out, l_hi, r_lo, start=False, stop=False)
                return pe.matmul(out, l_lo, r_hi, start=False, stop=last)

            def post(t):
                pe.wait_ge(s_xn, t + 1)
                at_least(pe, s_xr, t * 2)
                for k in range(KC):
                    mm = pe.transpose(p_h[k // 4][:, k % 4 * P:(k % 4 + 1) * P], xn[:, k * P:(k + 1) * P], ident[:, :])
                mm.then_inc(s_ht, 1)

            def turn_mix(t, slot):
                pe.wait_ge(s_mix, t + 1)
                at_least(pe, s_mlo, t * 2)
                for k in range(KC):
                    mm = pe.transpose(p_m[k // 4][:, k % 4 * P:(k % 4 + 1) * P], mix[:, slot, k * P:(k + 1) * P],
                                      ident[:, :])
                mm.then_inc(s_mt, 1)

            def body(t, slot, nth):
                first = isinstance(t, int) and t == 0
                if first:
                    pe.wait_ge(s_in, 16 * len(loads))
                    turn_mix(0, 0)
                if not (isinstance(t, int) and t == NT):
                    turn_mix(t + 1, 1 - slot)
                pe.wait_ge(s_mlo, t * 2 + 2)
                at_least(pe, s_h, t * 2)
                for n in range(2):
                    for k in range(KC):
                        if first and n == 0:
                            pe.wait_ge(s_wlo, k + 1)
                        mm = split(p_y[n][:, :], mT_hi[:, slot, k, :], mT_lo[:, slot, k, :], w_hi[:, k, n * 512:(n + 1) * 512],
                                   w_lo[:, k, n * 512:(n + 1) * 512], k == 0, k == KC - 1)
                    mm.then_inc(s_y, 1)
                if not first:
                    post(t - 1)

            tiles(pe, body)
            post(NT)

        @block.scalar
        def _(act):
            def post(t):
                act.wait_ge(s_ht, t + 1)
                at_least(act, s_xo, t * 16)
                for n in range(2):
                    act.activation(xT[:, 4 * n:4 * n + 4, :], p_h[n][:, :].rearrange("p (k i) -> p k i", k=4),
                                   ACT.Copy).then_inc(s_xr, 1)

            def m_hi(t, slot):
                act.wait_ge(s_mt, t + 1)
                at_least(act, s_y, t * 2 - 2)
                for n in range(2):
                    act.activation(mT_hi[:, slot, 4 * n:4 * n + 4, :], p_m[n][:, :].rearrange("p (k i) -> p k i", k=4),
                                   ACT.Copy).then_inc(s_mhi, 1)

            def body(t, slot, nth):
                first = isinstance(t, int) and t == 0
                if first:
                    m_hi(0, 0)
                    for k in range(KC):
                        act.wait_ge(s_w[k % 2], k // 2 * 16 + 16)
                        act.activation(w_hi[:, k, :], w_raw[:, k % 2, :], ACT.Copy).then_inc(s_whi, 1)
                if not (isinstance(t, int) and t == NT):
                    m_hi(t + 1, 1 - slot)
                if not first:
                    post(t - 1)
                act.wait_ge(s_h, t * 2 + 2)
                at_least(act, s_ms, t)
                at_least(act, s_ht, t)
                act.activation(xn[:, :], h1[:, slot, :], ACT.Square, accum_out=ss[:, :]).then_inc(s_ss, 1)
                act.wait_ge(s_ss, t + 1)
                act.wait_ge(s_rs, t + 1)
                act.activation(xn[:, :], h1[:, slot, :], ACT.Copy, scale=rstd[:, :]).then_inc(s_xn, 1)

            tiles(act, body)
            post(NT)

        @block.vector
        def _(dve):
            def gate_mix(t, slot, nth):
                dve.wait_ge(s_mix_in[slot], nth * 16 + 16)
                dve.tensor_tensor(mix[:, slot, W0:DM], mix[:, slot, W0:DM],
                                  o_all[:, bass.ds(t, 1), :].rearrange("p o n -> p (o n)"), ALU.mult).then_inc(s_mix, 1)

            def m_lo(t, slot):
                dve.wait_ge(s_mhi, t * 2 + 2)
                at_least(dve, s_y, t * 2 - 2)
                for n in range(2):
                    dve.tensor_tensor(mT_lo[:, slot, 4 * n:4 * n + 4, :], p_m[n][:, :].rearrange("p (k i) -> p k i", k=4),
                                      mT_hi[:, slot, 4 * n:4 * n + 4, :].bitcast(F32), ALU.subtract).then_inc(s_mlo, 1)

            def body(t, slot, nth):
                if isinstance(t, int) and t == 0:
                    gate_mix(0, 0, 0)
                    m_lo(0, 0)
                    gate_mix(1, 1, 0)
                    for k in range(KC):
                        dve.wait_ge(s_whi, k + 1)
                        dve.wait_ge(s_w[k % 2], k // 2 * 16 + 16)
                        dve.tensor_tensor(w_lo[:, k, :], w_raw[:, k % 2, :], w_hi[:, k, :].bitcast(F32),
                                          ALU.subtract).then_inc(s_wlo, 1)
                if not (isinstance(t, int) and t == NT):
                    m_lo(t + 1, 1 - slot)
                if not (isinstance(t, int) and t >= NT - 1):
                    gate_mix(t + 2, slot, nth + 1)
                dve.wait_ge(s_x[slot], nth * 16 + 16)
                at_least(dve, s_ho[slot], nth * 16)
                at_least(dve, s_xn, t - 1)
                for n in range(2):
                    dve.wait_ge(s_y, t * 2 + (n + 1))
                    dve.tensor_tensor(h1[:, slot, n * 512:(n + 1) * 512], p_y[n][:, :], x[:, slot, n * 512:(n + 1) * 512],
                                      ALU.add).then_inc(s_h, 1)

            tiles(dve, body)

        @block.gpsimd
        def _(pool):
            pool.memset(half[:, :], -0.5).then_inc(s_half, 1)
            pool.wait_ge(s_half, 1)

            def body(t, slot, nth):
                if isinstance(t, int) and t == NT - 1:
                    pool.wait_ge(s_h, 2 * (NT - 1))
                    pool.memset(x[:, 0, :], 0.0).then_inc(s_zero, 1)
                pool.wait_ge(s_ss, t + 1)
                at_least(pool, s_xn, t)
                settle(pool, s_pool)
                pool.tensor_scalar(ms[:, :], ss[:, :], 1.0 / DM, EPS, ALU.mult, ALU.add).then_inc(s_ms, 1)
                pool.wait_ge(s_ms, t + 1)
                pool.tensor_tensor(rstd[:, :], ms[:, :], half[:, :], ALU.pow).then_inc(s_rs, 1)

            tiles(pool, body)


def stage_g(nc, io, cat, ba, gd):
    with Stage(nc, "G") as st:
        sb, ps, sem = st.sb, st.ps, st.sem
        T = NT + 1
        consts = {n: sb(n, [P, P]) for n in ("tri", "tri_samp", "last_samp")}
        ones = sb("ones", [P, P])
        own = sb("own", [P, DB])
        rate, dt = sb("rate", [P, H1]), sb("dt", [P, H1])
        ident = sb("ident", [P, P])
        bt = sb("bt", [P, T, 2 * H1])
        y, e, sp_, g = (sb(n, [P, T, H1]) for n in ("y", "e", "sp", "g"))
        gb = sb("gb", [P, DB, H1])
        gap = sb("gap", [P, T, H1])
        p_c, p_t, p_b = ps("c"), ps("t"), ps("b")
        s_in, s_one = sem("loaded"), sem("ones_set")
        s_v, s_a, s_p = sem("vector_step"), sem("scalar_step"), sem("sums")
        s_bt, s_bc = sem("b_turned"), sem("b_by_token")
        block = st.block()
        loads = [(consts[n][:, :], io["consts"][:, cat[n][0]:cat[n][1]]) for n in consts]
        loads += [(ident[:, :], io["consts"][:, cat["ident"][0]:cat["ident"][1]]), (own[:, :], io["consts"][:, cat["own_batch"][0]:cat["own_batch"][1]]),
                  (rate[:, :], io["a_log"].to_broadcast([P, H1])), (dt[:, :], io["dt_bias"].to_broadcast([P, H1]))]
        n_in = 16 * len(loads)
        over = lambda v: v[:, :].unsqueeze(1).to_broadcast([P, T, H1])

        @block.sync
        def _(sp):
            load_all(sp, s_in, loads)

        @block.gpsimd
        def _(pool):
            pool.memset(ones[:, :], 1.0).then_inc(s_one, 1)
            pool.memset(bt[:, NT, :], 0.0).then_inc(s_one, 1)

        @block.vector
        def _(dve):
            dve.wait_ge(s_in, n_in)
            dve.wait_ge(s_bt, 1)
            dve.wait_ge(s_one, 2)
            n = NT * 2 * H1
            dve.tensor_copy(bt[:, 0:NT, :], p_b[:, 0:n].rearrange("p (t n) -> p t n", n=2 * H1))
            dve.tensor_copy(bt[0:NS, NT, :], p_b[0:NS, n:n + 2 * H1]).then_inc(s_bc, 1)
            dve.wait_ge(s_bc, 1)
            dve.tensor_tensor(y[:, :, :], bt[:, :, H1:2 * H1], over(dt), ALU.add).then_inc(s_v, 1)
            dve.wait_ge(s_v, 1)
            dve.tensor_scalar(sp_[:, :, :], y[:, :, :], 0.0, None, ALU.max).then_inc(s_v, 1)
            dve.wait_ge(s_a, 5)
            dve.wait_ge(s_v, 2)
            dve.tensor_tensor(sp_[:, :, :], sp_[:, :, :], e[:, :, :], ALU.add).then_inc(s_v, 1)
            dve.tensor_scalar(rate[:, :], rate[:, :], -1.0, None, ALU.mult).then_inc(s_v, 1)
            dve.wait_ge(s_v, 4)
            dve.tensor_tensor(g[:, :, :], sp_[:, :, :], over(rate), ALU.mult).then_inc(s_v, 1)
            dve.wait_ge(s_v, 5)
            dve.tensor_tensor(gb[:, :, :], g[:, NT, :].unsqueeze(1).to_broadcast([P, DB, H1]),
                              own[:, :].unsqueeze(2).to_broadcast([P, DB, H1]), ALU.mult).then_inc(s_v, 1)
            dve.wait_ge(s_p, 1)
            dve.tensor_copy(gd[:, 1, :, :], p_c[:, 0:T * H1].rearrange("p (t h) -> p t h", h=H1)).then_inc(s_v, 1)
            dve.wait_ge(s_v, 7)
            dve.wait_ge(s_p, 2)
            dve.tensor_tensor(gap[:, :, :], p_t[:, 0:T * H1].rearrange("p (t h) -> p t h", h=H1), gd[:, 1, :, :],
                              ALU.subtract).then_inc(s_v, 1)

        @block.scalar
        def _(act):
            act.wait_ge(s_bc, 1)
            act.activation(gd[:, 0, :, :], bt[:, :, 0:H1], ACT.Sigmoid).then_inc(s_a, 1)
            act.wait_ge(s_v, 1)
            act.activation(e[:, :, :], y[:, :, :], ACT.Abs).then_inc(s_a, 1)
            act.wait_ge(s_a, 2)
            act.activation(e[:, :, :], e[:, :, :], ACT.Exp, scale=-1.0).then_inc(s_a, 1)
            act.wait_ge(s_a, 3)
            act.wait_ge(s_one, 1)
            act.activation(e[:, :, :], e[:, :, :], ACT.Ln, bias=ones[:, 0:1]).then_inc(s_a, 1)
            act.wait_ge(s_in, n_in)
            act.activation(rate[:, :], rate[:, :], ACT.Exp).then_inc(s_a, 1)
            act.wait_ge(s_v, 8)
            act.activation(gd[:, 2, :, :], gd[:, 1, :, :], ACT.Exp).then_inc(s_a, 1)
            act.activation(gd[:, 3, :, :], gap[:, :, :], ACT.Exp).then_inc(s_a, 1)
            act.activation(gd[:, 4, :, :], p_t[:, 0:T * H1].rearrange("p (t h) -> p t h", h=H1), ACT.Exp).then_inc(s_a, 1)
            act.wait_ge(s_p, 3)
            act.activation(gd[:, 5, 0:DB, :], p_c[:, T * H1:(T + DB) * H1].rearrange("p (t h) -> p t h", h=H1),
                           ACT.Exp).then_inc(s_a, 1)

        @block.tensor
        def _(pe):
            pe.wait_ge(s_in, n_in)
            for t in range(T):
                n = P if t < NT else NS
                mm = pe.transpose(p_b[0:n, t * 2 * H1:(t + 1) * 2 * H1], ba[:, t * P:t * P + n], ident[0:2 * H1, 0:2 * H1])
            mm.then_inc(s_bt, 1)
            pe.wait_ge(s_v, 5)
            pe.wait_ge(s_one, 1)
            flat = g[:, :, :].rearrange("p t h -> p (t h)")
            n = NT * H1
            pe.matmul(p_c[:, 0:n], consts["tri"][:, :], flat[:, 0:n], start=True, stop=True)
            pe.matmul(p_c[:, n:n + H1], consts["tri_samp"][:, :], flat[:, n:n + H1], start=True, stop=True).then_inc(s_p, 1)
            pe.matmul(p_t[:, 0:n], ones[:, :], flat[:, 0:n], start=True, stop=True)
            pe.matmul(p_t[:, n:n + H1], consts["last_samp"][:, :], flat[:, n:n + H1], start=True, stop=True).then_inc(s_p, 1)
            pe.wait_ge(s_v, 7)
            pe.matmul(p_c[:, n + H1:n + H1 + DB * H1], ones[:, :], gb[:, :, :].rearrange("p b h -> p (b h)"),
                      start=True, stop=True).then_inc(s_p, 1)


def stage_d(nc, io, cat, ba):
    with Stage(nc, "D") as st:
        sb, ps, sem = st.sb, st.ps, st.sem
        NB = 5
        BT = (SEQ + NS) // NB
        LP = SEQ - (NB - 1) * BT
        NCV = CONV // P
        NST = NCV + H1
        TOK = SEQ + NS
        HB = DB * (CW - 1)
        xT_hi, xT_lo = (sb(n, [P, KC, TOK], F32R) for n in ("xT_hi", "xT_lo"))
        w_raw = sb("w_raw", [P, 2, KC, P])
        w_hi, w_lo = (sb(n, [P, 2, KC, P], F32R) for n in ("w_hi", "w_lo"))
        g_odd = sb("g_odd", [P, KC])
        ident = sb("ident", [P, P])
        ext = sb("ext", [P, 2, CW - 1 + SEQ])
        ext_s = sb("ext_s", [P, 2, DB, CW - 1 + DS])
        last_s = sb("last_s", [P, 2, HB])
        out = sb("out", [P, 2, TOK])
        taps = sb("taps", [P, NCV, CW])
        hist = sb("hist", [P, NCV, HB])
        tap = sb("tap", [P, 2, CW])
        rows_p = sb("rows_p", [CW - 1, P])
        rows_s = sb("rows_s", [HB, P])
        p_y = [ps(f"y{i}") for i in range(NB)]
        p_r = ps("r")
        s_in, s_set, s_pre, s_prc = sem("loaded"), sem("set"), sem("small_turned"), sem("small_out")
        s_xt = [sem(f"xT_in{i}") for i in range(NB)]
        s_w = [sem(f"w_in{i}") for i in range(2)]
        s_xhi, s_xlo = sem("xT_hi"), sem("xT_lo")
        s_wg, s_whi, s_wlo = sem("w_scaled"), sem("w_hi"), sem("w_lo")
        s_y = [sem(f"projected{i}") for i in range(NB)]
        s_ev = [sem(f"block_out{i}") for i in range(NB)]
        s_tap, s_cv, s_sl, s_r, s_ro = (sem(n) for n in ("tap_ready", "conv_step", "silu_done", "rows_turned", "rows_ready"))
        s_o = [sem(f"stored{i}") for i in range(2)]
        s_rs, s_last = sem("rows_stored"), sem("last_rows")
        block = st.block()
        STEPS = 2 * CW

        @block.sync
        def _(sp):
            sp.dma_start(g_odd[:, :], io["norm_odd"].rearrange("o (k p) -> p (o k)", p=P),
                         allow_slow_non_contiguous=True).then_inc(s_in, 16)
            sp.dma_start(ident[:, :], io["consts"][:, cat["ident"][0]:cat["ident"][1]]).then_inc(s_in, 16)
            sp.dma_start(out[0:CW, 0, 0:SEQ], io["conv_w"][0, :, 0:SEQ]).then_inc(s_in, 16)
            sp.dma_start(out[0:CW, 1, 0:CONV - SEQ], io["conv_w"][0, :, SEQ:CONV]).then_inc(s_in, 16)
            sp.dma_start(ext[0:HB, 0, 0:SEQ], io["state_conv"].rearrange("o b r c -> (o b r) c")[:, 0:SEQ]).then_inc(s_in, 16)
            sp.dma_start(ext[0:HB, 1, 0:CONV - SEQ], io["state_conv"].rearrange("o b r c -> (o b r) c")[:, SEQ:CONV]).then_inc(
                s_in, 16)

            def load_w(c, slot):
                sp.dma_start(w_raw[:, slot, :, :], io["w_in_odd"].rearrange("o (k p) n -> p (o k) n", p=P)[
                    :, :, bass.ds(c * P, P)]).then_inc(s_w[slot], 16)

            load_w(0, 0)
            load_w(1, 1)
            for n in range(NB):
                cols = slice(n * BT, (n + 1) * BT)
                sp.dma_start(xT_lo[:, :, cols].bitcast(F32), io["xT"][:, :, cols]).then_inc(s_xt[n], 16)

            def rows(c):
                sp.wait_ge(s_ro, c * 2 + 2)
                sp.dma_start(io["conv_prompt"][0, 0, :, bass.ds(c * P, P)], rows_p[:, :]).then_inc(s_rs, 16)
                sp.dma_start(io["conv_sample"].rearrange("o b r c -> (o b r) c")[:, bass.ds(c * P, P)],
                             rows_s[:, :]).then_inc(s_rs, 16)

            def body(c, slot, nth, more=True):
                if more:
                    sp.wait_ge(s_wlo, c + 1)
                    load_w(c + 2, slot)
                if isinstance(c, int) and (c == 0 or c > NCV):
                    pass
                else:
                    rows(c - 1)
                sp.wait_ge(s_sl, c + 1)
                sp.dma_start(io["strips"][bass.ds(c, 1), :, :].rearrange("o p n -> p (o n)"),
                             out[:, slot, :]).then_inc(s_o[slot], 16)

            body(0, 0, 0)
            body(1, 1, 0)
            with sp.Fori(1, NCV // 2) as i:
                body(i * 2, 0, i)
                body(i * 2 + 1, 1, i)
            for c in range(NCV, NST):
                body(c, c % 2, c // 2, more=c + 2 < NST)
                if c == NST - 2:
                    sp.wait_ge(s_wlo, NST - 1)
                    sp.dma_start(w_raw[:, 0, :, 0:2 * H1], io["w_in_odd"].rearrange("o (k p) n -> p (o k) n", p=P)[
                        :, :, ODD_IN - 2 * H1:ODD_IN]).then_inc(s_w[0], 16)
            for s in s_o:
                sp.wait_ge(s, 16 * NST // 2)
            sp.wait_ge(s_rs, 32 * NCV)

        @block.tensor
        def _(pe):
            pe.wait_ge(s_in, 16 * 6)
            for c in range(NCV):
                half, at = divmod(c * P, SEQ)
                mm = pe.transpose(p_r[:, c * CW:(c + 1) * CW], out[0:CW, half, at:at + P], ident[0:CW, 0:CW])
            mm.then_inc(s_pre, 1)
            for c in range(NCV):
                half, at = divmod(c * P, SEQ)
                mm = pe.transpose(p_y[c // 12][:, c % 12 * HB:(c % 12 + 1) * HB], ext[0:HB, half, at:at + P],
                                  ident[0:HB, 0:HB])
            mm.then_inc(s_pre, 1)
            pe.wait_ge(s_prc, 3)

            def body(c, slot, nth, first=False):
                pe.wait_ge(s_wlo, c + 1)
                for n in range(NB):
                    if first:
                        pe.wait_ge(s_xlo, n + 1)
                    at_least(pe, s_ev[n], c)
                    dst = p_y[n][:, 0:BT]
                    cols = slice(n * BT, (n + 1) * BT)
                    for k in range(KC):
                        pe.matmul(dst, w_hi[:, slot, k, :], xT_hi[:, k, cols], start=(k == 0), stop=False)
                        pe.matmul(dst, w_hi[:, slot, k, :], xT_lo[:, k, cols], start=False, stop=False)
                        mm = pe.matmul(dst, w_lo[:, slot, k, :], xT_hi[:, k, cols], start=False, stop=(k == KC - 1))
                    mm.then_inc(s_y[n], 1)
                if isinstance(c, int) and (c == 0 or c > NCV):
                    return
                pe.wait_ge(s_last, c)
                pe.wait_ge(s_ev[NB - 1], c)
                at_least(pe, s_ro, (c - 1) * 2)
                pe.transpose(p_r[0:CW - 1, 0:P], ext[:, 1 - slot, SEQ:SEQ + CW - 1], ident[:, :])
                pe.transpose(p_r[0:HB, P:2 * P], last_s[:, 1 - slot, :], ident[:, :]).then_inc(s_r, 1)

            for c in range(2):
                body(c, c, 0, first=(c == 0))
            with pe.Fori(1, NCV // 2) as i:
                body(i * 2, 0, i)
                body(i * 2 + 1, 1, i)
            for c in range(NCV, NST):
                body(c, c % 2, c // 2)
            pe.wait_ge(s_wlo, NST + 1)
            for n in range(NB):
                pe.wait_ge(s_ev[n], NST)
                dst, cols = p_y[n][0:2 * H1, 0:BT], slice(n * BT, (n + 1) * BT)
                for k in range(KC):
                    pe.matmul(dst, w_hi[:, 0, k, 0:2 * H1], xT_hi[:, k, cols], start=(k == 0), stop=False)
                    pe.matmul(dst, w_hi[:, 0, k, 0:2 * H1], xT_lo[:, k, cols], start=False, stop=False)
                    mm = pe.matmul(dst, w_lo[:, 0, k, 0:2 * H1], xT_hi[:, k, cols], start=False, stop=(k == KC - 1))
                mm.then_inc(s_y[n], 1)

        @block.scalar
        def _(act):
            def body(c, slot, nth, conv=True, first=False):
                if conv and not first:
                    act.wait_ge(s_cv, c * STEPS - STEPS)
                    act.wait_ge(s_r, c - 1)
                for n in range(NB):
                    act.wait_ge(s_y[n], c + 1)
                    if not conv:
                        act.wait_ge(s_o[slot], nth * 16)
                        mm = act.activation(out[:, slot, n * BT:(n + 1) * BT], p_y[n][:, 0:BT], ACT.Silu)
                    else:
                        m = BT if n < NB - 1 else LP
                        mm = act.activation(ext[:, slot, CW - 1 + n * BT:CW - 1 + n * BT + m], p_y[n][:, 0:m], ACT.Copy)
                        if n == NB - 1:
                            mm = act.activation(ext_s[:, slot, :, CW - 1:CW - 1 + DS],
                                                p_y[n][:, LP:BT].rearrange("p (b t) -> p b t", t=DS), ACT.Copy)
                    mm.then_inc(s_ev[n], 1)
                if conv:
                    act.wait_ge(s_cv, c * STEPS + STEPS)
                    act.activation(out[:, slot, :], out[:, slot, :], ACT.Silu).then_inc(s_sl, 1)
                else:
                    for n in range(NB):
                        act.wait_ge(s_ev[n], c + 1)
                    act.sem_inc(s_sl, 1)

            for n in range(NB):
                cols = slice(n * BT, (n + 1) * BT)
                act.wait_ge(s_xt[n], 16)
                act.activation(xT_hi[:, :, cols], xT_lo[:, :, cols].bitcast(F32), ACT.Copy).then_inc(s_xhi, 1)
            act.wait_ge(s_prc, 3)
            act.wait_ge(s_set, 1)
            body(0, 0, 0, first=True)
            body(1, 1, 0, first=True)
            with act.Fori(1, NCV // 2) as i:
                body(i * 2, 0, i)
                body(i * 2 + 1, 1, i)
            for c in range(NCV, NST):
                body(c, c % 2, c // 2, conv=False)
            for n in range(NB):
                act.wait_ge(s_y[n], NST + 1)
                act.activation(ba[:, n * BT:(n + 1) * BT], p_y[n][0:2 * H1, 0:BT], ACT.Copy).then_inc(s_ev[n], 1)

        @block.vector
        def _(dve):
            dve.wait_ge(s_pre, 1)
            dve.tensor_copy(taps[:, :, :], p_r[:, 0:NCV * CW].rearrange("p (c j) -> p c j", j=CW)).then_inc(s_prc, 1)
            dve.wait_ge(s_pre, 2)
            for n in range(2):
                dve.tensor_copy(hist[:, 12 * n:12 * n + 12, :], p_y[n][:, 0:12 * HB].rearrange(
                    "p (c j) -> p c j", j=HB)).then_inc(s_prc, 1)
            dve.wait_ge(s_prc, 3)
            dve.memset(ext[:, :, 0:CW - 1], 0.0).then_inc(s_set, 1)

            def split_w(c, slot, nth, m=P):
                dve.wait_ge(s_w[slot], nth * 16 + 16)
                dve.tensor_tensor(w_raw[:, slot, :, 0:m], w_raw[:, slot, :, 0:m],
                                  g_odd[:, :].unsqueeze(2).to_broadcast([P, KC, m]), ALU.mult).then_inc(s_wg, 1)
                dve.wait_ge(s_wg, c + 1)
                if not (isinstance(c, int) and c < 2):
                    dve.wait_ge(s_y[NB - 1], c - 1)
                dve.tensor_copy(w_hi[:, slot, :, 0:m], w_raw[:, slot, :, 0:m]).then_inc(s_whi, 1)
                dve.wait_ge(s_whi, c + 1)
                dve.tensor_tensor(w_lo[:, slot, :, 0:m], w_raw[:, slot, :, 0:m], w_hi[:, slot, :, 0:m].bitcast(F32),
                                  ALU.subtract).then_inc(s_wlo, 1)

            def rows(c):
                dve.wait_ge(s_r, c + 1)
                at_least(dve, s_rs, c * 32)
                dve.tensor_copy(rows_p[:, :], p_r[0:CW - 1, 0:P]).then_inc(s_ro, 1)
                dve.tensor_copy(rows_s[:, :], p_r[0:HB, P:2 * P]).then_inc(s_ro, 1)

            def body(c, slot, nth):
                if not (isinstance(c, int) and c < 2):
                    dve.wait_ge(s_sl, c - 1)
                    dve.wait_ge(s_r, c - 1)
                dve.tensor_copy(tap[:, slot, :], taps[:, bass.ds(c, 1), :].rearrange("p o j -> p (o j)")).then_inc(s_tap, 1)
                dve.tensor_copy(ext_s[:, slot, :, 0:CW - 1], hist[:, bass.ds(c, 1), :].rearrange(
                    "p o (b r) -> p (o b) r", r=CW - 1)).then_inc(s_tap, 1)
                split_w(c + 1, 1 - slot, nth + slot)
                dve.wait_ge(s_tap, c * 2 + 2)
                dve.wait_ge(s_o[slot], nth * 16)
                for n in range(NB):
                    dve.wait_ge(s_ev[n], c + 1)
                dve.tensor_copy(last_s[:, slot, :].rearrange("p (b r) -> p b r", r=CW - 1),
                                ext_s[:, slot, :, DS:DS + CW - 1]).then_inc(s_last, 1)
                y, ys = out[:, slot, 0:SEQ], out[:, slot, SEQ:TOK].rearrange("p (b t) -> p b t", t=DS)
                for j in range(CW):
                    if j == 0:
                        dve.tensor_scalar(y, ext[:, slot, 0:SEQ], tap[:, slot, 0:1], None, ALU.mult).then_inc(s_cv, 1)
                        dve.tensor_scalar(ys, ext_s[:, slot, :, 0:DS], tap[:, slot, 0:1], None, ALU.mult).then_inc(s_cv, 1)
                    else:
                        dve.wait_ge(s_cv, c * STEPS + 2 * j)
                        dve.scalar_tensor_tensor(y, ext[:, slot, j:j + SEQ], tap[:, slot, j:j + 1], y, ALU.mult,
                                                 ALU.add).then_inc(s_cv, 1)
                        dve.scalar_tensor_tensor(ys, ext_s[:, slot, :, j:j + DS], tap[:, slot, j:j + 1], ys, ALU.mult,
                                                 ALU.add).then_inc(s_cv, 1)
                if not (isinstance(c, int) and c == 0):
                    rows(c - 1)

            split_w(0, 0, 0)
            for n in range(NB):
                cols = slice(n * BT, (n + 1) * BT)
                dve.wait_ge(s_xhi, n + 1)
                dve.tensor_tensor(xT_lo[:, :, cols], xT_lo[:, :, cols].bitcast(F32), xT_hi[:, :, cols].bitcast(F32),
                                  ALU.subtract).then_inc(s_xlo, 1)
            body(0, 0, 0)
            body(1, 1, 0)
            with dve.Fori(1, NCV // 2) as i:
                body(i * 2, 0, i)
                body(i * 2 + 1, 1, i)
            split_w(NCV + 1, 1, NCV // 2)
            rows(NCV - 1)
            for c in range(NCV + 2, NST):
                split_w(c, c % 2, c // 2)
            split_w(NST, 0, NST // 2, m=2 * H1)


def stage_e(nc, io, cat, gd):
    with Stage(nc, "E") as st:
        sb, ps, sem = st.sb, st.ps, st.sem
        CH = 4
        NU = NT // CH
        LAST = NU * H1
        ident = sb("ident", [P, P])
        ident_b = sb("ident_b", [P, P], BF16)
        mask_f = sb("mask_f", [P, CH * P])
        mask = sb("mask", [P, CH * P], BF16)
        levels = sb("levels", [P, LEVELS, P])
        g_o = sb("g_o", [P, 1])
        half = sb("half", [P, 2 * CH])
        src = sb("src", [P, 2, 3, CH * P])
        z = sb("z", [P, 2, CH * P])
        sm = sb("sm", [P, NU, 5, CH])
        k_tok = sb("k_tok", [P, 2, CH, P])
        sq = sb("sq", [P, 2, CH, P])
        ss, sse, rn = (sb(n, [P, 2 * CH]) for n in ("ss", "sse", "rn"))
        nb, brk, kwf, ktf = (sb(n, [P, CH]) for n in ("nb", "brk", "kwf", "ktf"))
        rq = sb("rq", [P, NU, CH])
        erow = sb("erow", [P, CH, P])
        dec = sb("dec", [P, CH, P])
        kbT = sb("kbT", [P, CH, P])
        lt = sb("lt", [P, CH, P])
        nbs = sb("nbs", [P, 2, LEVELS, CH, P])
        ut = sb("ut", [P, 2, 2, 2, 2, P])
        gm = sb("gm", [P, 2, 2, P])
        kw = sb("kw", [P, 2, CH, P])
        uf, nwT = (sb(n, [P, 2, CH, P]) for n in ("uf", "nwT"))
        vb, qe, attT, kt = (sb(n, [P, NU, CH, P]) for n in ("vb", "qe", "attT", "kt"))
        state = sb("state", [P, 2, P])
        vn = sb("vn", [P, 2, P])
        o_sb, on = (sb(n, [P, CH, P]) for n in ("o_sb", "on"))
        junk = sb("junk", [P, P])
        oss, ose, orn = (sb(n, [P, CH]) for n in ("oss", "ose", "orn"))
        oT = sb("oT", [P, CH, P])
        p_l = [ps(f"l{i}") for i in range(2)]
        p_a, p_b = ps("a"), ps("b")
        p_v, p_o, p_s, p_t = ps("v"), ps("o"), ps("s"), ps("t")
        s_in, s_cst, s_half = sem("loaded"), sem("cast"), sem("half_set")
        s_src = [sem(f"src_in{i}") for i in range(2)]
        s_z = [sem(f"z_in{i}") for i in range(2)]
        s_sm = sem("columns")
        s_ktr, s_vtr, s_qtr, s_g, s_gm, s_br, s_kq, s_kk, s_t0 = (sem(n) for n in (
            "k_turned", "v_turned", "q_turned", "gc_rows", "gc_masked", "b_rows", "kq", "kk", "u_turned"))
        s_ktok, s_sq, s_er, s_dec = (sem(n) for n in ("k_tok", "squares", "exp_rows", "decay"))
        s_vb, s_ss, s_kb, s_qe, s_att, s_lt = (sem(n) for n in ("vb", "sums", "kbT", "qe", "att", "lt"))
        s_sse, s_rn, s_brk, s_kwf, s_nb, s_rq, s_kw, s_ktw = (sem(n) for n in (
            "sums_eps", "norm", "b_norm", "kw_factor", "neg_bias", "q_norm", "kw", "kt"))
        s_nbs, s_u0, s_t1 = sem("level_masked"), sem("u_first"), sem("t_first")
        s_x = [sem(f"lt_t{i}") for i in range(2)]
        s_gr = [sem(f"g_ready{i}") for i in range(2)]
        s_y = [sem(f"ut_product{i}") for i in range(2)]
        s_ut = [sem(f"ut_ready{i}") for i in range(2)]
        s_w, s_wn = sem("w_product"), sem("w_ready")
        s_v, s_vn, s_o, s_ds, s_st = (sem(n) for n in ("v_product", "v_new", "o_product", "state_product", "state_ready"))
        s_os, s_oss, s_ose, s_orn, s_on, s_ot, s_oT = (sem(n) for n in (
            "o_out", "o_squares", "o_mean", "o_norm", "o_normed", "o_turned", "oT_ready"))
        s_fin = sem("state_stored")
        s_oo = sem("oT_stored")
        s_pool = sem("pool_waits_settled")
        block = st.block()
        n_in = 16 * 4
        ORDER = ["x1", "turn_k", "turn_q", "v0", "y1", "s0", "x2", "turn_v", "rows_g", "v1", "y2", "s1", "x3", "decay", "rows_b",
                 "v2", "y3", "s2", "x4", "kk", "v3", "y4", "s3", "x5", "kq", "y5", "x6", "y6", "first", "w", "out"]
        RECUR = {"v0", "v1", "v2", "v3", "s0", "s1", "s2", "s3", "out"}
        PREPARE = {"turn_k", "turn_q", "turn_v", "rows_g", "decay", "rows_b", "kq", "kk", "first"}

        def later(h, g, k):
            return h * NU + g + k, (g + k) % NU, h + (g + k) // NU

        def run(eng, prepare, invert, recur):
            def turn(h, g, first=0, last=2):
                for name in ORDER:
                    if name in RECUR:
                        if first <= 0:
                            recur(name, *later(h, g, 0))
                    elif name in PREPARE:
                        if last >= 2:
                            prepare(name, *later(h, g, 2))
                    elif first <= 1 <= last:
                        invert(name, *later(h, g, 1))

            turn(0, -2, first=2)
            turn(0, -1, first=1)
            for g in range(NU):
                turn(0, g)
            with eng.Fori(1, H1 - 1) as h:
                for g in range(NU):
                    turn(h, g)
            for g in range(NU):
                turn(H1 - 1, g, last=NU - 1 - g)

        def halves(a):
            return a.rearrange("p (c i) -> p c i", c=CH)

        @block.sync
        def _(sp):
            def const(name):
                return io["consts"][:, cat[name][0]:cat[name][1]]

            lv = (cat["level0"][0], cat[f"level{LEVELS - 1}"][1])
            for dst, s in ((ident[:, :], const("ident")), (mask_f[:, :], const("mask_tri")),
                           (levels[:, :, :], io["consts"][:, lv[0]:lv[1]].rearrange("p (l i) -> p l i", i=P)),
                           (g_o[:, :], io["o_norm"].rearrange("o e -> e o"))):
                sp.dma_start(dst, s, allow_slow_non_contiguous=True).then_inc(s_in, 16)

            def strip(n, g, h):
                return io["strips"][bass.ds(h + n * H1, 1), :, g * CH * P:(g + 1) * CH * P].rearrange("o p n -> p (o n)")

            def load(w, g, h):
                for n in range(3):
                    sp.dma_start(src[:, g % 2, n, :], strip(n, g, h)).then_inc(s_src[g % 2], 16)

            def load_z(w, g, h):
                sp.dma_start(z[:, g % 2, :], strip(3, g, h)).then_inc(s_z[g % 2], 16)

            def turn(h, g, last=3):
                w = h * NU + g
                if last >= 3:
                    sp.wait_ge(s_kq, w + 2)
                    sp.wait_ge(s_qe, w + 2)
                    load(*later(h, g, 3))
                if g == NU - 1:
                    sp.wait_ge(s_st, h * NT + NT)
                    sp.dma_start(io["delta_prompt"][0, 0, bass.ds(h, 1), :, :].rearrange("o p n -> p (o n)"),
                                 state[:, 0, :]).then_inc(s_fin, 16)
                sp.wait_ge(s_oT, w + 1)
                sp.dma_start(io["oT"][bass.ds(h, 1), :, g * CH * P:(g + 1) * CH * P].rearrange("o p n -> p (o n)"),
                             oT[:, :, :].rearrange("p c i -> p (c i)")).then_inc(s_oo, 16)
                if last >= 2:
                    load_z(*later(h, g, 2))

            load(0, 0, 0)
            load(1, 1, 0)
            load_z(0, 0, 0)
            load_z(1, 1, 0)
            sp.wait_ge(s_kq, 1)
            sp.wait_ge(s_qe, 1)
            load(2, 2, 0)
            for g in range(NU):
                turn(0, g)
            with sp.Fori(1, H1 - 1) as h:
                for g in range(NU):
                    turn(h, g)
            for g in range(NU):
                turn(H1 - 1, g, last=NU - 1 - g)
            sp.wait_ge(s_fin, 16 * H1)
            sp.wait_ge(s_oo, 16 * LAST)

        @block.tensor
        def _(pe):
            pe.wait_ge(s_in, n_in)
            pe.wait_ge(s_cst, 2)

            cs = [slice(c * P, (c + 1) * P) for c in range(CH)]

            def prepare(name, w, g, h):
                q_, k_, v_ = (src[:, g % 2, n, :] for n in range(3))

                def turn(bank, t, s):
                    for c in range(CH):
                        mm = pe.transpose(bank[:, cs[c]], t[:, cs[c]], ident[:, :])
                    mm.then_inc(s, 1)

                if name == "turn_k":
                    pe.wait_ge(s_src[g % 2], (h * 2 + g // 2) * 48 + 48)
                    at_least(pe, s_t1, w)
                    turn(p_a, k_, s_ktr)
                elif name == "turn_q":
                    at_least(pe, s_lt, w)
                    turn(p_b, q_, s_qtr)
                elif name == "turn_v":
                    pe.wait_ge(s_sq, w * 2 + 2)
                    turn(p_b, v_, s_vtr)
                elif name == "rows_g":
                    pe.wait_ge(s_sm, w + 1)
                    for c in range(CH):
                        mm = pe.matmul(p_a[:, cs[c]], sm[:, g, 1, c:c + 1].to_broadcast([P, P]), ident[:, :],
                                       start=(c == 0), stop=True, skip_group_check=True)
                    mm.then_inc(s_g, 1)
                elif name == "decay":
                    pe.wait_ge(s_er, w + 1)
                    pe.matmul(p_a[:, :], ident_b[:, :], mask[:, :], start=False, stop=True,
                              skip_group_check=True).then_inc(s_gm, 1)
                elif name == "rows_b":
                    pe.wait_ge(s_brk, w + 1)
                    pe.wait_ge(s_vb, w + 1)
                    for c in range(CH):
                        mm = pe.matmul(p_b[:, cs[c]], brk[:, c:c + 1].to_broadcast([P, P]), ident[:, :],
                                       start=True, stop=True)
                    mm.then_inc(s_br, 1)
                elif name == "kq":
                    pe.wait_ge(s_dec, w * CH + CH)
                    for c in range(CH):
                        mm = pe.matmul(p_a[:, cs[c]], k_[:, cs[c]], q_[:, cs[c]], start=True, stop=True)
                    mm.then_inc(s_kq, 1)
                elif name == "kk":
                    pe.wait_ge(s_kb, w + 1)
                    for c in range(CH):
                        mm = pe.matmul(p_b[:, cs[c]], k_[:, cs[c]], kbT[:, c, :], start=True, stop=True)
                    mm.then_inc(s_kk, 1)
                elif name == "first":
                    pe.wait_ge(s_u0, w + 1)
                    pe.wait_ge(s_att, w + 1)
                    for c in range(CH):
                        mm = pe.transpose(p_a[:, cs[c]], ut[:, 0, c // 2, 0, c % 2, :], ident[:, :])
                    mm.then_inc(s_t0, 1)

            def invert(name, w, g, h):
                if name == "w":
                    pe.wait_ge(s_kw, w + 1)
                    for hf in range(2):
                        pe.wait_ge(s_ut[hf], w * (LEVELS - 1) + LEVELS - 1)
                        for c in range(2):
                            mm = pe.matmul(p_l[hf][:, cs[c]], kw[:, g % 2, 2 * hf + c, :], uf[:, g % 2, 2 * hf + c, :],
                                           start=True, stop=True)
                        mm.then_inc(s_w, 1)
                    return
                n = int(name[1])
                old = (n - 1) % 2
                for hf in range(2):
                    if name[0] == "x":
                        if n == 1:
                            pe.wait_ge(s_t1, w + 1)
                            at_least(pe, s_wn, w * 2)
                        else:
                            pe.wait_ge(s_ut[hf], w * (LEVELS - 1) + n - 1)
                        pe.wait_ge(s_nbs, w * LEVELS + n + 1)
                        for c in range(2):
                            mm = pe.matmul(p_l[hf][:, cs[c]], nbs[:, g % 2, n, 2 * hf + c, :], ut[:, old, hf, 1, c, :],
                                           start=True, stop=True)
                        mm.then_inc(s_x[hf], 1)
                    else:
                        pe.wait_ge(s_gr[hf], w * (LEVELS - 1) + n)
                        for c in range(2):
                            mm = pe.matmul(p_l[hf][:, cs[c]], gm[:, hf, c, :], ut[:, old, hf, 0, c, :],
                                           start=True, stop=True)
                        if n < LEVELS - 1:
                            for c in range(2):
                                mm = pe.matmul(p_l[hf][:, cs[2 + c]], ut[:, old, hf, 0, c, :], gm[:, hf, c, :],
                                               start=True, stop=True)
                        mm.then_inc(s_y[hf], 1)

            def recur(name, w, g, h):
                if name == "out":
                    pe.wait_ge(s_on, w + 1)
                    for c in range(CH):
                        mm = pe.transpose(p_t[:, c * P:(c + 1) * P], on[:, c, :], ident[:, :])
                    mm.then_inc(s_ot, 1)
                    return
                c = int(name[1])
                n = w * CH + c
                head_start = g == 0 and c == 0
                old = c % 2
                if name[0] == "v":
                    if c == 0:
                        pe.wait_ge(s_wn, w * 2 + 2)
                    at_least(pe, s_vn, n)
                    pe.matmul(p_v[:, 0:P], uf[:, g % 2, c, :], vb[:, g, c, :], start=True, stop=head_start).then_inc(
                        s_v, 1) if head_start else pe.matmul(p_v[:, 0:P], uf[:, g % 2, c, :], vb[:, g, c, :],
                                                             start=True, stop=False)
                    if not head_start:
                        pe.wait_ge(s_st, n)
                        pe.matmul(p_v[:, 0:P], nwT[:, g % 2, c, :], state[:, old, :], start=False, stop=True).then_inc(s_v, 1)
                else:
                    at_least(pe, s_oss, n)
                    if not head_start:
                        pe.matmul(p_o[:, 0:P], qe[:, g, c, :], state[:, old, :], start=True, stop=False)
                    pe.wait_ge(s_vn, n + 1)
                    if c == 0:
                        pe.wait_ge(s_ktw, w + 1)
                    pe.matmul(p_s[:, 0:P], kt[:, g, c, :], vn[:, c % 2, :], start=True, stop=True).then_inc(s_ds, 1)
                    pe.matmul(p_o[:, 0:P], attT[:, g, c, :], vn[:, c % 2, :], start=head_start, stop=True).then_inc(s_o, 1)

            run(pe, prepare, invert, recur)

        @block.scalar
        def _(act):
            def prepare(name, w, g, h):
                if name == "turn_k":
                    act.wait_ge(s_ktr, w + 1)
                    at_least(act, s_ktw, w - 1)
                    act.activation(k_tok[:, g % 2, :, :], halves(p_a[:, :]), ACT.Copy).then_inc(s_ktok, 1)
                    at_least(act, s_ss, w)
                    act.activation(sq[:, 1, :, :], halves(p_a[:, :]), ACT.Square).then_inc(s_sq, 1)
                elif name == "turn_q":
                    act.wait_ge(s_qtr, w + 1)
                    act.activation(sq[:, 0, :, :], halves(p_b[:, :]), ACT.Square).then_inc(s_sq, 1)
                elif name == "rows_g":
                    act.wait_ge(s_g, w + 1)
                    at_least(act, s_qe, w)
                    act.activation(erow[:, :, :], halves(p_a[:, :]), ACT.Exp).then_inc(s_er, 1)
                elif name == "decay":
                    act.wait_ge(s_gm, w + 1)
                    act.wait_ge(s_nb, w + 1)
                    at_least(act, s_att, w)
                    for c in range(CH):
                        act.activation(dec[:, c, :], p_a[:, c * P:(c + 1) * P], ACT.Exp, bias=nb[:, c:c + 1]).then_inc(s_dec, 1)
                elif name == "first":
                    act.wait_ge(s_t0, w + 1)
                    act.activation(ut[:, 0, :, 1, :, :].rearrange("p f c i -> p f (c i)"),
                                   p_a[:, :].rearrange("p (f n) -> p f n", f=2), ACT.Copy).then_inc(s_t1, 1)

            def invert(name, w, g, h):
                if name == "w":
                    for hf in range(2):
                        act.wait_ge(s_w, w * 2 + hf + 1)
                        act.activation(nwT[:, g % 2, 2 * hf:2 * hf + 2, :], p_l[hf][:, 0:2 * P].rearrange(
                            "p (c i) -> p c i", c=2), ACT.Copy, scale=-1.0).then_inc(s_wn, 1)
                elif name[0] == "y":
                    n = int(name[1])
                    for hf in range(2):
                        act.wait_ge(s_y[hf], w * (LEVELS - 1) + n)
                        if n < LEVELS - 1:
                            act.activation(ut[:, n % 2, hf, :, :, :].rearrange("p a c i -> p (a c) i"),
                                           halves(p_l[hf][:, :]), ACT.Copy).then_inc(s_ut[hf], 1)
                        else:
                            at_least(act, s_oT, w - 1)
                            act.activation(uf[:, g % 2, 2 * hf:2 * hf + 2, :], p_l[hf][:, 0:2 * P].rearrange(
                                "p (c i) -> p c i", c=2), ACT.Copy).then_inc(s_ut[hf], 1)

            def recur(name, w, g, h):
                if name[0] == "s":
                    c = int(name[1])
                    n = w * CH + c
                    act.wait_ge(s_o, n + 1)
                    if c == 0:
                        at_least(act, s_on, w)
                        at_least(act, s_ose, w)
                    act.activation(o_sb[:, c, :], p_o[:, 0:P], ACT.Copy, scale=rq[:, g, c:c + 1]).then_inc(s_os, 1)
                    at_least(act, s_oss, n)
                    act.activation(junk[:, :], p_o[:, 0:P], ACT.Square, scale=rq[:, g, c:c + 1],
                                   accum_out=oss[:, c:c + 1]).then_inc(s_oss, 1)

            run(act, prepare, invert, recur)

        @block.vector
        def _(dve):
            dve.wait_ge(s_in, n_in)
            dve.tensor_copy(ident_b[:, :], ident[:, :]).then_inc(s_cst, 1)
            dve.tensor_copy(mask[:, :], mask_f[:, :]).then_inc(s_cst, 1)

            def prepare(name, w, g, h):
                if name == "turn_q":
                    dve.wait_ge(s_sq, w * 2 + 2)
                    at_least(dve, s_sse, w)
                    dve.tensor_reduce(ss[:, :], sq[:, :, :, :].rearrange("p a c i -> p (a c) i"), AX.X, ALU.add).then_inc(s_ss, 1)
                elif name == "turn_v":
                    dve.wait_ge(s_vtr, w + 1)
                    dve.wait_ge(s_sm, w + 1)
                    at_least(dve, s_oT, w - 2)
                    dve.tensor_tensor(vb[:, g, :, :], halves(p_b[:, :]),
                                      sm[:, g, 0, :].unsqueeze(2).to_broadcast([P, CH, P]), ALU.mult).then_inc(s_vb, 1)
                elif name == "rows_g":
                    dve.wait_ge(s_er, w + 1)
                    dve.tensor_tensor(qe[:, g, :, :], halves(src[:, g % 2, 0, :]), erow[:, :, :], ALU.mult).then_inc(s_qe, 1)
                elif name == "rows_b":
                    dve.wait_ge(s_br, w + 1)
                    at_least(dve, s_kk, w)
                    dve.tensor_tensor(kbT[:, :, :], halves(src[:, g % 2, 1, :]), halves(p_b[:, :]), ALU.mult).then_inc(s_kb, 1)
                elif name == "kq":
                    dve.wait_ge(s_kq, w + 1)
                    for c in range(CH):
                        mm = dve.scalar_tensor_tensor(attT[:, g, c, :], p_a[:, c * P:(c + 1) * P], rn[:, CH + c:CH + c + 1],
                                                      dec[:, c, :], ALU.mult, ALU.mult)
                    mm.then_inc(s_att, 1)
                elif name == "kk":
                    dve.wait_ge(s_kk, w + 1)
                    dve.wait_ge(s_dec, w * CH + CH)
                    dve.wait_ge(s_rn, w + 1)
                    at_least(dve, s_nbs, w * LEVELS)
                    for c in range(CH):
                        mm = dve.scalar_tensor_tensor(lt[:, c, :], p_b[:, c * P:(c + 1) * P], rn[:, CH + c:CH + c + 1],
                                                      dec[:, c, :], ALU.mult, ALU.mult)
                    mm.then_inc(s_lt, 1)
                elif name == "first":
                    dve.wait_ge(s_nbs, w * LEVELS + 1)
                    at_least(dve, s_y[1], w * (LEVELS - 1) - 1)
                    for hf in range(2):
                        mm = dve.tensor_tensor(ut[:, 0, hf, 0, :, :], nbs[:, g % 2, 0, 2 * hf:2 * hf + 2, :],
                                               ident[:, :].unsqueeze(1).to_broadcast([P, 2, P]), ALU.add)
                    mm.then_inc(s_u0, 1)

            def invert(name, w, g, h):
                if name[0] == "x":
                    n = int(name[1])
                    for hf in range(2):
                        dve.wait_ge(s_x[hf], w * (LEVELS - 1) + n)
                        dve.tensor_tensor(gm[:, hf, :, :], p_l[hf][:, 0:2 * P].rearrange("p (c i) -> p c i", c=2),
                                          ident[:, :].unsqueeze(1).to_broadcast([P, 2, P]), ALU.add).then_inc(s_gr[hf], 1)

            def recur(name, w, g, h):
                if name == "out":
                    dve.wait_ge(s_orn, w + 1)
                    dve.wait_ge(s_os, w * CH + CH)
                    at_least(dve, s_ot, w)
                    dve.tensor_tensor(on[:, :, :], o_sb[:, :, :], orn[:, :].unsqueeze(2).to_broadcast([P, CH, P]),
                                      ALU.mult).then_inc(s_on, 1)
                    dve.wait_ge(s_ot, w + 1)
                    at_least(dve, s_oo, w * 16)
                    dve.wait_ge(s_z[g % 2], (h * 2 + g // 2) * 16 + 16)
                    dve.scalar_tensor_tensor(oT[:, :, :], halves(p_t[:, :]), g_o[:, 0:1], halves(z[:, g % 2, :]),
                                             ALU.mult, ALU.mult).then_inc(s_oT, 1)
                    return
                c = int(name[1])
                n = w * CH + c
                if name[0] == "v":
                    dve.wait_ge(s_v, n + 1)
                    at_least(dve, s_o, n if c == 0 else n - 1)
                    dve.tensor_copy(vn[:, c % 2, :], p_v[:, 0:P]).then_inc(s_vn, 1)
                else:
                    dve.wait_ge(s_ds, n + 1)
                    new = (c + 1) % 2
                    if g == 0 and c == 0:
                        dve.tensor_copy(state[:, new, :], p_s[:, 0:P]).then_inc(s_st, 1)
                    else:
                        if g == 0 and c == 1:
                            at_least(dve, s_fin, h * 16)
                        dve.wait_ge(s_st, n)
                        dve.scalar_tensor_tensor(state[:, new, :], state[:, c % 2, :], sm[:, g, 4, c:c + 1],
                                                 p_s[:, 0:P], ALU.mult, ALU.add).then_inc(s_st, 1)

            run(dve, prepare, invert, recur)

        @block.gpsimd
        def _(pool):
            pool.memset(half[:, :], -0.5).then_inc(s_half, 1)

            def prepare(name, w, g, h):
                if name == "turn_k":
                    at_least(pool, s_oT, w - 2)
                    pool.tensor_copy(sm[:, g, :, :], gd[:, 0:5, g * CH:(g + 1) * CH, bass.ds(h, 1)].rearrange(
                        "p f c o -> p f (c o)")).then_inc(s_sm, 1)
                    pool.wait_ge(s_sm, w + 1)
                    at_least(pool, s_dec, w * CH)
                    settle(pool, s_pool)
                    pool.tensor_scalar(nb[:, :], sm[:, g, 1, :], -1.0, None, ALU.mult).then_inc(s_nb, 1)
                elif name == "turn_q":
                    pool.wait_ge(s_ss, w + 1)
                    settle(pool, s_pool)
                    pool.tensor_scalar(sse[:, :], ss[:, :], EPS, None, ALU.add).then_inc(s_sse, 1)
                    pool.wait_ge(s_sse, w + 1)
                    at_least(pool, s_att, w)
                    pool.tensor_tensor(rn[:, :], sse[:, :], half[:, :], ALU.pow).then_inc(s_rn, 1)
                    pool.wait_ge(s_rn, w + 1)
                    at_least(pool, s_br, w)
                    pool.tensor_tensor(brk[:, :], sm[:, g, 0, :], rn[:, CH:2 * CH], ALU.mult).then_inc(s_brk, 1)
                    at_least(pool, s_kw, w)
                    pool.wait_ge(s_brk, w + 1)
                    pool.tensor_tensor(kwf[:, :], brk[:, :], sm[:, g, 2, :], ALU.mult).then_inc(s_kwf, 1)
                    at_least(pool, s_ktw, w)
                    pool.tensor_tensor(ktf[:, :], rn[:, CH:2 * CH], sm[:, g, 3, :], ALU.mult).then_inc(s_rq, 1)
                    pool.tensor_scalar(rq[:, g, :], rn[:, 0:CH], D1 ** -0.5, None, ALU.mult).then_inc(s_rq, 1)
                elif name == "kk":
                    pool.wait_ge(s_lt, w + 1)
                    at_least(pool, s_w, w * 2 - 2)
                    mask_levels(g, range(3))
                elif name == "kq":
                    mask_levels(g, range(3, LEVELS))
                    pool.wait_ge(s_ktok, w + 1)
                    pool.wait_ge(s_kwf, w + 1)
                    pool.tensor_tensor(kw[:, g % 2, :, :], k_tok[:, g % 2, :, :], kwf[:, :].unsqueeze(2).to_broadcast(
                        [P, CH, P]), ALU.mult).then_inc(s_kw, 1)
                    pool.wait_ge(s_rq, w * 2 + 2)
                    pool.tensor_tensor(kt[:, g, :, :], k_tok[:, g % 2, :, :], ktf[:, :].unsqueeze(2).to_broadcast(
                        [P, CH, P]), ALU.mult).then_inc(s_ktw, 1)

            def mask_levels(g, levels_now):
                for n in levels_now:
                    pool.tensor_tensor(nbs[:, g % 2, n, :, :], lt[:, :, :],
                                       levels[:, n, :].unsqueeze(1).to_broadcast([P, CH, P]), ALU.mult).then_inc(s_nbs, 1)

            def invert(name, w, g, h):
                pass

            def recur(name, w, g, h):
                if name == "s3":
                    pool.wait_ge(s_oss, w * CH + CH)
                    at_least(pool, s_orn, w)
                    settle(pool, s_pool)
                    pool.tensor_scalar(ose[:, :], oss[:, :], 1.0 / D1, EPS, ALU.mult, ALU.add).then_inc(s_ose, 1)
                    pool.wait_ge(s_ose, w + 1)
                    at_least(pool, s_on, w)
                    pool.tensor_tensor(orn[:, :], ose[:, :], half[:, 0:CH], ALU.pow).then_inc(s_orn, 1)

            pool.wait_ge(s_in, n_in)
            pool.wait_ge(s_half, 1)
            run(pool, prepare, invert, recur)


def stage_h(nc, io, cat, gd):
    with Stage(nc, "H") as st:
        sb, ps, sem = st.sb, st.ps, st.sem
        ident = sb("ident", [P, P])
        own = sb("own", [P, DB])
        own_cols = sb("own_cols", [P, DB, NS])
        mask = sb("mask", [NS, NS])
        strict = sb("strict", [NS, NS])
        g_o = sb("g_o", [P, 1])
        half = sb("half", [NS, 2 * H1])
        src = sb("src", [P, 4, H1, NS])
        state = sb("state", [P, DB, H1, D1])
        faded = sb("faded", [P, DB, H1, D1])
        k_tok, q_tok, kb, kt, kw, vb, vn, sq_k, sq_q, qe = (sb(n, [NS, H1, D1]) for n in (
            "k_tok", "q_tok", "kb", "kt", "kw", "vb", "vn", "sq_k", "sq_q", "qe"))
        ss, sse, rn = (sb(n, [NS, 2, H1]) for n in ("ss", "sse", "rn"))
        oss, ose, orn = (sb(n, [NS, H1]) for n in ("oss", "ose", "orn"))
        gap = sb("gap", [NS, H1, NS])
        dec = sb("dec", [NS, H1, NS])
        turned = sb("turned", [P, 3, H1, NS])
        qnT = sb("qnT", [P, H1, NS])
        att, m, n_, r, u = (sb(x, [NS, H1, NS]) for x in ("att", "m", "n", "r", "u"))
        mi = sb("mi", [NS, H1, NS])
        wz, qz = (sb(n, [P, H1, DB, NS]) for n in ("wz", "qz"))
        vx = sb("vx", [NS, 2, DB, D1])
        oT = sb("oT", [P, H1, NS])
        p = [ps(f"b{i}") for i in range(8)]
        s_in, s_src, s_state, s_half = sem("loaded"), sem("src_in"), sem("state_in"), sem("half_set")
        s_tr, s_qk, s_sq, s_ss, s_sse, s_rn = (sem(n) for n in ("turned", "qk_out", "squares", "sums", "sums_eps", "norms"))
        s_vb, s_kn, s_qn, s_kb, s_kw, s_kt, s_qe = (sem(n) for n in ("vb", "k_normed", "q_normed", "kb", "kw", "kt", "q_exp"))
        s_g, s_gap1, s_gap2, s_dec = (sem(n) for n in ("gc_rows", "gc_masked", "gap", "decay"))
        s_bt, s_bT, s_kk, s_m1, s_m, s_mi, s_att = (sem(n) for n in (
            "back_turned", "back_ready", "scores", "m_decayed", "m_ready", "m_plus_i", "att_ready"))
        s_nt, s_n, s_nn, s_r, s_up, s_u, s_wp, s_wz, s_qz = (sem(n) for n in (
            "m_turned", "n_ready", "n_squared", "r_ready", "u_product", "u_ready", "w_product", "w_spread", "q_spread"))
        s_v, s_vn, s_vx, s_ds, s_new, s_o = (sem(n) for n in (
            "v_product", "v_new", "v_spread", "state_product", "state_ready", "o_product"))
        s_osq, s_oss, s_ose, s_orn, s_on, s_ot, s_oT = (sem(n) for n in (
            "o_squares", "o_sums", "o_mean", "o_norm", "o_normed", "o_turned", "oT_ready"))
        s_fade, s_out = sem("faded"), sem("stored")
        block = st.block()
        loads = [(ident[:, :], io["consts"][:, cat["ident"][0]:cat["ident"][1]]),
                 (own[:, :], io["consts"][:, cat["own_batch"][0]:cat["own_batch"][1]]),
                 (own_cols[:, :, :], io["consts"][:, cat["own_cols"][0]:cat["own_cols"][1]].rearrange(
                     "p (b t) -> p b t", t=NS)),
                 (mask[:, :], io["consts"][0:NS, cat["mask_tri_samp"][0]:cat["mask_tri_samp"][0] + NS]),
                 (strict[:, :], io["consts"][0:NS, cat["strict_samp"][0]:cat["strict_samp"][0] + NS]),
                 (g_o[:, :], io["o_norm"].rearrange("o e -> e o"))]
        n_in = 16 * len(loads)
        col = lambda a: a.unsqueeze(2).to_broadcast([NS, H1, D1])
        beta, gc, egc, erest = (gd[0:NS, f, NT, :] for f in range(4))

        def heads(bank, n):
            return p[bank + n][0:NS, :].rearrange("p (h d) -> p h d", d=D1)

        @block.sync
        def _(sp):
            for n in range(4):
                sp.dma_start(src[:, n, :, :], io["strips"][n * H1:(n + 1) * H1, :, SEQ:SEQ + NS].rearrange(
                    "h p t -> p h t")).then_inc(s_src, 16)
            load_all(sp, s_in, loads)
            for b in range(DB):
                sp.dma_start(state[:, b, :, :], io["state_delta"][0, b, :, :, :].rearrange("h k v -> k h v")).then_inc(
                    s_state, 16)
            for h in range(H1):
                sp.wait_ge(s_new, 2 * h + 2)
                sp.dma_start(io["delta_sample"][0, :, h, :, :].rearrange("b k v -> k b v"), faded[:, :, h, :]).then_inc(
                    s_out, 16)
            sp.wait_ge(s_oT, 1)
            sp.dma_start(io["oT"][:, :, SEQ:SEQ + NS].rearrange("h p t -> p h t"), oT[:, :, :]).then_inc(s_out, 16)
            sp.wait_ge(s_out, 16 * (H1 + 1))

        @block.tensor
        def _(pe):
            pe.wait_ge(s_in, n_in)
            pe.wait_ge(s_src, 64)
            for bank, n in ((0, 1), (2, 0), (4, 2)):
                for h in range(H1):
                    mm = pe.transpose(p[bank + h // 4][0:NS, h % 4 * D1:(h % 4 + 1) * D1], src[:, n, h, :], ident[:, :])
                mm.then_inc(s_tr, 1)
            for h in range(H1):
                mm = pe.matmul(p[6][0:NS, h * NS:(h + 1) * NS], gd[0:NS, 1, NT, h:h + 1].to_broadcast([NS, NS]),
                               ident[0:NS, 0:NS], start=True, stop=True)
            mm.then_inc(s_g, 1)
            for n, (ready, t) in enumerate(((s_kn, k_tok), (s_kb, kb), (s_qe, qe), (s_qn, q_tok))):
                pe.wait_ge(ready, 1)
                for h in range(H1):
                    mm = pe.transpose(p[n][:, h * NS:(h + 1) * NS], t[:, h, :], ident[0:NS, 0:NS])
                mm.then_inc(s_bt, 1)
            pe.wait_ge(s_bT, 4)
            pe.wait_ge(s_vb, 2)
            for bank, t in ((4, turned[:, 1]), (5, qnT)):
                for h in range(H1):
                    mm = pe.matmul(p[bank][0:NS, h * NS:(h + 1) * NS], turned[:, 0, h, :], t[:, h, :], start=True, stop=True)
                mm.then_inc(s_kk, 1)
            pe.wait_ge(s_m, 1)
            for h in range(H1):
                mm = pe.transpose(p[7][0:NS, h * NS:(h + 1) * NS], m[:, h, :], ident[0:NS, 0:NS])
            mm.then_inc(s_nt, 1)
            pe.wait_ge(s_n, 1)
            for h in range(H1):
                mm = pe.matmul(p[0][0:NS, h * NS:(h + 1) * NS], m[:, h, :], n_[:, h, :], start=True, stop=True)
            mm.then_inc(s_nn, 1)
            pe.wait_ge(s_r, 1)
            pe.wait_ge(s_mi, 1)
            for h in range(H1):
                mm = pe.matmul(p[1][0:NS, h * NS:(h + 1) * NS], r[:, h, :], mi[:, h, :], start=True, stop=True)
            mm.then_inc(s_up, 1)
            pe.wait_ge(s_u, 1)
            pe.wait_ge(s_kw, 1)
            for h in range(H1):
                mm = pe.matmul(p[6][:, h * NS:(h + 1) * NS], kw[:, h, :], u[:, h, :], start=True, stop=True)
            mm.then_inc(s_wp, 1)
            pe.wait_ge(s_wz, 1)
            pe.wait_ge(s_state, 16 * DB)
            pe.wait_ge(s_vb, 2)
            for h in range(H1):
                out = p[h // 4][0:NS, h % 4 * D1:(h % 4 + 1) * D1]
                pe.matmul(out, u[:, h, :], vb[:, h, :], start=True, stop=False)
                for b in range(DB):
                    mm = pe.matmul(out, wz[:, h, b, :], state[:, b, h, :], start=False, stop=(b == DB - 1))
                if h % 4 == 3:
                    mm.then_inc(s_v, 1)
            pe.wait_ge(s_qz, 1)
            pe.wait_ge(s_att, 1)
            for h in range(H1):
                out = p[2 + h // 4][0:NS, h % 4 * D1:(h % 4 + 1) * D1]
                for b in range(DB):
                    pe.matmul(out, qz[:, h, b, :], state[:, b, h, :], start=(b == 0), stop=False)
                pe.wait_ge(s_vn, h // 4 + 1)
                mm = pe.matmul(out, att[:, h, :], vn[:, h, :], start=False, stop=True)
                if h % 4 == 3:
                    mm.then_inc(s_o, 1)
            pe.wait_ge(s_kt, 1)
            for h in range(H1):
                pe.wait_ge(s_vx, h + 1)
                for n in range(2):
                    if h >= 2:
                        pe.wait_ge(s_new, 2 * (h - 2) + n + 1)
                    pe.matmul(p[4 + h % 2 * 2 + n][:, :], kt[:, h, :], vx[:, h % 2, 4 * n:4 * n + 4, :].rearrange(
                        "p b d -> p (b d)"), start=True, stop=True).then_inc(s_ds, 1)
            pe.wait_ge(s_on, 1)
            for h in range(H1):
                mm = pe.transpose(p[0][:, h * NS:(h + 1) * NS], sq_k[:, h, :], ident[0:NS, 0:NS])
            mm.then_inc(s_ot, 1)

        @block.scalar
        def _(act):
            act.wait_ge(s_tr, 1)
            for n in range(2):
                act.activation(sq_k[:, 4 * n:4 * n + 4, :], heads(0, n), ACT.Square).then_inc(s_sq, 1)
            act.wait_ge(s_tr, 2)
            for n in range(2):
                act.activation(sq_q[:, 4 * n:4 * n + 4, :], heads(2, n), ACT.Square).then_inc(s_sq, 1)
            act.wait_ge(s_gap2, 1)
            act.activation(dec[:, :, :], gap[:, :, :], ACT.Exp).then_inc(s_dec, 1)
            for n, dst in enumerate((turned[:, 0], turned[:, 1], turned[:, 2], qnT[:, :, :])):
                act.wait_ge(s_bt, n + 1)
                act.activation(dst, p[n][:, 0:H1 * NS].rearrange("p (h t) -> p h t", t=NS),
                               ACT.Copy).then_inc(s_bT, 1)
            act.wait_ge(s_nt, 1)
            act.activation(n_[:, :, :], p[7][0:NS, 0:H1 * NS].rearrange("p (h t) -> p h t", t=NS), ACT.Copy).then_inc(s_n, 1)
            act.wait_ge(s_up, 1)
            act.activation(u[:, :, :], p[1][0:NS, 0:H1 * NS].rearrange("p (h t) -> p h t", t=NS), ACT.Copy).then_inc(s_u, 1)
            for n in range(2):
                act.wait_ge(s_v, n + 1)
                act.activation(vn[:, 4 * n:4 * n + 4, :], heads(0, n), ACT.Copy).then_inc(s_vn, 1)
            act.wait_ge(s_ss, 1)
            for n in range(2):
                act.wait_ge(s_o, n + 1)
                act.activation(sq_q[:, 4 * n:4 * n + 4, :], heads(2, n), ACT.Square).then_inc(s_osq, 1)

        def grow(dve, h):
            dve.wait_ge(s_fade, h + 1)
            for n in range(2):
                dve.wait_ge(s_ds, 2 * h + n + 1)
                dve.tensor_tensor(faded[:, 4 * n:4 * n + 4, h, :], faded[:, 4 * n:4 * n + 4, h, :],
                                  p[4 + h % 2 * 2 + n][:, :].rearrange("p (b d) -> p b d", d=D1),
                                  ALU.add).then_inc(s_new, 1)

        @block.vector
        def _(dve):
            dve.wait_ge(s_tr, 3)
            for n in range(2):
                dve.tensor_tensor(vb[:, 4 * n:4 * n + 4, :], heads(4, n), col(beta)[:, 4 * n:4 * n + 4, :],
                                  ALU.mult).then_inc(s_vb, 1)
            dve.wait_ge(s_g, 1)
            dve.wait_ge(s_in, n_in)
            dve.tensor_tensor(gap[:, :, :], p[6][0:NS, 0:H1 * NS].rearrange("p (h t) -> p h t", t=NS),
                              mask[:, :].unsqueeze(1).to_broadcast([NS, H1, NS]), ALU.add).then_inc(s_gap1, 1)
            dve.wait_ge(s_gap1, 1)
            dve.tensor_tensor(gap[:, :, :], gap[:, :, :], gc.unsqueeze(2).to_broadcast([NS, H1, NS]),
                              ALU.subtract).then_inc(s_gap2, 1)
            dve.wait_ge(s_sq, 4)
            dve.tensor_reduce(ss[:, 0, :], sq_k[:, :, :], AX.X, ALU.add)
            dve.tensor_reduce(ss[:, 1, :], sq_q[:, :, :], AX.X, ALU.add).then_inc(s_ss, 1)
            dve.wait_ge(s_rn, 1)
            for n in range(2):
                mm = dve.tensor_tensor(k_tok[:, 4 * n:4 * n + 4, :], heads(0, n), col(rn[:, 0, :])[:, 4 * n:4 * n + 4, :],
                                       ALU.mult)
            mm.then_inc(s_kn, 1)
            dve.wait_ge(s_kn, 1)
            dve.tensor_tensor(kb[:, :, :], k_tok[:, :, :], col(beta), ALU.mult).then_inc(s_kb, 1)
            for n in range(2):
                mm = dve.scalar_tensor_tensor(q_tok[:, 4 * n:4 * n + 4, :], heads(2, n), D1 ** -0.5,
                                              col(rn[:, 1, :])[:, 4 * n:4 * n + 4, :], ALU.mult, ALU.mult)
            mm.then_inc(s_qn, 1)
            dve.wait_ge(s_qn, 1)
            dve.tensor_tensor(qe[:, :, :], q_tok[:, :, :], col(egc), ALU.mult).then_inc(s_qe, 1)
            dve.wait_ge(s_kb, 1)
            dve.scalar_tensor_tensor(kw[:, :, :], kb[:, :, :], -1.0, col(egc), ALU.mult, ALU.mult).then_inc(s_kw, 1)
            dve.tensor_tensor(kt[:, :, :], k_tok[:, :, :], col(erest), ALU.mult).then_inc(s_kt, 1)
            dve.wait_ge(s_bT, 3)
            dve.tensor_tensor(qz[:, :, :, :], turned[:, 2].unsqueeze(2).to_broadcast([P, H1, DB, NS]),
                              own_cols[:, :, :].unsqueeze(1).to_broadcast([P, H1, DB, NS]), ALU.mult).then_inc(s_qz, 1)
            dve.wait_ge(s_dec, 1)
            dve.wait_ge(s_kk, 2)
            dve.tensor_tensor(m[:, :, :], p[4][0:NS, 0:H1 * NS].rearrange("p (h t) -> p h t", t=NS), dec[:, :, :],
                              ALU.mult).then_inc(s_m1, 1)
            dve.wait_ge(s_m1, 1)
            dve.tensor_tensor(m[:, :, :], m[:, :, :], strict[:, :].unsqueeze(1).to_broadcast([NS, H1, NS]),
                              ALU.mult).then_inc(s_m, 1)
            eye = ident[0:NS, 0:NS].unsqueeze(1).to_broadcast([NS, H1, NS])
            dve.tensor_tensor(att[:, :, :], p[5][0:NS, 0:H1 * NS].rearrange("p (h t) -> p h t", t=NS), dec[:, :, :],
                              ALU.mult).then_inc(s_att, 1)
            dve.wait_ge(s_m, 1)
            dve.tensor_tensor(mi[:, :, :], m[:, :, :], eye, ALU.add).then_inc(s_mi, 1)
            dve.wait_ge(s_nn, 1)
            dve.tensor_tensor(r[:, :, :], p[0][0:NS, 0:H1 * NS].rearrange("p (h t) -> p h t", t=NS), eye,
                              ALU.add).then_inc(s_r, 1)
            dve.wait_ge(s_wp, 1)
            dve.tensor_tensor(wz[:, :, :, :], p[6][:, 0:H1 * NS].rearrange("p (h t) -> p h t", t=NS).unsqueeze(
                2).to_broadcast([P, H1, DB, NS]), own_cols[:, :, :].unsqueeze(1).to_broadcast([P, H1, DB, NS]),
                ALU.mult).then_inc(s_wz, 1)
            for h in range(H1):
                dve.wait_ge(s_vn, h // 4 + 1)
                if h >= 2:
                    dve.wait_ge(s_ds, 2 * h - 2)
                dve.tensor_tensor(vx[:, h % 2, :, :], vn[:, h, :].unsqueeze(1).to_broadcast([NS, DB, D1]),
                                  own[0:NS, :].unsqueeze(2).to_broadcast([NS, DB, D1]), ALU.mult).then_inc(s_vx, 1)
                if h >= 1:
                    grow(dve, h - 1)
            grow(dve, H1 - 1)
            dve.wait_ge(s_osq, 2)
            dve.tensor_reduce(oss[:, :], sq_q[:, :, :], AX.X, ALU.add).then_inc(s_oss, 1)
            dve.wait_ge(s_orn, 1)
            for n in range(2):
                mm = dve.tensor_tensor(sq_k[:, 4 * n:4 * n + 4, :], heads(2, n), col(orn[:, :])[:, 4 * n:4 * n + 4, :],
                                       ALU.mult)
            mm.then_inc(s_on, 1)
            dve.wait_ge(s_ot, 1)
            dve.scalar_tensor_tensor(oT[:, :, :], p[0][:, 0:H1 * NS].rearrange("p (h t) -> p h t", t=NS), g_o[:, 0:1],
                                     src[:, 3, :, :], ALU.mult, ALU.mult).then_inc(s_oT, 1)

        @block.gpsimd
        def _(pool):
            pool.memset(half[:, :], -0.5).then_inc(s_half, 1)
            pool.wait_ge(s_half, 1)
            pool.wait_ge(s_ss, 1)
            pool.tensor_scalar(sse[:, :, :], ss[:, :, :], EPS, None, ALU.add).then_inc(s_sse, 1)
            pool.wait_ge(s_sse, 1)
            pool.tensor_tensor(rn[:, :, :], sse[:, :, :], half[:, :].rearrange("p (a h) -> p a h", a=2),
                               ALU.pow).then_inc(s_rn, 1)
            pool.wait_ge(s_state, 16 * DB)
            for h in range(H1):
                pool.tensor_tensor(faded[:, :, h, :], state[:, :, h, :], gd[:, 5, 0:DB, h].unsqueeze(2).to_broadcast(
                    [P, DB, D1]), ALU.mult).then_inc(s_fade, 1)
            pool.wait_ge(s_oss, 1)
            pool.tensor_scalar(ose[:, :], oss[:, :], 1.0 / D1, EPS, ALU.mult, ALU.add).then_inc(s_ose, 1)
            pool.wait_ge(s_ose, 1)
            pool.tensor_tensor(orn[:, :], ose[:, :], half[:, 0:H1], ALU.pow).then_inc(s_orn, 1)


def stage_f(nc, io, cat):
    with Stage(nc, "F") as st:
        sb, ps, sem = st.sb, st.ps, st.sem
        w_raw = sb("w_raw", [P, H1, DM])
        w_hi, w_lo = (sb(n, [P, H1, DM], F32R) for n in ("w_hi", "w_lo"))
        o = sb("o", [P, 2, H1, P])
        h1 = sb("h1", [P, 2, DM])
        o_hi, o_lo = (sb(n, [P, 2, H1, P], F32R) for n in ("o_hi", "o_lo"))
        y = sb("y", [P, 2, DM])
        p_y = [ps(f"y{i}") for i in range(4)]
        s_w = [sem(f"w_in{k}") for k in range(H1)]
        s_whi, s_wlo = sem("w_hi"), sem("w_lo")
        s_o = [sem(f"o_in{i}") for i in range(2)]
        s_h = [sem(f"h1_in{i}") for i in range(2)]
        s_ohi, s_olo, s_p, s_y = (sem(n) for n in ("o_hi", "o_lo", "projected", "y_ready"))
        s_st = [sem(f"stored{i}") for i in range(2)]
        s_sp = sem("sync_waits_settled")
        block = st.block()

        @block.sync
        def _(sp):
            def load(t, slot):
                n = NS if isinstance(t, int) and t == NT else P
                sp.dma_start(o[:, slot, :, 0:n], io["oT"][:, :, bass.ds(t * P, n)].rearrange("h p n -> p h n")).then_inc(
                    s_o[slot], 16)
                sp.dma_start(h1[0:n, slot, :], io["h1"][bass.ds(t, 1), 0:n, :].rearrange("o p n -> p (o n)")).then_inc(
                    s_h[slot], 16)

            for k in range(H1):
                sp.dma_start(w_raw[:, k, :], io["w_out_odd"][0, k * P:(k + 1) * P, :]).then_inc(s_w[k], 16)
                if k == 0:
                    load(0, 0)
                    load(1, 1)

            def body(t, slot, nth):
                sp.wait_ge(s_y, t * 2 + 2)
                settle(sp, s_sp)
                if isinstance(t, int) and t == NT:
                    sp.dma_start(io["y_sample"].rearrange("b t d -> (b t) d"), y[0:NS, slot, :]).then_inc(s_st[slot], 16)
                else:
                    sp.dma_start(io["y_prompt"][0, bass.ds(t * P, P), :], y[:, slot, :]).then_inc(s_st[slot], 16)
                if not (isinstance(t, int) and t >= NT - 1):
                    load(t + 2, slot)

            tiles(sp, body)
            sp.wait_ge(s_st[0], 16 * (NT // 2 + 1))
            sp.wait_ge(s_st[1], 16 * (NT // 2))

        @block.tensor
        def _(pe):
            def body(t, slot, nth):
                m = NS if isinstance(t, int) and t == NT else P
                pe.wait_ge(s_olo, t + 1)
                at_least(pe, s_y, t * 2 - 2)
                for n in range(2):
                    cols = slice(n * 512, (n + 1) * 512)
                    out = p_y[2 * slot + n][0:m, :]
                    for k in range(H1):
                        if isinstance(t, int) and t == 0:
                            pe.wait_ge(s_wlo, k + 1)
                        pe.matmul(out, o_hi[:, slot, k, 0:m], w_hi[:, k, cols], start=(k == 0), stop=False)
                        pe.matmul(out, o_hi[:, slot, k, 0:m], w_lo[:, k, cols], start=False, stop=False)
                        mm = pe.matmul(out, o_lo[:, slot, k, 0:m], w_hi[:, k, cols], start=False, stop=(k == H1 - 1))
                    mm.then_inc(s_p, 1)

            tiles(pe, body)

        @block.scalar
        def _(act):
            def body(t, slot, nth):
                n = NS if isinstance(t, int) and t == NT else P
                act.wait_ge(s_o[slot], nth * 16 + 16)
                at_least(act, s_p, t * 2 - 2)
                act.activation(o_hi[:, slot, :, 0:n], o[:, slot, :, 0:n], ACT.Copy).then_inc(s_ohi, 1)
                if isinstance(t, int) and t == 0:
                    for k in range(H1):
                        act.wait_ge(s_w[k], 16)
                        act.activation(w_hi[:, k, :], w_raw[:, k, :], ACT.Copy).then_inc(s_whi, 1)

            tiles(act, body)

        @block.vector
        def _(dve):
            def split_o(t, slot, nth):
                n = NS if isinstance(t, int) and t == NT else P
                dve.wait_ge(s_ohi, t + 1)
                dve.wait_ge(s_o[slot], nth * 16 + 16)
                at_least(dve, s_p, t * 2 - 2)
                dve.tensor_tensor(o_lo[:, slot, :, 0:n], o[:, slot, :, 0:n], o_hi[:, slot, :, 0:n].bitcast(F32),
                                  ALU.subtract).then_inc(s_olo, 1)

            def body(t, slot, nth):
                if isinstance(t, int) and t == 0:
                    split_o(0, 0, 0)
                    for k in range(H1):
                        dve.wait_ge(s_whi, k + 1)
                        dve.tensor_tensor(w_lo[:, k, :], w_raw[:, k, :], w_hi[:, k, :].bitcast(F32),
                                          ALU.subtract).then_inc(s_wlo, 1)
                m = NS if isinstance(t, int) and t == NT else P
                if not (isinstance(t, int) and t == NT):
                    split_o(t + 1, 1 - slot, nth + slot)
                dve.wait_ge(s_h[slot], nth * 16 + 16)
                dve.wait_ge(s_st[slot], nth * 16) if not (isinstance(t, int) and t < 2) else None
                for n in range(2):
                    dve.wait_ge(s_p, t * 2 + (n + 1))
                    dve.tensor_tensor(y[0:m, slot, n * 512:(n + 1) * 512], p_y[2 * slot + n][0:m, :],
                                      h1[0:m, slot, n * 512:(n + 1) * 512], ALU.add).then_inc(s_y, 1)

            tiles(dve, body)


OUTS = [("y_prompt", (1, SEQ, DM)), ("y_sample", (DB, DS, DM)),
        ("pool_prompt", (1, 1, BUF, W0)), ("pool_sample", (1, DB, BUF, W0)),
        ("k_prompt", (1, 1, SEQ, H0, HD)), ("v_prompt", (1, 1, SEQ, H0, HD)),
        ("k_sample", (1, DB, DS, H0, HD)), ("v_sample", (1, DB, DS, H0, HD)),
        ("conv_prompt", (1, 1, CW - 1, CONV)), ("conv_sample", (1, DB, CW - 1, CONV)),
        ("delta_prompt", (1, 1, H1, D1, D1)), ("delta_sample", (1, DB, H1, D1, D1))]
SCRATCH = [("mixgate", (NT + 1, P, DM)),
           ("q_turned", ((NT + 1) * 4, P, P)),
           ("k_turned", (P, 4, (NT + 1) * P)),
           ("h1", (NT + 1, P, DM)),
           ("xT", (P, KC, (NT + 1) * P)),
           ("strips", (4 * H1, P, SEQ + NS)),
           ("oT", (H1, P, (NT + 1) * P))]


def build(nc, io, cat):
    with nc.sbuf_tensor("gd", [P, 6, NT + 1, H1], F32) as gd:
        stage_a(nc, io, cat, heads=False)
        stage_a(nc, io, cat, heads=True)
        with nc.sbuf_tensor("o_all", [P, NT + 1, W0], F32) as o_all:
            stage_b(nc, io, cat, o_all)
            stage_s(nc, io, cat, o_all)
            stage_c(nc, io, cat, o_all)
        with nc.sbuf_tensor("ba", [2 * H1, SEQ + NS], F32) as ba:
            stage_d(nc, io, cat, ba)
            stage_g(nc, io, cat, ba, gd)
        stage_e(nc, io, cat, gd)
        stage_h(nc, io, cat, gd)
        stage_f(nc, io, cat)


def kernel(**inputs):
    import concourse.bacc as bacc
    from concourse.bass_utils import run_bass_kernel_spmd

    nc = bacc.Bacc("TRN2", target_bir_lowering=False, num_devices=1)
    consts, cat = constants()
    arrays = {name: np.ascontiguousarray(a) for name, a in inputs.items()}
    arrays["consts"] = consts
    io = {}
    for name, a in arrays.items():
        io[name] = nc.dram_tensor(f"in_{name}", a.shape, mybir.dt.from_np(a.dtype), kind="ExternalInput").ap()
    for name, shape in OUTS:
        io[name] = nc.dram_tensor(f"out_{name}", shape, F32, kind="ExternalOutput").ap()
    for name, shape in SCRATCH:
        io[name] = nc.dram_tensor(f"scratch_{name}", shape, F32, kind="Internal").ap()
    build(nc, io, cat)
    r = run_bass_kernel_spmd(nc, [{f"in_{name}": a for name, a in arrays.items()}], core_ids=[0])
    return tuple(r.results[0][f"out_{name}"] for name, _ in OUTS)
```
